# Optimizing a Trainium2 kernel written in Bass

```python
import math
import jax, jax.numpy as jnp
from jax import lax
import numpy as np

D_MODEL = 1024
BATCH = 1
SEQ = 512
DEPTH = 1

MIX_WIDTH = D_MODEL
DA_HEADS = 4
DA_QK_DIM = 64
DA_V_DIM = 2 * DA_QK_DIM
DA_WIDTH = DA_HEADS * DA_V_DIM
RET_HEADS = 4
RET_QK_DIM = 64
RET_V_DIM = 2 * RET_QK_DIM
RET_WIDTH = RET_HEADS * RET_V_DIM
Q_BLOCK = 128
RET_CHUNK = 128
EPS = 1e-6

DA_Q_COLS = DA_HEADS * 2 * DA_QK_DIM
DA_K_COLS = DA_HEADS * 2 * DA_QK_DIM
DA_V_COLS = DA_WIDTH
DA_G_COLS = DA_WIDTH
RET_Q_COLS = RET_HEADS * RET_QK_DIM
RET_K_COLS = RET_HEADS * RET_QK_DIM
RET_V_COLS = RET_WIDTH
RET_G_COLS = RET_WIDTH
IN_WIDTH = DA_Q_COLS + DA_K_COLS + DA_V_COLS + DA_G_COLS + RET_Q_COLS + RET_K_COLS + RET_V_COLS + RET_G_COLS


def _rms(x, w=None):
    xf = x.astype(jnp.float32)
    y = xf * lax.rsqrt(jnp.mean(xf * xf, axis=-1, keepdims=True) + EPS)
    if w is not None:
        y = y * w.astype(jnp.float32)
    return y.astype(x.dtype)

def _alibi_slopes(n_heads):
    return jnp.asarray([2.0 ** (-8.0 * (i + 1) / n_heads) for i in range(n_heads)], dtype=jnp.float32)

def _diff_attention(q, k, v, lam, slopes):
    b, s = q.shape[0], q.shape[1]
    q = jnp.transpose(q, (0, 2, 3, 1, 4))
    k = jnp.transpose(k, (0, 2, 3, 1, 4))
    v = jnp.transpose(v, (0, 2, 1, 3))
    scale = DA_QK_DIM ** -0.5
    key_pos = jnp.arange(s)

    def block(i):
        start = i * Q_BLOCK
        qb = lax.dynamic_slice_in_dim(q, start, Q_BLOCK, axis=3)
        sc = jnp.einsum('bhmqd,bhmkd->bhmqk', qb, k).astype(jnp.float32) * scale
        qpos = start + jnp.arange(Q_BLOCK)
        dist = jnp.abs(qpos[:, None] - key_pos[None, :]).astype(jnp.float32)
        sc = sc - (slopes[:, None, None] * dist)[None, :, None]
        p = jax.nn.softmax(sc, axis=-1)
        w = p[:, :, 0] - lam * p[:, :, 1]
        return jnp.einsum('bhqk,bhkd->bhqd', w.astype(v.dtype), v)

    out = lax.map(block, jnp.arange(s // Q_BLOCK))
    return jnp.transpose(out, (1, 0, 3, 2, 4)).reshape(b, s, DA_HEADS, DA_V_DIM)

def _retention_dir(q, k, v, log_g, inclusive):
    b, h, s, dk = q.shape
    dv = v.shape[-1]
    nc = s // RET_CHUNK

    def chunks(t):
        return jnp.moveaxis(t.reshape(b, h, nc, RET_CHUNK, t.shape[-1]), 2, 0)

    n = jnp.arange(RET_CHUNK)
    diff = n[:, None] - n[None, :]
    mask = diff >= 0 if inclusive else diff > 0
    dmat = jnp.where(mask[None], jnp.exp(log_g[:, None, None] * jnp.maximum(diff, 0).astype(jnp.float32)), 0.0)
    xi = jnp.exp(log_g[:, None] * (n + 1).astype(jnp.float32))
    zeta = jnp.exp(log_g[:, None] * (RET_CHUNK - 1 - n).astype(jnp.float32))
    chunk_decay = jnp.exp(log_g * RET_CHUNK)

    def step(state, qkv):
        qc, kc, vc = qkv
        inner = jnp.einsum('bhqk,bhkv->bhqv', jnp.einsum('bhqd,bhkd->bhqk', qc, kc) * dmat, vc)
        cross = jnp.einsum('bhqd,bhdv->bhqv', qc * xi[..., None], state)
        new_state = chunk_decay[:, None, None] * state + jnp.einsum('bhkd,bhkv->bhdv', kc * zeta[..., None], vc)
        return new_state, inner + cross

    state0 = jnp.zeros((b, h, dk, dv), jnp.float32)
    _, out = lax.scan(step, state0, (chunks(q), chunks(k), chunks(v)))
    return jnp.moveaxis(out, 0, 2).reshape(b, h, s, dv)

def _bidirectional_retention(q, k, v, decay_fwd, decay_bwd):
    qf = jnp.transpose(q, (0, 2, 1, 3)).astype(jnp.float32)
    kf = jnp.transpose(k, (0, 2, 1, 3)).astype(jnp.float32) * (RET_QK_DIM ** -0.5)
    vf = jnp.transpose(v, (0, 2, 1, 3)).astype(jnp.float32)
    lg_f = jax.nn.log_sigmoid(decay_fwd.astype(jnp.float32))
    lg_b = jax.nn.log_sigmoid(decay_bwd.astype(jnp.float32))
    fwd = _retention_dir(qf, kf, vf, lg_f, True)
    flip = lambda t: jnp.flip(t, axis=2)
    bwd = flip(_retention_dir(flip(qf), flip(kf), flip(vf), lg_b, False))
    out = _rms(fwd + bwd)
    return jnp.transpose(out, (0, 2, 1, 3)).astype(q.dtype)

def first_inputs(seed: int = 0) -> dict:
    key = jax.random.key(seed)
    ks = jax.random.split(key, 14)
    x = jax.random.normal(ks[0], (BATCH, SEQ, D_MODEL), jnp.float32)
    norm_w = 1.0 + 0.02 * jax.random.normal(ks[1], (DEPTH, D_MODEL), jnp.float32)
    w_in = jax.random.normal(ks[2], (DEPTH, D_MODEL, IN_WIDTH), jnp.float32) * D_MODEL ** -0.5
    q_norm_w = 1.0 + 0.02 * jax.random.normal(ks[3], (DEPTH, DA_QK_DIM), jnp.float32)
    k_norm_w = 1.0 + 0.02 * jax.random.normal(ks[4], (DEPTH, DA_QK_DIM), jnp.float32)
    lambda_q1 = 0.1 * jax.random.normal(ks[5], (DEPTH, DA_QK_DIM), jnp.float32)
    lambda_k1 = 0.1 * jax.random.normal(ks[6], (DEPTH, DA_QK_DIM), jnp.float32)
    lambda_q2 = 0.1 * jax.random.normal(ks[7], (DEPTH, DA_QK_DIM), jnp.float32)
    lambda_k2 = 0.1 * jax.random.normal(ks[8], (DEPTH, DA_QK_DIM), jnp.float32)
    subln_w = 1.0 + 0.02 * jax.random.normal(ks[9], (DEPTH, DA_V_DIM), jnp.float32)
    gamma = 1.0 - 2.0 ** (-5.0 - jnp.arange(RET_HEADS, dtype=jnp.float32))
    base_logit = jnp.log(gamma) - jnp.log1p(-gamma)
    ret_decay_fwd = base_logit[None] + 0.1 * jax.random.normal(ks[10], (DEPTH, RET_HEADS), jnp.float32)
    ret_decay_bwd = base_logit[None] + 0.1 * jax.random.normal(ks[11], (DEPTH, RET_HEADS), jnp.float32)
    w_out = jax.random.normal(ks[12], (DEPTH, MIX_WIDTH, D_MODEL), jnp.float32) * (MIX_WIDTH ** -0.5) / math.sqrt(2.0 * DEPTH)
    return {"x": x, "norm_w": norm_w, "w_in": w_in, "q_norm_w": q_norm_w, "k_norm_w": k_norm_w,
            "lambda_q1": lambda_q1, "lambda_k1": lambda_k1, "lambda_q2": lambda_q2, "lambda_k2": lambda_k2,
            "subln_w": subln_w, "ret_decay_fwd": ret_decay_fwd, "ret_decay_bwd": ret_decay_bwd, "w_out": w_out}

def first_block(x, norm_w, w_in, q_norm_w, k_norm_w, lambda_q1, lambda_k1, lambda_q2, lambda_k2,
              subln_w, ret_decay_fwd, ret_decay_bwd, w_out):
    b, s, _ = x.shape
    slopes = _alibi_slopes(DA_HEADS)
    sizes = [DA_Q_COLS, DA_K_COLS, DA_V_COLS, DA_G_COLS, RET_Q_COLS, RET_K_COLS, RET_V_COLS, RET_G_COLS]
    offsets = [int(o) for o in np.cumsum(sizes)[:-1]]
    for l in range(DEPTH):
        xn = _rms(x, norm_w[l])
        h = jnp.einsum('bsd,de->bse', xn, w_in[l])
        qa, ka, va, ga, qr, kr, vr, gr = jnp.split(h, offsets, axis=-1)

        lambda_init = 0.8 - 0.6 * math.exp(-0.3 * l)
        lam = (jnp.exp(jnp.sum(lambda_q1[l].astype(jnp.float32) * lambda_k1[l].astype(jnp.float32)))
               - jnp.exp(jnp.sum(lambda_q2[l].astype(jnp.float32) * lambda_k2[l].astype(jnp.float32)))
               + lambda_init)
        qa = _rms(qa.reshape(b, s, DA_HEADS, 2, DA_QK_DIM), q_norm_w[l])
        ka = _rms(ka.reshape(b, s, DA_HEADS, 2, DA_QK_DIM), k_norm_w[l])
        va = va.reshape(b, s, DA_HEADS, DA_V_DIM)
        oa = _diff_attention(qa, ka, va, lam, slopes)
        oa = (_rms(oa, subln_w[l]) * (1.0 - lambda_init)).reshape(b, s, DA_WIDTH)

        qr = qr.reshape(b, s, RET_HEADS, RET_QK_DIM)
        kr = kr.reshape(b, s, RET_HEADS, RET_QK_DIM)
        vr = vr.reshape(b, s, RET_HEADS, RET_V_DIM)
        orr = _bidirectional_retention(qr, kr, vr, ret_decay_fwd[l], ret_decay_bwd[l]).reshape(b, s, RET_WIDTH)

        mixed = jnp.concatenate([oa * jax.nn.silu(ga), orr * jax.nn.silu(gr)], axis=-1)
        x = x + jnp.einsum('bse,ed->bsd', mixed, w_out[l])
    return x


CONV_WIDTH = D_MODEL
CONV_K = 3
N_Q_HEADS = 16
N_KV_HEADS = 4
HEAD_DIM = 64
ATTN_WIDTH = N_Q_HEADS * HEAD_DIM
KV_WIDTH = N_KV_HEADS * HEAD_DIM
WINDOW = 128
BLOCK = 128
N_BRANCHES = 2
NEG_INF = -1e30

IN_SIZES = (CONV_WIDTH, CONV_WIDTH, CONV_WIDTH, CONV_WIDTH,
            ATTN_WIDTH, KV_WIDTH, KV_WIDTH, ATTN_WIDTH,
            N_BRANCHES * D_MODEL)
IN_COLS = sum(IN_SIZES)
SPLIT_POINTS = tuple(int(c) for c in np.cumsum(IN_SIZES)[:-1])


def rms_norm(x, g):
    xf = x.astype(jnp.float32)
    y = xf * lax.rsqrt(jnp.mean(xf * xf, axis=-1, keepdims=True) + EPS)
    return (y * g.astype(jnp.float32)).astype(x.dtype)

def causal_depthwise_conv(u, w):
    s = u.shape[1]
    up = jnp.pad(u, ((0, 0), (CONV_K - 1, 0), (0, 0)))
    y = up[:, 0:s] * w[0]
    for k in range(1, CONV_K):
        y = y + up[:, k:k + s] * w[k]
    return y

def sliding_window_attention(q, k, v, sinks):
    b, s = q.shape[0], q.shape[1]
    nb = s // BLOCK
    g = N_Q_HEADS // N_KV_HEADS
    qb = q.reshape(b, nb, BLOCK, N_KV_HEADS, g, HEAD_DIM)

    def band(t):
        tb = t.reshape(b, nb, BLOCK, N_KV_HEADS, HEAD_DIM)
        prev = jnp.pad(tb[:, :-1], ((0, 0), (1, 0), (0, 0), (0, 0), (0, 0)))
        return jnp.concatenate([prev, tb], axis=2)

    kb, vb = band(k), band(v)
    scale = HEAD_DIM ** -0.5
    scores = jnp.einsum('bnqhgd,bnkhd->bnhgqk', qb.astype(jnp.float32),
                        kb.astype(jnp.float32)) * scale
    blk = jnp.arange(nb)[:, None, None]
    q_pos = blk * BLOCK + jnp.arange(BLOCK)[None, :, None]
    k_pos = (blk - 1) * BLOCK + jnp.arange(2 * BLOCK)[None, None, :]
    diff = q_pos - k_pos
    valid = (diff >= 0) & (diff < WINDOW) & (k_pos >= 0)
    scores = jnp.where(valid[None, :, None, None], scores, NEG_INF)
    sink = sinks.astype(jnp.float32).reshape(N_KV_HEADS, g)[None, None, :, :, None, None]
    m = jnp.maximum(jnp.max(scores, axis=-1, keepdims=True), sink)
    p = jnp.exp(scores - m)
    p = p / (jnp.sum(p, axis=-1, keepdims=True) + jnp.exp(sink - m))
    out = jnp.einsum('bnhgqk,bnkhd->bnqhgd', p.astype(v.dtype), vb)
    return out.reshape(b, s, ATTN_WIDTH)

def hybrid_layer(x, norm_g, w_in, conv_w, q_norm_g, k_norm_g, sinks,
                 w_conv_out, w_attn_out, gate_b, w_out):
    b, s, _ = x.shape
    h = rms_norm(x, norm_g)
    u = jnp.einsum('bsd,dc->bsc', h, w_in)
    v_c, b_c, c_c, z_c, q, k, v, z_a, gate_logits = jnp.split(u, SPLIT_POINTS, axis=-1)

    y_c = b_c * causal_depthwise_conv(c_c * v_c, conv_w)
    y_c = y_c * jax.nn.silu(z_c)
    y_a = jnp.einsum('bsc,cd->bsd', y_c, w_conv_out)

    q = rms_norm(q.reshape(b, s, N_Q_HEADS, HEAD_DIM), q_norm_g)
    k = rms_norm(k.reshape(b, s, N_KV_HEADS, HEAD_DIM), k_norm_g)
    v = v.reshape(b, s, N_KV_HEADS, HEAD_DIM)
    o = sliding_window_attention(q, k, v, sinks) * jax.nn.silu(z_a)
    y_b = jnp.einsum('bsc,cd->bsd', o, w_attn_out)

    gates = jax.nn.sigmoid(gate_logits + gate_b)
    g_a, g_b = jnp.split(gates, N_BRANCHES, axis=-1)
    merged = g_a * y_a + g_b * y_b
    return x + jnp.einsum('bsd,de->bse', merged, w_out)

def second_inputs(seed: int = 0) -> dict:
    key = jax.random.key(seed)
    ks = jax.random.split(key, 12)
    f32 = jnp.float32
    x = jax.random.normal(ks[0], (BATCH, SEQ, D_MODEL), f32)
    norm_g = 1.0 + 0.05 * jax.random.normal(ks[1], (DEPTH, D_MODEL), f32)
    w_in = jax.random.normal(ks[2], (DEPTH, D_MODEL, IN_COLS), f32) * D_MODEL ** -0.5
    conv_w = jax.random.normal(ks[3], (DEPTH, CONV_K, CONV_WIDTH), f32) * CONV_K ** -0.5
    q_norm_g = 1.0 + 0.05 * jax.random.normal(ks[4], (DEPTH, HEAD_DIM), f32)
    k_norm_g = 1.0 + 0.05 * jax.random.normal(ks[5], (DEPTH, HEAD_DIM), f32)
    sinks = 0.5 * jax.random.normal(ks[6], (DEPTH, N_Q_HEADS), f32)
    w_conv_out = jax.random.normal(ks[7], (DEPTH, CONV_WIDTH, D_MODEL), f32) * CONV_WIDTH ** -0.5
    w_attn_out = jax.random.normal(ks[8], (DEPTH, ATTN_WIDTH, D_MODEL), f32) * ATTN_WIDTH ** -0.5
    gate_b = 0.02 * jax.random.normal(ks[9], (DEPTH, N_BRANCHES * D_MODEL), f32)
    w_out = jax.random.normal(ks[10], (DEPTH, D_MODEL, D_MODEL), f32) * D_MODEL ** -0.5
    return {"x": x, "norm_g": norm_g, "w_in": w_in, "conv_w": conv_w,
            "q_norm_g": q_norm_g, "k_norm_g": k_norm_g, "sinks": sinks,
            "w_conv_out": w_conv_out, "w_attn_out": w_attn_out,
            "gate_b": gate_b, "w_out": w_out}

def second_block(x, norm_g, w_in, conv_w, q_norm_g, k_norm_g, sinks,
              w_conv_out, w_attn_out, gate_b, w_out):
    for l in range(DEPTH):
        x = hybrid_layer(x, norm_g[l], w_in[l], conv_w[l], q_norm_g[l], k_norm_g[l],
                         sinks[l], w_conv_out[l], w_attn_out[l], gate_b[l], w_out[l])
    return x


def setup_inputs(seed=0):
    out = dict(first_inputs(seed))
    for name, value in second_inputs(seed + 1).items():
        if name != "x":
            out[name + "_2"] = value
    return out


def reference(
    x, norm_w, w_in, q_norm_w, k_norm_w, lambda_q1, lambda_k1, lambda_q2, lambda_k2, subln_w,
    ret_decay_fwd, ret_decay_bwd, w_out, norm_g_2, w_in_2, conv_w_2, q_norm_g_2, k_norm_g_2,
    sinks_2, w_conv_out_2, w_attn_out_2, gate_b_2, w_out_2,
):
    x = first_block(
        x, norm_w, w_in, q_norm_w, k_norm_w, lambda_q1, lambda_k1, lambda_q2, lambda_k2,
        subln_w, ret_decay_fwd, ret_decay_bwd, w_out,
    )
    return second_block(
        x, norm_g_2, w_in_2, conv_w_2, q_norm_g_2, k_norm_g_2, sinks_2, w_conv_out_2,
        w_attn_out_2, gate_b_2, w_out_2,
    )


_drawn_inputs = setup_inputs


def setup_inputs(seed=0):
    import zlib

    import numpy as np

    out = dict(_drawn_inputs(seed))
    spreads = {}
    factors = {'norm_w': 3.102,
     'q_norm_w': 8.0,
     'k_norm_w': 8.0,
     'lambda_q1': 64.0,
     'lambda_q2': 3.71,
     'lambda_k2': 5.695,
     'subln_w': 8.0,
     'q_norm_g_2': 39.417,
     'k_norm_g_2': 33.595,
     'sinks_2': 64.0,
     'gate_b_2': 64.0,
     'norm_g_2': 3.589}
    for name, (base, spread) in spreads.items():
        noise = np.random.default_rng([zlib.crc32(name.encode()), seed]).standard_normal(out[name].shape)
        drawn = base * np.exp(spread * noise) if base else spread * noise
        out[name] = __import__('jax').numpy.asarray(drawn.astype(out[name].dtype))
    for name, factor in factors.items():
        out[name] = (out[name] * factor).astype(out[name].dtype)
    return out
```

```python
from contextlib import ExitStack

import concourse.bass as bass
from concourse import mybir

F32 = mybir.dt.float32
F32R = mybir.dt.float32r
I32 = mybir.dt.int32
ALU = mybir.AluOpType
ACT = mybir.ActivationFunctionType
AXX = mybir.AxisListType.X

P = 128
S = 512
ST = S // P
D = 1024
KC = D // P
EPS = 1e-6
LAMBDA_INIT = 0.8 - 0.6
HD = 64
QK_SCALE = HD ** -0.5
DA_HEADS = 4
RET_HEADS = 4
KV_HEADS = 4
GROUP = 4
TAB = (2 * ST - 1) * P
CENTRE = (ST - 1) * P
BIG = 1e30
R_GATE = 3 * KC
R_KW = R_GATE + 2 * KC
ROWS = R_KW + 5
SLOTS = 4
RSQRT_SEED = 0x5F3759DF

NAT, TRA = "natural", "transposed"
(U_K, U_Q, U_V, U_RQK, U_RV, U_GA, U_GR, U_O0, U_O1, U_KV, U_Q20, U_Q21, U_Z0, U_Z1) = range(14)
U_CONV = 14
U_GATE_A = U_CONV + KC
U_GATE_B = U_GATE_A + KC // 2
U_OUT = U_GATE_B + KC // 2
UNITS = U_OUT + 2
PIECES = 4 * UNITS
CV, CB, CC, CZ, Q2, K2, Z2, G2 = 0, 1024, 2048, 3072, 4096, 5120, 5632, 6656


def unit_columns(u):
    if u < U_CONV:
        return [
            (NAT, [("w_in", 512)]), (NAT, [("w_in", 0)]), (NAT, [("w_in", 1024)]),
            (TRA, [("w_in", 2048 + P * j) for j in range(4)]), (NAT, [("w_in", 2560)]),
            (TRA, [("w_in", 1536 + P * j) for j in range(4)]), (TRA, [("w_in", 3072 + P * j) for j in range(4)]),
            (NAT, [("w_out", 0)]), (NAT, [("w_out", 512)]),
            (NAT, [("w_in_2", K2)]), (NAT, [("w_in_2", Q2)]), (NAT, [("w_in_2", Q2 + 512)]),
            (TRA, [("w_in_2", Z2 + P * j) for j in range(4)]),
            (TRA, [("w_in_2", Z2 + 512 + P * j) for j in range(4)])][u]
    if u < U_GATE_A:
        t = u - U_CONV
        return TRA, [("w_in_2", c + P * t) for c in (CV, CC, CB, CZ)]
    if u < U_OUT:
        t = 2 * ((u - U_GATE_A) % (KC // 2))
        gate, other = (G2, "w_conv_out_2") if u < U_GATE_B else (G2 + D, "w_attn_out_2")
        return TRA, [("w_in_2", gate + P * t), (other, P * t), ("w_in_2", gate + P * t + P), (other, P * t + P)]
    return NAT, [("w_out_2", 512 * (u - U_OUT))]


UNIT = [unit_columns(u) for u in range(UNITS)]
NATURAL_BEFORE = [sum(UNIT[v][0] == NAT for v in range(u)) for u in range(UNITS)]


def tile_number(u, j):
    return 8 + 4 * u + j + (8 if u >= U_KV else 0)


DA_STEPS = DA_HEADS * ST
WIN_STEPS = ST * KV_HEADS
DA_FIRST = 4 * U_RQK
WIN_FIRST = 4 * U_Z0 + 5


TURNS = [("KT", U_Q, 0), ("QT", U_V, 0), ("KT2", U_Q20, 0), ("QT2", U_Q21, 0), ("QT2", U_Z0, 4)]


def steps_after(n, half):
    out = []
    for kind, unit, first in TURNS:
        j = 2 * (n - 4 * unit) + half - 3
        if 0 <= j < 4:
            out.append((kind, first + j))
    g = 2 * (n - DA_FIRST) + half
    if 3 <= g < DA_STEPS + 3:
        out.append(("AV", g - 3))
    if 2 <= g < DA_STEPS + 2:
        out.append(("TW", g - 2))
    if 0 <= g < DA_STEPS:
        out.append(("S", g))
    r = g - DA_STEPS - 1
    if 2 <= r < DA_STEPS + 2:
        out.append(("RA", r - 2))
    if 0 <= r < DA_STEPS:
        out.append(("RS", r))
    finals = {19: 0, 21: 1, 23: 2, 25: 3, 27: 4, 29: 5, 33: 6, 36: 7}
    if g in finals:
        out.append(("F", finals[g]))
    a = 2 * (n - WIN_FIRST) + half
    if 4 <= a < WIN_STEPS + 4:
        out.append(("F2", a - 4))
    if 1 <= a < WIN_STEPS + 1:
        out.append(("TPa", a - 1))
    if 0 <= a < WIN_STEPS:
        out.append(("S2", a))
    if 2 <= a < WIN_STEPS + 2:
        out.append(("AV2", a - 2))
    if 1 <= a < WIN_STEPS + 1:
        out.append(("TPb", a - 1))
    s = a - (WIN_STEPS + 5)
    if 0 <= s < 2 * KC and s % 2 == 0:
        out.append(("OS", s // 2))
    return out


STEPS = {(n, half): steps_after(n, half) for n in range(PIECES) for half in range(2)}
BANK_T_USERS = ("KT", "QT", "TW", "F", "KT2", "QT2", "TPa", "TPb")
T_USE = {}
for _n in range(PIECES):
    for _half in range(2):
        for _step in STEPS[(_n, _half)]:
            if _step[0] in BANK_T_USERS:
                T_USE[_step] = len(T_USE)


def tiles_done(n, half):
    u, q = divmod(n, 4)
    if UNIT[u][0] == TRA:
        return [(u, q)] if half == 1 else []
    return [(u, 2 * half), (u, 2 * half + 1)] if q == 3 else []


def build(nc, a):
    with ExitStack() as ctx:
        def sb(name, shape, dt=F32, stack=ctx):
            return stack.enter_context(nc.sbuf_tensor(name, shape, dt))

        def sem(name):
            return ctx.enter_context(nc.semaphore(name))

        w_raw = sb("w_raw", [P, SLOTS, D])
        w_hi = sb("w_hi", [P, SLOTS, D], F32R)
        w_lo = sb("w_lo", [P, SLOTS, D], F32R)
        xt_hi = sb("xt_hi", [P, KC, S], F32R)
        xt_lo = sb("xt_lo", [P, KC, S], F32R)
        ident = sb("ident", [P, P])
        mask = sb("mask", [P, 2 * P])
        rows = sb("rows", [ROWS, P]); cols = sb("cols", [P, ROWS])
        qws = sb("qws", [P, 1]); q2ws = sb("q2ws", [P, 1]); sub_s = sb("sub_s", [P, 1])
        lam_v = sb("lam_v", [P, 4, HD]); lam_s = sb("lam_s", [P, 2]); lam_e = sb("lam_e", [P, 2]); lam = sb("lam", [P, 1])
        lam_j = sb("lam_j", [P, HD])
        dec = sb("dec", [P, 8]); dec_a = sb("dec_a", [P, 8]); dec_e = sb("dec_e", [P, 8])
        dec_z = sb("dec_z", [P, 8]); dec_q = sb("dec_q", [P, 8]); dec_p = sb("dec_p", [P, 8])
        log_g = sb("log_g", [P, 8]); neg_log_b = sb("neg_log_b", [P, 4])
        sink = sb("sink", [P, 16]); neg_sink = sb("neg_sink", [P, 16])
        half_b = sb("half_b", [P, 16])
        ssq = sb("ssq", [P, 4]); ssq_half = sb("ssq_half", [P, 4, 2])
        rs_v = sb("rs_v", [P, 32]); rs_y = sb("rs_y", [P, 32]); rs_t = sb("rs_t", [P, 32])
        mx = sb("mx", [P, 2, 2]); neg_mx = sb("neg_mx", [P, 2, 2]); den = sb("den", [P, 2, 2])
        rec = sb("rec", [P, 2, 2]); lam_rec = sb("lam_rec", [P, 2, 1])
        mx2 = sb("mx2", [P, 4, 4]); neg_m2 = sb("neg_m2", [P, 4, 4]); sink_m = sb("sink_m", [P, 4, 4])
        den2 = sb("den2", [P, 4, 4]); sink_e = sb("sink_e", [P, 4, 4]); rec2 = sb("rec2", [P, 4, 4])

        conv_w = cols[:, 0:R_GATE].rearrange("p (k t) -> p k t", k=3)
        gate_b = cols[:, R_GATE:R_KW]
        kw, qw, k2w, q2w, sub_w = (cols[:, r:r + 1] for r in range(R_KW, ROWS))

        start = ExitStack()
        x_in = sb("x_in", [P, ST, D], stack=start)
        xs_1 = sb("xs_1", [P, ST, D], stack=start)
        norm_1 = sb("norm_1", [P, D], stack=start)
        start.close()

        one = ExitStack()
        qT = sb("qT", [P, DA_HEADS, S], stack=one)
        kT = sb("kT", [P, DA_HEADS, S], stack=one)
        va = sb("va", [P, ST, 512], stack=one)
        rqkT = sb("rqkT", [P, 4, S], stack=one)
        vr = sb("vr", [P, ST, 512], stack=one)
        prob = sb("prob", [P, 2, 2, S], stack=one)
        wT = sb("wT", [P, 2, S], stack=one)
        o_raw = sb("o_raw", [P, 4, ST, P], stack=one)
        sq = sb("sq", [P, S], stack=one)
        th = sb("th", [P, S], stack=one)
        gT = sb("gT", [P, KC, S], stack=one)
        mix_hi = sb("mix_hi", [P, KC, S], F32R, stack=one)
        mix_lo = sb("mix_lo", [P, KC, S], F32R, stack=one)
        table = sb("table", [P, 2, TAB], stack=one)
        diff = sb("diff", [P, TAB], stack=one)
        one.close()
        stage = prob[:].rearrange("p a b s -> p (a b) s")

        two = ExitStack()
        x1 = sb("x1", [P, ST, D], stack=two)
        gT2 = sb("gT2", [P, KC, S], stack=two)
        yc_hi = sb("yc_hi", [P, KC, S], F32R, stack=two)
        yc_lo = sb("yc_lo", [P, KC, S], F32R, stack=two)
        th2 = sb("th2", [P, S], stack=two)
        acc = sb("acc", [P, S], stack=two)
        later = ExitStack()
        o2_hi = sb("o2_hi", [P, KC, S], F32R, stack=later)
        o2_lo = sb("o2_lo", [P, KC, S], F32R, stack=later)
        part = sb("part", [P, KC, S], stack=later)
        later.close()
        qT2 = sb("qT2", [P, KC, S], stack=two)
        kT2 = sb("kT2", [P, KV_HEADS, S], stack=two)
        v2 = sb("v2", [P, ST, 256], stack=two)
        prob2 = sb("prob2", [P, 2, GROUP, 256], stack=two)
        pT = sb("pT", [P, 2, 2, 512], stack=two)
        o2n = sb("o2n", [P, 4, 256], stack=two)
        sq2 = sb("sq2", [P, S], stack=two)
        vt = sb("vt", [P, S], stack=two)
        cv = sb("cv", [P, S + 2], stack=two)
        two.close()
        xs_2 = qT2[:].rearrange("p c s -> p (c s)").rearrange("p (t d) -> p t d", t=ST)
        k_dup = qT2[:, 0:4, :]
        norm_2 = gT2[:, 0:2, :].rearrange("p c s -> p (c s)")
        stage2 = prob2[:].rearrange("p a b s -> p (a b s)").rearrange("p (t s) -> p t s", t=4)

        proj = ctx.enter_context(nc.psum_tensor("proj", [P, SLOTS, S], F32))
        score = ctx.enter_context(nc.psum_tensor("score", [P, 2, S], F32))
        bank_t = ctx.enter_context(nc.psum_tensor("bank_t", [P, S], F32))
        bank_o = ctx.enter_context(nc.psum_tensor("bank_o", [P, S], F32))

        x_landed = [sem(f"x_landed{s}") for s in range(ST)]
        x_again = sem("x_again")
        params = sem("params")
        rows_turned = sem("rows_turned")
        norm_1_landed = sem("norm_1_landed")
        norm_2_landed = sem("norm_2_landed")
        raw_landed = [sem(f"raw_landed{i}") for i in range(SLOTS)]
        slot_open = sem("slot_open")
        hi_done = sem("hi_done")
        w_split = sem("w_split")
        piece_done = sem("piece_done")
        natural_done = sem("natural_done")
        evacuated = [sem(f"evacuated{b}") for b in range(SLOTS)]
        xt_done = sem("xt_done")
        xt_hi_done = sem("xt_hi_done")
        setup = sem("setup")
        setup_mask = sem("setup_mask")
        diff_done = sem("diff_done")
        ssq_done = sem("ssq_done")
        xs_done = sem("xs_done")
        dec_abs = sem("dec_abs"); dec_exp = sem("dec_exp")
        lam_sum = sem("lam_sum"); lam_exp = sem("lam_exp")
        weights_ready = sem("weights_ready")
        sq_done = sem("sq_done"); sq_used = sem("sq_used")
        heads_done = sem("heads_done")
        t_done = sem("t_done"); t_free = sem("t_free")
        scores_done = sem("scores_done"); score_read = sem("score_read")
        neg_max = sem("neg_max"); exp_done = sem("exp_done"); weight_done = sem("weight_done")
        av_done = sem("av_done"); o_free = sem("o_free"); o_normed = sem("o_normed")
        decay_arg = sem("decay_arg"); decay_done = sem("decay_done")
        ret_scores = sem("ret_scores"); ret_weight = sem("ret_weight")
        th_done = sem("th_done"); mixed = sem("mixed")
        scores2 = sem("scores2"); score2_read = sem("score2_read"); neg_max2 = sem("neg_max2")
        exp2_done = sem("exp2_done"); av2_done = sem("av2_done"); o2_normed = sem("o2_normed")
        o2_turned = sem("o2_turned"); o2_gated = sem("o2_gated")
        o2_split = sem("o2_split"); yc_done = sem("yc_done"); merged = sem("merged")
        cv_zero = sem("cv_zero")
        act_chain = sem("act_chain"); dve_chain = sem("dve_chain"); pool_chain = sem("pool_chain")
        out_written = sem("out_written")

        def wait_tile(eng, u, j):
            if UNIT[u][0] == NAT and j < 3:
                eng.wait_ge(natural_done, 3 * NATURAL_BEFORE[u] + j + 1)
            else:
                eng.wait_ge(piece_done, 4 * u + j + 1)

        def wait_evacuated(eng, u, j):
            eng.wait_ge(evacuated[j], tile_number(u, j) // 4 + 1)

        def bank(u, j):
            return proj[:, j, :]

        N_PARAMS = 18
        block = ctx.enter_context(nc.Block())

        @block.sync
        def _(sp):
            for s in range(ST):
                sp.dma_start(x_in[:, s, :], a["x"][0, s * P:(s + 1) * P, :]).then_inc(x_landed[s], 16)
            for n in range(PIECES):
                u, q = divmod(n, 4)
                kind, cols = UNIT[u]
                if n >= SLOTS:
                    sp.wait_ge(w_split, n - SLOTS + 1)
                if kind == NAT:
                    w, c = cols[0]
                    src = a[w][0, 256 * q:256 * q + 256, c:c + 512].rearrange("(k p) c -> p k c", p=P)
                    dst = w_raw[:, n % SLOTS, :].rearrange("p (k c) -> p k c", k=2)
                else:
                    w, c = cols[q]
                    src = a[w][0, :, c:c + P].rearrange("(k p) c -> p k c", p=P)
                    dst = w_raw[:, n % SLOTS, :].rearrange("p (k c) -> p k c", k=KC)
                sp.dma_start(dst, src).then_inc(raw_landed[n % SLOTS], 16)
            for h in range(2):
                for s in range(ST):
                    wait_evacuated(sp, U_OUT + h, s)
                    sp.dma_start(a["out"][0, s * P:(s + 1) * P, h * 512:(h + 1) * 512],
                                 x1[:, s, h * 512:(h + 1) * 512]).then_inc(out_written, 16)
            sp.wait_ge(out_written, 16 * 2 * ST)

        @block.gpsimd
        def _(pool):
            pool.memset(ident[:], 0.0).then_inc(pool_chain, 1)
            pool.wait_ge(pool_chain, 1)
            pool.affine_select(out=ident[:], in_=ident[:], compare_op=ALU.not_equal, fill=1.0, base=0,
                               pattern=[[-1, P]], channel_multiplier=1).then_inc(setup, 1)

            pool.iota(table[:, 0, :].bitcast(I32), pattern=[[1, TAB]], base=-CENTRE, channel_multiplier=-1).then_inc(setup, 1)
            pool.memset(mask[:], 0.0).then_inc(pool_chain, 1)
            pool.wait_ge(pool_chain, 2)
            pool.affine_select(out=mask[:], in_=mask[:], compare_op=ALU.is_ge, fill=BIG, base=P,
                               pattern=[[-1, 2 * P]], channel_multiplier=1).then_inc(pool_chain, 1)
            pool.wait_ge(pool_chain, 3)
            pool.affine_select(out=mask[:], in_=mask[:], compare_op=ALU.is_ge, fill=BIG, base=-1,
                               pattern=[[1, 2 * P]], channel_multiplier=-1).then_inc(setup_mask, 1)

            def split(n, slot):
                pool.tensor_scalar(w_hi[:, slot, :], w_raw[:, slot, :], 1.0, 1.0, ALU.mult, ALU.mult).then_inc(hi_done, 1)
                pool.wait_ge(hi_done, n + 1)
                pool.tensor_tensor(w_lo[:, slot, :], w_raw[:, slot, :], w_hi[:, slot, :].bitcast(F32),
                                   ALU.subtract).then_inc(w_split, 1)

            for n in range(SLOTS):
                pool.wait_ge(raw_landed[n], 16)
                split(n, n)
            with pool.Fori(1, PIECES // SLOTS) as g:
                for slot in range(SLOTS):
                    pool.wait_ge(raw_landed[slot], 16 * g + 16)
                    pool.wait_ge(piece_done, SLOTS * g + slot - SLOTS + 1)
                    pool.sem_inc(slot_open, 1)
                    split(SLOTS * g + slot, slot)

        @block.scalar
        def _(act):
            act.dma_start(norm_1[:], a["norm_w"][0, :].partition_broadcast(P)).then_inc(norm_1_landed, 16)
            act.dma_start(rows[0:R_GATE, :], a["conv_w_2"][0].rearrange("k (t p) -> (k t) p", p=P)).then_inc(params, 16)
            act.dma_start(rows[R_GATE:R_KW, :], a["gate_b_2"].rearrange("o (t p) -> (o t) p", p=P)).then_inc(params, 16)
            for i, w in enumerate(("k_norm_w", "q_norm_w", "k_norm_g_2", "q_norm_g_2")):
                for h in range(2):
                    act.dma_start(rows[R_KW + i:R_KW + i + 1, h * HD:(h + 1) * HD], a[w]).then_inc(params, 16)
            act.dma_start(rows[ROWS - 1:ROWS, :], a["subln_w"]).then_inc(params, 16)
            for i, w in enumerate(("lambda_q1", "lambda_q2", "lambda_k1", "lambda_k2")):
                act.dma_start(lam_v[:, i, :], a[w][0, :].partition_broadcast(P)).then_inc(params, 16)
            for i, w in enumerate(("ret_decay_fwd", "ret_decay_bwd")):
                act.dma_start(dec[:, 4 * i:4 * i + 4], a[w][0, :].partition_broadcast(P)).then_inc(params, 16)
            act.dma_start(sink[:], a["sinks_2"][0, :].partition_broadcast(P)).then_inc(params, 16)

            chain = [0]

            def done(ins):
                chain[0] += 1
                ins.then_inc(act_chain, 1)
                act.wait_ge(act_chain, chain[0])

            for s in range(ST):
                act.wait_ge(x_landed[s], 16)
                act.activation(xs_1[:, s, :], x_in[:, s, :], ACT.Square, accum_out=ssq[:, s:s + 1]).then_inc(ssq_done, 1)

            def take_xt(b):
                for i in range(8):
                    half, s = divmod(i, ST)
                    act.wait_ge(xt_done, 8 * b + i + 1)
                    act.activation(xt_hi[:, 4 * half:4 * half + 4, s * P:(s + 1) * P],
                                   proj[:, s, :].rearrange("p (k r) -> p k r", k=4), ACT.Copy).then_inc(xt_hi_done, 1)

            take_xt(0)
            act.wait_ge(dec_abs, 1)
            act.activation(dec_e[:], dec_a[:], ACT.Exp, scale=-1.0).then_inc(dec_exp, 1)
            act.wait_ge(lam_sum, 1)
            act.activation(lam_e[:], lam_s[:], ACT.Exp).then_inc(lam_exp, 1)

            squares = [0]

            def square(dst, src):
                if squares[0]:
                    act.wait_ge(sq_used, squares[0])
                act.activation(dst, src, ACT.Square).then_inc(sq_done, 1)
                squares[0] += 1

            last_tanh = ()

            for n in range(PIECES):
                for half in range(2):
                    for u, j in tiles_done(n, half):
                        if u >= U_CONV and u < U_GATE_A and j in (1, 2):
                            continue
                        if u >= U_GATE_A and (u >= U_OUT or j % 2):
                            continue
                        wait_tile(act, u, j)
                        b = bank(u, j)
                        if u in (U_K, U_Q):
                            if u == U_Q:
                                act.wait_ge(t_done, T_USE[("KT", 3)] + 1)
                            act.activation(stage[:, j, :], b, ACT.Copy).then_inc(evacuated[j], 1)
                            wait_evacuated(act, u, j)
                            square(sq[:], stage[:, j, :])
                        elif u in (U_V, U_RV):
                            act.activation((va if u == U_V else vr)[:, j, :], b, ACT.Copy).then_inc(evacuated[j], 1)
                        elif u == U_RQK:
                            act.activation(rqkT[:, j, :], b, ACT.Copy, scale=1.0 if j < 2 else QK_SCALE).then_inc(evacuated[j], 1)
                        elif u in (U_O0, U_O1):
                            h = u - U_O0
                            wait_evacuated(act, u, j)
                            act.wait_ge(sq_used, squares[0])
                            act.wait_ge(ssq_done, ST + ST * h + j)
                            act.activation(sq[:], x1[:, j, h * 512:(h + 1) * 512], ACT.Square,
                                           accum_out=ssq_half[:, j, h:h + 1]).then_inc(ssq_done, 1)
                        elif u == U_KV:
                            done(act.activation(v2[:, j, :], b[:, 256:512], ACT.Copy))
                            act.activation(stage2[:, j, 0:256], b[:, 0:256], ACT.Copy).then_inc(evacuated[j], 1)
                            wait_evacuated(act, u, j)
                            square(sq2[:, 0:256], stage2[:, j, 0:256])
                        elif u in (U_Q20, U_Q21):
                            if u == U_Q20:
                                act.wait_ge(heads_done, 8 + ST)
                            else:
                                act.wait_ge(t_done, T_USE[("QT2", 3)] + 1)
                            act.activation(stage2[:, j, :], b, ACT.Copy).then_inc(evacuated[j], 1)
                            wait_evacuated(act, u, j)
                            square(sq2[:], stage2[:, j, :])
                        elif U_CONV <= u < U_GATE_A and j == 0:
                            if u > U_CONV:
                                wait_evacuated(act, u - 1, 1)
                            act.activation(vt[:], b, ACT.Copy).then_inc(evacuated[0], 1)
                        else:
                            if U_CONV < u <= U_GATE_A and last_tanh[0] < U_GATE_A:
                                act.wait_ge(yc_done, u - U_CONV)
                            elif last_tanh:
                                wait_evacuated(act, last_tanh[0], last_tanh[1] + (u >= U_GATE_A))
                            last_tanh = (u, j)
                            if u in (U_GA, U_GR):
                                act.activation(th[:], b, ACT.Tanh, scale=0.5).then_inc(th_done, 1)
                            elif u < U_GATE_A:
                                act.activation(th2[:], b, ACT.Tanh, scale=0.5).then_inc(th_done, 1)
                            else:
                                t = 2 * ((u - U_GATE_A) % (KC // 2)) + j // 2 + (KC if u >= U_GATE_B else 0)
                                act.activation(th2[:], b, ACT.Tanh, bias=half_b[:, t:t + 1], scale=0.5).then_inc(evacuated[j], 1)

                    for kind, m in STEPS[(n, half)]:
                        if kind in ("KT", "QT"):
                            if (kind, m) == ("KT", 0):
                                act.wait_ge(weights_ready, 1)
                            act.wait_ge(t_done, T_USE[(kind, m)] + 1)
                            act.activation((kT if kind == "KT" else qT)[:, m, :], bank_t[:], ACT.Copy,
                                           scale=(kw if kind == "KT" else qws[:])).then_inc(t_free, 1)
                        elif kind == "TW":
                            act.wait_ge(t_done, T_USE[(kind, m)] + 1)
                            if m >= 2:
                                act.wait_ge(av_done, m - 1)
                            act.activation(wT[:, m % 2, :], bank_t[:], ACT.Copy).then_inc(t_free, 1)
                        elif kind == "S":
                            act.wait_ge(neg_max, m + 1)
                            for mp in range(2):
                                act.activation(prob[:, m % 2, mp, :], prob[:, m % 2, mp, :], ACT.Exp,
                                               bias=neg_mx[:, m % 2, mp:mp + 1],
                                               accum_out=den[:, m % 2, mp:mp + 1]).then_inc(exp_done, 1)
                        elif kind in ("AV", "RA") and m % ST == ST - 1:
                            h = m // ST + (DA_HEADS if kind == "RA" else 0)
                            act.wait_ge(av_done, ST * h + ST)
                            if h >= 4:
                                act.wait_ge(t_done, T_USE[("F", h - 4)] + 1)
                            o = o_raw[:, h % 4, :, :].rearrange("p i v -> p (i v)")
                            act.activation(o, bank_o[:], ACT.Copy).then_inc(o_free, 1)
                            act.wait_ge(o_free, h + 1)
                            square(sq[:], o)
                        elif kind in ("KT2", "QT2"):
                            act.wait_ge(t_done, T_USE[(kind, m)] + 1)
                            act.activation((kT2 if kind == "KT2" else qT2)[:, m, :], bank_t[:], ACT.Copy,
                                           scale=(k2w if kind == "KT2" else q2ws[:])).then_inc(t_free, 1)
                        elif kind == "S2":
                            width = P if m < KV_HEADS else 2 * P
                            act.wait_ge(neg_max2, m + 1)
                            for r in range(GROUP):
                                act.activation(prob2[:, m % 2, r, 0:width], prob2[:, m % 2, r, 0:width], ACT.Exp,
                                               bias=neg_m2[:, m % 4, r:r + 1], accum_out=den2[:, m % 4, r:r + 1])
                            act.activation(sink_e[:, m % 4, :], sink_m[:, m % 4, :], ACT.Exp).then_inc(exp2_done, 1)
                        elif kind == "TPa":
                            act.wait_ge(t_done, T_USE[(kind, m)] + 1)
                            if m >= 2:
                                act.wait_ge(av2_done, m - 1)
                            chunks = 1 if m < KV_HEADS else 2
                            act.activation(pT[:, m % 2, 0, :].rearrange("p (r x) -> p r x", r=2)[:, :, 0:chunks * P],
                                           bank_t[:].rearrange("p (r x) -> p r x", r=2)[:, :, 0:chunks * P],
                                           ACT.Copy).then_inc(t_free, 1)
                    g = 2 * (n - DA_FIRST) + half
                    if DA_STEPS - 1 <= g < DA_STEPS - 1 + 4 * RET_HEADS and (g - DA_STEPS + 1) % 4 == 0:
                        h = (g - DA_STEPS + 1) // 4
                        act.wait_ge(decay_arg, h + 1)
                        act.activation(table[:, h % 2, :], table[:, h % 2, :], ACT.Exp).then_inc(decay_done, 1)
                    if (n, half) == (4 * U_GR + 3, 1):
                        act.wait_ge(scores_done, DA_STEPS)
                        act.dma_start(x1[:], a["x"][0].rearrange("(t p) d -> p t d", p=P)).then_inc(x_again, 16)
                        act.wait_ge(av_done, DA_STEPS)
                        act.dma_start(norm_2, a["norm_g_2"][0, :].partition_broadcast(P)).then_inc(norm_2_landed, 16)
                    if (n, half) == (4 * U_O1 + 3, 1):
                        take_xt(1)

        @block.vector
        def _(dve):
            chain = [0]

            def done(ins):
                chain[0] += 1
                ins.then_inc(dve_chain, 1)
                dve.wait_ge(dve_chain, chain[0])

            def rsqrt(n, width):
                v, y, t = rs_v[:, 0:n], rs_y[:, 0:n], rs_t[:, 0:n]
                done(dve.tensor_scalar(v, v, 1.0 / width, EPS, ALU.mult, ALU.add))
                done(dve.tensor_scalar(t.bitcast(I32), v.bitcast(I32), 1, None, ALU.logical_shift_right))
                done(dve.tensor_scalar(y.bitcast(I32), t.bitcast(I32), -1.0, float(RSQRT_SEED), ALU.mult, ALU.add))
                for _ in range(3):
                    done(dve.scalar_tensor_tensor(out=t, in0=y, scalar=-0.5, in1=y, op0=ALU.mult, op1=ALU.mult))
                    done(dve.tensor_tensor(t, t, v, ALU.mult))
                    done(dve.scalar_tensor_tensor(out=y, in0=t, scalar=1.5, in1=y, op0=ALU.add, op1=ALU.mult))

            def take_xt_low(b):
                for i in range(8):
                    half, s = divmod(i, ST)
                    dve.wait_ge(xt_hi_done, 8 * b + i + 1)
                    dst = (slice(None), slice(4 * half, 4 * half + 4), slice(s * P, (s + 1) * P))
                    dve.tensor_tensor(xt_lo[dst], proj[:, s, :].rearrange("p (k r) -> p k r", k=4),
                                      xt_hi[dst].bitcast(F32), ALU.subtract).then_inc(evacuated[s], 1)

            dve.wait_ge(ssq_done, ST)
            done(dve.tensor_copy(rs_v[:, 0:ST], ssq[:]))
            rsqrt(ST, D)
            dve.wait_ge(norm_1_landed, 16)
            for s in range(ST):
                dve.scalar_tensor_tensor(out=xs_1[:, s, :], in0=x_in[:, s, :], scalar=rs_y[:, s:s + 1], in1=norm_1[:],
                                         op0=ALU.mult, op1=ALU.mult).then_inc(xs_done, 1)
            dve.wait_ge(params, 16 * N_PARAMS)
            done(dve.tensor_scalar(dec_a[:], dec[:], -1.0, None, ALU.mult))
            dve.tensor_tensor(dec_a[:], dec_a[:], dec[:], ALU.max).then_inc(dec_abs, 1)
            take_xt_low(0)
            dve.wait_ge(rows_turned, 1)
            done(dve.tensor_copy(cols[:], bank_t[:, 0:ROWS]))
            done(dve.tensor_tensor_reduce(lam_j[:], lam_v[:, 0, :], lam_v[:, 2, :], 1.0, 0.0, ALU.mult, ALU.add, lam_s[:, 0:1]))
            dve.tensor_tensor_reduce(lam_j[:], lam_v[:, 1, :], lam_v[:, 3, :], 1.0, 0.0, ALU.mult, ALU.add,
                                     lam_s[:, 1:2]).then_inc(lam_sum, 1)
            dve.tensor_scalar(q2ws[:], q2w, QK_SCALE, None, ALU.mult)
            dve.tensor_scalar(sub_s[:], sub_w, 1.0 - LAMBDA_INIT, 0.5, ALU.mult, ALU.mult)
            dve.tensor_scalar(neg_sink[:], sink[:], -1.0, None, ALU.mult)
            dve.tensor_scalar(half_b[:], gate_b, 0.5, None, ALU.mult)
            dve.tensor_scalar(qws[:], qw, QK_SCALE, None, ALU.mult).then_inc(weights_ready, 1)
            dve.wait_ge(dec_exp, 1)
            done(dve.tensor_scalar(dec_z[:], dec_e[:], 2.0, None, ALU.add))
            done(dve.reciprocal(dec_z[:], dec_z[:]))
            done(dve.tensor_tensor(dec_z[:], dec_z[:], dec_e[:], ALU.mult))
            done(dve.tensor_tensor(dec_q[:], dec_z[:], dec_z[:], ALU.mult))
            done(dve.tensor_scalar(dec_p[:], dec_q[:], 1.0 / 17, None, ALU.mult))
            for k in range(15, 2, -2):
                done(dve.scalar_tensor_tensor(out=dec_p[:], in0=dec_p[:], scalar=1.0 / k, in1=dec_q[:], op0=ALU.add, op1=ALU.mult))
            done(dve.scalar_tensor_tensor(out=dec_p[:], in0=dec_p[:], scalar=1.0, in1=dec_z[:], op0=ALU.add, op1=ALU.mult))
            done(dve.tensor_scalar(dec_p[:], dec_p[:], 2.0, None, ALU.mult))
            done(dve.scalar_tensor_tensor(out=log_g[:], in0=dec[:], scalar=0.0, in1=dec_p[:], op0=ALU.min, op1=ALU.subtract))
            done(dve.tensor_scalar(neg_log_b[:], log_g[:, 4:8], -1.0, None, ALU.mult))
            dve.wait_ge(lam_exp, 1)
            done(dve.scalar_tensor_tensor(out=lam[:], in0=lam_e[:, 0:1], scalar=LAMBDA_INIT, in1=lam_e[:, 1:2],
                                          op0=ALU.add, op1=ALU.subtract))
            dve.wait_ge(setup, 2)
            done(dve.tensor_copy(diff[:], table[:, 0, :].bitcast(I32)))

            def distance_table(h):
                slope = 2.0 ** (-8.0 * (h + 1) / DA_HEADS)
                done(dve.tensor_scalar(table[:, h % 2, :], diff[:], -slope, None, ALU.mult))
                done(dve.scalar_tensor_tensor(out=table[:, h % 2, :], in0=diff[:], scalar=slope, in1=table[:, h % 2, :],
                                              op0=ALU.mult, op1=ALU.max))

            def decay_exponent(h):
                done(dve.tensor_scalar(table[:, h % 2, :], diff[:], neg_log_b[:, h:h + 1], None, ALU.mult))
                dve.scalar_tensor_tensor(out=table[:, h % 2, :], in0=diff[:], scalar=log_g[:, h:h + 1], in1=table[:, h % 2, :],
                                         op0=ALU.mult, op1=ALU.min).then_inc(decay_arg, 1)

            distance_table(0)
            distance_table(1)

            sums = [0]

            def head_sums(dst, buf, heads):
                sums[0] += 1
                dve.wait_ge(sq_done, sums[0])
                dve.tensor_reduce(dst, buf.rearrange("p (h d) -> p h d", h=heads), AXX, ALU.add).then_inc(sq_used, 1)

            tanhs = [0]

            for n in range(PIECES):
                for half in range(2):
                    for u, j in tiles_done(n, half):
                        b = bank(u, j)
                        if u in (U_K, U_Q, U_KV, U_Q20, U_Q21):
                            heads = 4 if u == U_KV else 8
                            st, buf = (stage, sq) if u < U_KV else (stage2, sq2)
                            head_sums(rs_v[:, heads * j:heads * j + heads], buf[:, 0:heads * HD], heads)
                            if j == 3:
                                dve.wait_ge(sq_used, sums[0])
                                rsqrt(4 * heads, HD)
                                for s in range(ST):
                                    y = rs_y[:, heads * s:heads * s + heads]
                                    src = st[:, s, 0:heads * HD].rearrange("p (h d) -> p h d", h=heads)
                                    if u == U_KV:
                                        dve.tensor_tensor(
                                            k_dup[:, s, :].rearrange("p (h c d) -> p h c d", h=4, c=2),
                                            src.unsqueeze(2).broadcast_to([P, 4, 2, HD]),
                                            y.unsqueeze(2).unsqueeze(3).broadcast_to([P, 4, 2, HD]), ALU.mult).then_inc(heads_done, 1)
                                    else:
                                        dve.tensor_tensor(src, src, y.unsqueeze(2).broadcast_to([P, heads, HD]),
                                                          ALU.mult).then_inc(heads_done, 1)
                        elif u in (U_GA, U_GR, U_Z0, U_Z1):
                            tanhs[0] += 1
                            dve.wait_ge(th_done, tanhs[0])
                            dst = gT[:, 4 * (u - U_GA) + j, :] if u <= U_GR else gT2[:, 4 * (u - U_Z0) + j, :]
                            dve.scalar_tensor_tensor(out=dst, in0=(th if u <= U_GR else th2)[:], scalar=1.0, in1=b,
                                                     op0=ALU.add, op1=ALU.mult).then_inc(evacuated[j], 1)
                        elif u in (U_O0, U_O1, U_OUT, U_OUT + 1):
                            if (u, j) == (U_O0, 0):
                                dve.wait_ge(x_again, 16)
                            wait_tile(dve, u, j)
                            h = (u - U_O0) if u <= U_O1 else u - U_OUT
                            xh = x1[:, j, h * 512:(h + 1) * 512]
                            dve.tensor_tensor(xh, b, xh, ALU.add).then_inc(evacuated[j], 1)
                        elif U_CONV <= u < U_GATE_A:
                            t = u - U_CONV
                            if j == 0 and t == 0:
                                dve.memset(cv[:, 0:2], 0.0).then_inc(cv_zero, 1)
                                dve.wait_ge(cv_zero, 1)
                            if j == 1:
                                wait_evacuated(dve, u, 0)
                                wait_tile(dve, u, 1)
                                dve.tensor_tensor(cv[:, 2:S + 2], b, vt[:], ALU.mult).then_inc(evacuated[1], 1)
                                wait_evacuated(dve, u, 1)
                                done(dve.tensor_scalar(acc[:], cv[:, 0:S], conv_w[:, 0, t:t + 1], None, ALU.mult))
                                for k in (1, 2):
                                    done(dve.scalar_tensor_tensor(out=acc[:], in0=cv[:, k:S + k], scalar=conv_w[:, k, t:t + 1],
                                                                  in1=acc[:], op0=ALU.mult, op1=ALU.add))
                            if j == 2:
                                wait_tile(dve, u, 2)
                                dve.tensor_tensor(acc[:], b, acc[:], ALU.mult).then_inc(evacuated[2], 1)
                                wait_evacuated(dve, u, 2)
                            if j == 3:
                                tanhs[0] += 1
                                dve.wait_ge(th_done, tanhs[0])
                                dve.scalar_tensor_tensor(out=th2[:], in0=th2[:], scalar=1.0, in1=b,
                                                         op0=ALU.add, op1=ALU.mult).then_inc(evacuated[3], 1)
                                wait_evacuated(dve, u, 3)
                                done(dve.scalar_tensor_tensor(out=acc[:], in0=acc[:], scalar=0.5, in1=th2[:], op0=ALU.mult, op1=ALU.mult))
                                done(dve.tensor_copy(yc_hi[:, t, :], acc[:]))
                                dve.tensor_tensor(yc_lo[:, t, :], acc[:], yc_hi[:, t, :].bitcast(F32), ALU.subtract).then_inc(yc_done, 1)
                        elif U_GATE_A <= u < U_OUT and j % 2:
                            t = 2 * ((u - U_GATE_A) % (KC // 2)) + j // 2
                            wait_evacuated(dve, u, j - 1)
                            wait_tile(dve, u, j)
                            if u >= U_GATE_B and t:
                                dve.wait_ge(merged, t)
                            dst = part[:, t, :] if u < U_GATE_B else acc[:]
                            dve.scalar_tensor_tensor(out=dst, in0=th2[:], scalar=1.0, in1=b,
                                                     op0=ALU.add, op1=ALU.mult).then_inc(evacuated[j], 1)
                            if u >= U_GATE_B:
                                wait_evacuated(dve, u, j)
                                done(dve.tensor_tensor(acc[:], acc[:], part[:, t, :], ALU.add))
                                done(dve.tensor_scalar(yc_hi[:, t, :], acc[:], 0.5, None, ALU.mult))
                                dve.scalar_tensor_tensor(out=yc_lo[:, t, :], in0=acc[:], scalar=0.5, in1=yc_hi[:, t, :].bitcast(F32),
                                                         op0=ALU.mult, op1=ALU.subtract).then_inc(merged, 1)

                    if (n, half) == (4 * U_O1 + 3, 1):
                        dve.wait_ge(ssq_done, ST + 2 * ST)
                        done(dve.tensor_tensor(rs_v[:, 0:ST], ssq_half[:, :, 0], ssq_half[:, :, 1], ALU.add))
                        rsqrt(ST, D)
                        dve.wait_ge(norm_2_landed, 16)
                        for s in range(ST):
                            dve.scalar_tensor_tensor(out=xs_2[:, s, :], in0=x1[:, s, :], scalar=rs_y[:, s:s + 1], in1=norm_2,
                                                     op0=ALU.mult, op1=ALU.mult).then_inc(xs_done, 1)
                        take_xt_low(1)

                    for kind, m in STEPS[(n, half)]:
                        if kind == "S":
                            h, i = divmod(m, ST)
                            sl = m % 2
                            dve.wait_ge(scores_done, m + 1)
                            if m >= 2:
                                dve.wait_ge(t_done, T_USE[("TW", m - 2)] + 1)
                            for mp in range(2):
                                dve.tensor_tensor_reduce(prob[:, sl, mp, :], score[:, mp, :], table[:, h % 2, CENTRE - i * P:CENTRE - i * P + S],
                                                         1.0, -3e38, ALU.subtract, ALU.max, mx[:, sl, mp:mp + 1]).then_inc(score_read, 1)
                            dve.wait_ge(score_read, 2 * m + 2)
                            dve.tensor_scalar(neg_mx[:, sl, :], mx[:, sl, :], -1.0, None, ALU.mult).then_inc(neg_max, 1)
                            if i == ST - 1 and h + 2 < DA_HEADS:
                                distance_table(h + 2)
                            elif i == ST - 1:
                                decay_exponent(h + 2 - DA_HEADS)
                            dve.wait_ge(exp_done, 2 * m + 2)
                            done(dve.reciprocal(rec[:, sl, :], den[:, sl, :]))
                            done(dve.tensor_tensor(lam_rec[:, sl, :], rec[:, sl, 1:2], lam[:], ALU.mult))
                            done(dve.tensor_scalar(prob[:, sl, 1, :], prob[:, sl, 1, :], lam_rec[:, sl, 0:1], None, ALU.mult))
                            dve.scalar_tensor_tensor(out=prob[:, sl, 0, :], in0=prob[:, sl, 0, :], scalar=rec[:, sl, 0:1],
                                                     in1=prob[:, sl, 1, :], op0=ALU.mult, op1=ALU.subtract).then_inc(weight_done, 1)
                        elif kind == "RS":
                            h, i = divmod(m, ST)
                            if i == 0:
                                dve.wait_ge(decay_done, h + 1)
                            dve.wait_ge(ret_scores, m + 1)
                            if m < 2:
                                dve.wait_ge(t_done, T_USE[("TW", DA_STEPS - 2 + m)] + 1)
                            else:
                                dve.wait_ge(av_done, DA_STEPS + m - 1)
                            dve.tensor_tensor(prob[:, m % 2, 0, :], score[:, m % 2, :], table[:, h % 2, i * P:i * P + S],
                                              ALU.mult).then_inc(ret_weight, 1)
                            if i == ST - 1 and h + 2 < RET_HEADS:
                                dve.wait_ge(ret_weight, m + 1)
                                decay_exponent(h + 2)
                        elif kind in ("AV", "RA") and m % ST == ST - 1:
                            h = m // ST + (DA_HEADS if kind == "RA" else 0)
                            head_sums(rs_v[:, 0:ST], sq[:], ST)
                            dve.wait_ge(sq_used, sums[0])
                            rsqrt(ST, P)
                            o = o_raw[:, h % 4, :, :]
                            dve.tensor_tensor(o, o, rs_y[:, 0:ST].unsqueeze(2).broadcast_to([P, ST, P]), ALU.mult).then_inc(o_normed, 1)
                        elif kind == "F":
                            dve.wait_ge(t_done, T_USE[(kind, m)] + 1)
                            wait_evacuated(dve, U_GA + m // 4, m % 4)
                            dve.scalar_tensor_tensor(out=gT[:, m, :], in0=bank_t[:], scalar=sub_s[:, 0:1] if m < DA_HEADS else 0.5,
                                                     in1=gT[:, m, :], op0=ALU.mult, op1=ALU.mult).then_inc(t_free, 1)
                            dve.wait_ge(t_free, T_USE[(kind, m)] + 1)
                            done(dve.tensor_copy(mix_hi[:, m, :], gT[:, m, :]))
                            dve.tensor_tensor(mix_lo[:, m, :], gT[:, m, :], mix_hi[:, m, :].bitcast(F32), ALU.subtract).then_inc(mixed, 1)
                        elif kind == "S2":
                            i, j = divmod(m, KV_HEADS)
                            width = P if i == 0 else 2 * P
                            if m == 0:
                                dve.wait_ge(setup_mask, 1)
                            dve.wait_ge(scores2, m + 1)
                            if m >= 2:
                                dve.wait_ge(t_done, T_USE[("TPb", m - 2)] + 1)
                            for r in range(GROUP):
                                last = dve.tensor_tensor_reduce(
                                    prob2[:, m % 2, r, 0:width], score[:, r % 2, (r // 2) * 256:(r // 2) * 256 + width],
                                    mask[:, 2 * P - width:2 * P], 1.0, -3e38, ALU.subtract, ALU.max, mx2[:, m % 4, r:r + 1])
                            last.then_inc(score2_read, 1)
                            dve.wait_ge(score2_read, m + 1)
                            done(dve.scalar_tensor_tensor(out=neg_m2[:, m % 4, :], in0=mx2[:, m % 4, :], scalar=-1.0,
                                                          in1=neg_sink[:, 4 * j:4 * j + 4], op0=ALU.mult, op1=ALU.min))
                            dve.tensor_tensor(sink_m[:, m % 4, :], neg_m2[:, m % 4, :], sink[:, 4 * j:4 * j + 4], ALU.add).then_inc(neg_max2, 1)
                        elif kind == "TPb":
                            dve.wait_ge(t_done, T_USE[(kind, m)] + 1)
                            if m >= 2:
                                dve.wait_ge(av2_done, m - 1)
                            chunks = 1 if m < KV_HEADS else 2
                            dve.tensor_copy(pT[:, m % 2, 1, :].rearrange("p (r x) -> p r x", r=2)[:, :, 0:chunks * P],
                                            bank_t[:].rearrange("p (r x) -> p r x", r=2)[:, :, 0:chunks * P]).then_inc(t_free, 1)
                        elif kind == "AV2":
                            dve.wait_ge(exp2_done, m + 1)
                            done(dve.tensor_tensor(den2[:, m % 4, :], den2[:, m % 4, :], sink_e[:, m % 4, :], ALU.add))
                            done(dve.reciprocal(rec2[:, m % 4, :], den2[:, m % 4, :]))
                            dve.wait_ge(av2_done, m + 1)
                            if m >= 4:
                                dve.wait_ge(o2_turned, m - 3)
                            dve.tensor_tensor(o2n[:, m % 4, :].rearrange("p (r d) -> p r d", r=GROUP),
                                              bank_o[:, 0:256].rearrange("p (r d) -> p r d", r=GROUP),
                                              rec2[:, m % 4, :].unsqueeze(2).broadcast_to([P, GROUP, HD]), ALU.mult).then_inc(o2_normed, 1)
                        elif kind == "F2":
                            i, j = divmod(m, KV_HEADS)
                            dve.wait_ge(o2_turned, m + 1)
                            for c in (2 * j, 2 * j + 1):
                                wait_evacuated(dve, U_Z0 + c // 4, c % 4)
                            g2 = gT2[:, 2 * j:2 * j + 2, i * P:(i + 1) * P]
                            dve.scalar_tensor_tensor(out=g2, in0=bank_o[:, 256:512].rearrange("p (c r) -> p c r", c=2), scalar=0.5,
                                                     in1=g2, op0=ALU.mult, op1=ALU.mult).then_inc(o2_gated, 1)
                        elif kind == "OS":
                            dve.wait_ge(o2_gated, WIN_STEPS)
                            done(dve.tensor_copy(o2_hi[:, m, :], gT2[:, m, :]))
                            dve.tensor_tensor(o2_lo[:, m, :], gT2[:, m, :], o2_hi[:, m, :].bitcast(F32), ALU.subtract).then_inc(o2_split, 1)

        @block.tensor
        def _(pe):
            def products(out, left, right, first, last):
                pe.matmul(out, left[0], right[0], start=first, stop=False)
                pe.matmul(out, left[0], right[1], start=False, stop=False)
                return pe.matmul(out, left[1], right[0], start=False, stop=last)

            def transposes(step, sources, outs):
                if T_USE[step]:
                    pe.wait_ge(t_free, T_USE[step])
                for src, dst in zip(sources, outs):
                    last = pe.transpose(dst, src, ident[:])
                last.then_inc(t_done, 1)

            def row_transposes(b, xs):
                for i in range(8):
                    half, s = divmod(i, ST)
                    pe.wait_ge(xs_done, ST * b + s + 1)
                    use = half + (0 if b == 0 else tile_number(U_O1, s) // 4 + 1)
                    if use:
                        pe.wait_ge(evacuated[s], use)
                    for k in range(4):
                        c = 4 * half + k
                        last = pe.transpose(proj[:, s, k * P:(k + 1) * P], xs[:, s, c * P:(c + 1) * P], ident[:])
                    last.then_inc(xt_done, 1)

            def quarters(t):
                return [t[:, c * P:(c + 1) * P] for c in range(4)]

            def step(kind, m):
                if kind in ("KT", "QT"):
                    pe.wait_ge(heads_done, ST if kind == "KT" else 2 * ST)
                    transposes((kind, m), [stage[:, s, m * P:(m + 1) * P] for s in range(ST)], quarters(bank_t))
                elif kind == "S":
                    h, i = divmod(m, ST)
                    if m == 0:
                        pe.wait_ge(t_free, T_USE[("QT", 3)] + 1)
                    else:
                        pe.wait_ge(score_read, 2 * m)
                    for mp in range(2):
                        r = slice(mp * HD, (mp + 1) * HD)
                        last = pe.matmul(score[:, mp, :], qT[r, h, i * P:(i + 1) * P], kT[r, h, :], start=True, stop=True)
                    last.then_inc(scores_done, 1)
                elif kind == "TW":
                    pe.wait_ge(weight_done, m + 1)
                    transposes((kind, m), quarters(prob[:, m % 2, 0, :]), quarters(bank_t))
                elif kind == "AV":
                    h, i = divmod(m, ST)
                    pe.wait_ge(t_free, T_USE[("TW", m)] + 1)
                    if m == 0:
                        for j in range(ST):
                            wait_evacuated(pe, U_V, j)
                    if i == 0 and h:
                        pe.wait_ge(o_free, h)
                    for c in range(4):
                        last = pe.matmul(bank_o[:, i * P:(i + 1) * P], wT[:, m % 2, c * P:(c + 1) * P],
                                         va[:, c, h * P:(h + 1) * P], start=(c == 0), stop=(c == 3))
                    last.then_inc(av_done, 1)
                elif kind == "RS":
                    h, i = divmod(m, ST)
                    r = slice((h % 2) * HD, (h % 2 + 1) * HD)
                    if m == 0:
                        for j in range(4):
                            wait_evacuated(pe, U_RQK, j)
                    if m < 2:
                        pe.wait_ge(score_read, 2 * DA_STEPS)
                    else:
                        pe.wait_ge(ret_weight, m - 1)
                    for c in range(4):
                        k = ST - 1 - c
                        last = pe.matmul(score[:, m % 2, c * P:(c + 1) * P], rqkT[r, 2 + h // 2, k * P:(k + 1) * P],
                                         rqkT[r, h // 2, i * P:(i + 1) * P], start=True, stop=True)
                    last.then_inc(ret_scores, 1)
                elif kind == "RA":
                    h, i = divmod(m, ST)
                    pe.wait_ge(ret_weight, m + 1)
                    if m == 0:
                        for j in range(ST):
                            wait_evacuated(pe, U_RV, j)
                    if i == 0:
                        pe.wait_ge(o_free, DA_HEADS + h)
                    for c in range(4):
                        last = pe.matmul(bank_o[:, i * P:(i + 1) * P], prob[:, m % 2, 0, c * P:(c + 1) * P],
                                         vr[:, ST - 1 - c, h * P:(h + 1) * P], start=(c == 0), stop=(c == 3))
                    last.then_inc(av_done, 1)
                elif kind == "F":
                    pe.wait_ge(o_normed, m + 1)
                    transposes((kind, m), [o_raw[:, m % 4, i, :] for i in range(ST)], quarters(bank_t))
                elif kind == "KT2":
                    pe.wait_ge(heads_done, 3 * ST)
                    transposes((kind, m), [k_dup[:, s, m * P:(m + 1) * P] for s in range(ST)], quarters(bank_t))
                elif kind == "QT2":
                    pe.wait_ge(heads_done, (4 + m // 4) * ST)
                    transposes((kind, m), [stage2[:, s, (m % 4) * P:(m % 4 + 1) * P] for s in range(ST)], quarters(bank_t))
                elif kind == "S2":
                    i, j = divmod(m, KV_HEADS)
                    keys = slice(max(i - 1, 0) * P, (i + 1) * P)
                    width = P if i == 0 else 2 * P
                    if m == 0:
                        pe.wait_ge(t_free, T_USE[("QT2", 7)] + 1)
                        pe.wait_ge(ret_weight, DA_STEPS)
                    else:
                        pe.wait_ge(score2_read, m)
                    for r in range(GROUP):
                        half = slice((r % 2) * HD, (r % 2 + 1) * HD)
                        last = pe.matmul(score[:, r % 2, (r // 2) * 256:(r // 2) * 256 + width],
                                         qT2[half, 2 * j + r // 2, i * P:(i + 1) * P], kT2[half, j, keys], start=True, stop=True)
                    last.then_inc(scores2, 1)
                elif kind in ("TPa", "TPb"):
                    pe.wait_ge(exp2_done, m + 1)
                    chunks = 1 if m < KV_HEADS else 2
                    first = 0 if kind == "TPa" else 2
                    pairs = [(r, c) for r in range(2) for c in range(chunks)]
                    transposes((kind, m), [prob2[:, m % 2, first + r, c * P:(c + 1) * P] for r, c in pairs],
                               [bank_t[:, (2 * r + c) * P:(2 * r + c + 1) * P] for r, c in pairs])
                elif kind == "AV2":
                    i, j = divmod(m, KV_HEADS)
                    pe.wait_ge(t_free, T_USE[("TPb", m)] + 1)
                    if m == 0:
                        for s in range(ST):
                            wait_evacuated(pe, U_KV, s)
                        pe.wait_ge(o_free, DA_HEADS + RET_HEADS)
                    else:
                        pe.wait_ge(o2_normed, m)
                    if m >= 2:
                        pe.wait_ge(o2_gated, m - 1)
                    chunks = 1 if i == 0 else 2
                    for r in range(GROUP):
                        for c in range(chunks):
                            tile = i - chunks + 1 + c
                            last = pe.matmul(bank_o[:, r * HD:(r + 1) * HD], pT[:, m % 2, r // 2, (2 * (r % 2) + c) * P:(2 * (r % 2) + c + 1) * P],
                                             v2[:, tile, j * HD:(j + 1) * HD], start=(c == 0), stop=(c == chunks - 1))
                    last.then_inc(av2_done, 1)
                elif kind == "F2":
                    pe.wait_ge(o2_normed, min(m + 2, WIN_STEPS))
                    if m:
                        pe.wait_ge(o2_gated, m)
                    for c in range(2):
                        last = pe.transpose(bank_o[:, (2 + c) * P:(3 + c) * P], o2n[:, m % 4, c * P:(c + 1) * P], ident[:])
                    last.then_inc(o2_turned, 1)

            pe.wait_ge(setup, 1)
            row_transposes(0, xs_1)
            pe.wait_ge(params, 16 * N_PARAMS)
            pe.transpose(bank_t[:, 0:ROWS], rows[:], ident[0:ROWS, 0:ROWS]).then_inc(rows_turned, 1)
            for n in range(PIECES):
                u, q = divmod(n, 4)
                slot = n % SLOTS
                if u == U_KV and q == 0:
                    row_transposes(1, xs_2)
                if u in (U_O0, U_O1):
                    left = (mix_hi, mix_lo)
                elif u >= U_OUT:
                    left = (yc_hi, yc_lo)
                else:
                    left = (xt_hi, xt_lo)
                if UNIT[u][0] == NAT:
                    w = [t[:, slot, :].rearrange("p (k c) -> p k c", k=2) for t in (w_hi, w_lo)]
                    order = [(kk, s) for kk in range(2) for s in range(ST)] if q < 3 else [(kk, s) for s in range(ST) for kk in range(2)]
                    for e, (kk, s) in enumerate(order):
                        if q == 0 and kk == 0:
                            pe.wait_ge(evacuated[s], tile_number(u, s) // 4)
                        if u == U_O0 and (s == 0 or q == 3):
                            pe.wait_ge(mixed, 2 * q + kk + 1)
                        if u == U_OUT and (s == 0 or q == 3):
                            pe.wait_ge(merged, 2 * q + kk + 1)
                        if e == 0:
                            pe.wait_ge(w_split, n + 1)
                        k = 2 * q + kk
                        last = products(bank(u, s), [t[:, k, s * P:(s + 1) * P] for t in left], [t[:, kk, :] for t in w],
                                        k == 0, k == KC - 1)
                        if e == 7:
                            last.then_inc(piece_done, 1)
                        elif q == 3 and kk == 1:
                            last.then_inc(natural_done, 1)
                        if e % 4 == 3:
                            for kind, m in STEPS[(n, e // 4)]:
                                step(kind, m)
                else:
                    w = [t[:, slot, :].rearrange("p (k c) -> p k c", k=KC) for t in (w_hi, w_lo)]
                    right = left
                    if U_GATE_A <= u < U_OUT and q % 2:
                        right = (yc_hi, yc_lo) if u < U_GATE_B else (o2_hi, o2_lo)
                        if u == U_GATE_A:
                            pe.wait_ge(yc_done, KC)
                        if u == U_GATE_B:
                            pe.wait_ge(o2_split, KC)
                    pe.wait_ge(evacuated[q], tile_number(u, q) // 4)
                    pe.wait_ge(w_split, n + 1)
                    for k in range(KC):
                        last = products(bank(u, q), [t[:, k, :] for t in w], [t[:, k, :] for t in right], k == 0, k == KC - 1)
                        if k == KC - 1:
                            last.then_inc(piece_done, 1)
                        if k % 4 == 3:
                            for kind, m in STEPS[(n, k // 4)]:
                                step(kind, m)


_INS = ["x", "norm_w", "w_in", "q_norm_w", "k_norm_w", "lambda_q1", "lambda_k1", "lambda_q2", "lambda_k2", "subln_w",
        "ret_decay_fwd", "ret_decay_bwd", "w_out", "norm_g_2", "w_in_2", "conv_w_2", "q_norm_g_2", "k_norm_g_2",
        "sinks_2", "w_conv_out_2", "w_attn_out_2", "gate_b_2", "w_out_2"]


def kernel(**inputs):
    import numpy as _np
    import concourse.bacc as _bacc
    from concourse import mybir as _mybir
    from concourse.bass_utils import run_bass_kernel_spmd as _run

    nc = _bacc.Bacc("TRN2", target_bir_lowering=False, num_devices=1)
    arrays, args = {}, {}
    for name in _INS:
        v = _np.ascontiguousarray(inputs[name])
        arrays[f"in_{name}_dram"] = v
        args[name] = nc.dram_tensor(f"in_{name}_dram", v.shape, _mybir.dt.from_np(v.dtype), kind="ExternalInput").ap()
    args["out"] = nc.dram_tensor("out_0_dram", (1, S, D), _mybir.dt.float32, kind="ExternalOutput").ap()
    build(nc, args)
    r = _run(nc, [arrays], core_ids=[0])
    return r.results[0]["out_0_dram"]
```

```python
from contextlib import ExitStack

import concourse.bass as bass
from concourse import mybir

F32 = mybir.dt.float32
F32R = mybir.dt.float32r
I32 = mybir.dt.int32
ALU = mybir.AluOpType
ACT = mybir.ActivationFunctionType
AXX = mybir.AxisListType.X

P = 128
S = 512
ST = S // P
D = 1024
KC = D // P
EPS = 1e-6
LAMBDA_INIT = 0.8 - 0.6
HD = 64
QK_SCALE = HD ** -0.5
DA_HEADS = 4
RET_HEADS = 4
KV_HEADS = 4
GROUP = 4
TAB = (2 * ST - 1) * P
CENTRE = (ST - 1) * P
BIG = 1e30
R_GATE = 3 * KC
R_KW = R_GATE + 2 * KC
ROWS = R_KW + 5
SLOTS = 4
RSQRT_SEED = 0x5F3759DF

NAT, TRA = "natural", "transposed"
(U_K, U_Q, U_V, U_RQK, U_RV, U_GA, U_GR, U_O0, U_O1, U_KV, U_Q20, U_Q21, U_Z0, U_Z1) = range(14)
U_CONV = 14
U_GATE_A = U_CONV + KC
U_GATE_B = U_GATE_A + KC // 2
U_OUT = U_GATE_B + KC // 2
UNITS = U_OUT + 2
PIECES = 4 * UNITS
CV, CB, CC, CZ, Q2, K2, Z2, G2 = 0, 1024, 2048, 3072, 4096, 5120, 5632, 6656


def unit_columns(u):
    if u < U_CONV:
        return [
            (NAT, [("w_in", 512)]), (NAT, [("w_in", 0)]), (NAT, [("w_in", 1024)]),
            (TRA, [("w_in", 2048 + P * j) for j in range(4)]), (NAT, [("w_in", 2560)]),
            (TRA, [("w_in", 1536 + P * j) for j in range(4)]), (TRA, [("w_in", 3072 + P * j) for j in range(4)]),
            (NAT, [("w_out", 0)]), (NAT, [("w_out", 512)]),
            (NAT, [("w_in_2", K2)]), (NAT, [("w_in_2", Q2)]), (NAT, [("w_in_2", Q2 + 512)]),
            (TRA, [("w_in_2", Z2 + P * j) for j in range(4)]),
            (TRA, [("w_in_2", Z2 + 512 + P * j) for j in range(4)])][u]
    if u < U_GATE_A:
        t = u - U_CONV
        return TRA, [("w_in_2", c + P * t) for c in (CV, CC, CB, CZ)]
    if u < U_OUT:
        t = 2 * ((u - U_GATE_A) % (KC // 2))
        gate, other = (G2, "w_conv_out_2") if u < U_GATE_B else (G2 + D, "w_attn_out_2")
        return TRA, [("w_in_2", gate + P * t), (other, P * t), ("w_in_2", gate + P * t + P), (other, P * t + P)]
    return NAT, [("w_out_2", 512 * (u - U_OUT))]


UNIT = [unit_columns(u) for u in range(UNITS)]
NATURAL_BEFORE = [sum(UNIT[v][0] == NAT for v in range(u)) for u in range(UNITS)]


DA_STEPS = DA_HEADS * ST
WIN_STEPS = ST * KV_HEADS
DA_FIRST = 4 * U_RQK
WIN_FIRST = 4 * U_Z0 + 5


TURNS = [("KT", U_Q, 0), ("QT", U_V, 0), ("KT2", U_Q20, 0), ("QT2", U_Q21, 0), ("QT2", U_Z0, 4)]


def steps_after(n, half):
    out = []
    i = 2 * n + half
    if 0 <= i < 4:
        out.append(("XT", 4 + i))
    i = 2 * (n - 4 * U_O1 - 1) + half
    if 0 <= i < 4:
        out.append(("XT", KC + i))
    i = 2 * (n - 4 * U_KV) + half - 1
    if 0 <= i < 4:
        out.append(("XT", KC + 4 + i))
    for b, unit in enumerate((U_K, U_KV)):
        i = 2 * (n - 4 * unit) + half
        if i == 4:
            out.append(("RS_X", b))
        if i == 6:
            out.append(("RS_ROW", b))
        if b and 9 <= i < 9 + KC:
            out.append(("XS", i - 9))
    if (n, half) == (2, 1):
        out.append(("ROWS", 0))
    i = 2 * (n - 4 * U_GA) + half
    if 2 <= i < 2 + 2 * KC and i % 2 == 0:
        out.append(("GATE", i // 2 - 1))
    for kind, unit, first in TURNS:
        j = 2 * (n - 4 * unit) + half - 3
        if 0 <= j < 4:
            out.append((kind, first + j))
    g = 2 * (n - DA_FIRST) + half
    if 3 <= g < DA_STEPS + 3:
        out.append(("AV", g - 3))
    if 2 <= g < DA_STEPS + 2:
        out.append(("TW", g - 2))
    if 0 <= g < DA_STEPS:
        out.append(("S", g))
    if 1 <= g < DA_STEPS + 1:
        out.append(("W", g - 1))
    if 3 <= g < DA_STEPS + 3 and g % ST == (ST - 1 + 3) % ST:
        out.append(("AN", (g - 3) // ST))
    r = g - DA_STEPS - 1
    if 2 <= r < DA_STEPS + 2:
        out.append(("RA", r - 2))
    if 0 <= r < DA_STEPS:
        out.append(("RS", r))
    finals = {20: 0, 21: 1, 23: 2, 25: 3, 27: 4, 29: 5, 33: 6, 36: 7}
    if g in finals:
        out.append(("F", finals[g]))
    k, odd = divmod(2 * (n - WIN_FIRST) + half, 2)
    if odd:
        if 0 <= k < WIN_STEPS:
            out.append(("W2", k))
        if 1 <= k < WIN_STEPS + 1:
            out.append(("TP", k - 1))
    else:
        if 0 <= k < WIN_STEPS:
            out.append(("S2", k))
        if 2 <= k < WIN_STEPS + 2:
            out.append(("AV2", k - 2))
        if 0 <= k - (WIN_STEPS + 3) < KC:
            out.append(("OS", k - (WIN_STEPS + 3)))
    return out


STEPS = {(n, half): steps_after(n, half) for n in range(PIECES) for half in range(2)}
BANK_T_USERS = ("KT", "QT", "TW", "F", "KT2", "QT2", "TP")
T_USE = {}
for _n in range(PIECES):
    for _half in range(2):
        for _step in STEPS[(_n, _half)]:
            if _step[0] in BANK_T_USERS:
                T_USE[_step] = len(T_USE)


def tiles_done(n, half):
    u, q = divmod(n, 4)
    if UNIT[u][0] == TRA:
        return [(u, q)] if half == 1 else []
    return [(u, 2 * half), (u, 2 * half + 1)] if q == 3 else []


def build(nc, a):
    with ExitStack() as ctx:
        def sb(name, shape, dt=F32, stack=ctx):
            return stack.enter_context(nc.sbuf_tensor(name, shape, dt))

        def sem(name):
            return ctx.enter_context(nc.semaphore(name))

        w_hi = sb("w_hi", [P, SLOTS, D], F32R)
        landing = ExitStack()
        w_raw = sb("w_raw", [P, SLOTS, D], stack=landing)
        landing.close()
        w_lo = sb("w_lo", [P, SLOTS, D], F32R)
        xt_hi = sb("xt_hi", [P, KC, S], F32R)
        xt_lo = sb("xt_lo", [P, KC, S], F32R)
        ident = sb("ident", [P, P])
        mask = sb("mask", [P, 2 * P])
        own = sb("own", [P, P])
        rows = sb("rows", [ROWS, P]); cols = sb("cols", [P, ROWS])
        norm_cols = sb("norm_cols", [P, 2 * KC])
        qws = sb("qws", [P, 1]); q2ws = sb("q2ws", [P, 1]); sub_s = sb("sub_s", [P, 1])
        lam_v = sb("lam_v", [P, 4, HD]); lam_s = sb("lam_s", [P, 2]); lam_e = sb("lam_e", [P, 2]); neg_lam = sb("neg_lam", [P, 1])
        lam_j = sb("lam_j", [P, HD])
        dec = sb("dec", [P, 8]); dec_a = sb("dec_a", [P, 8]); dec_e = sb("dec_e", [P, 8])
        dec_z = sb("dec_z", [P, 8]); dec_q = sb("dec_q", [P, 8]); dec_p = sb("dec_p", [P, 8])
        log_g = sb("log_g", [P, 8]); neg_log_b = sb("neg_log_b", [P, 4])
        sink = sb("sink", [P, 16]); neg_sink = sb("neg_sink", [P, 16])
        half_b = sb("half_b", [P, 16])
        rs_x = sb("rs_x", [P, 2, ST])
        ssq = sb("ssq", [P, 4]); ssq_half = sb("ssq_half", [P, 4, 2])
        rs_v = sb("rs_v", [P, 32]); rs_y = sb("rs_y", [P, 32]); rs_t = sb("rs_t", [P, 32])
        mx = sb("mx", [P, 2, 2]); neg_mx = sb("neg_mx", [P, 2, 2]); den = sb("den", [P, 2, 2])
        rec = sb("rec", [P, 8, 2]); lam_rec = sb("lam_rec", [P, 2, 1])
        mx2 = sb("mx2", [P, 4, 4]); neg_m2 = sb("neg_m2", [P, 4, 4]); sink_m = sb("sink_m", [P, 4, 4])
        den2 = sb("den2", [P, 4, 4]); sink_e = sb("sink_e", [P, 4, 4]); rec2 = sb("rec2", [P, 4, 4])

        conv_w = cols[:, 0:R_GATE].rearrange("p (k t) -> p k t", k=3)
        gate_b = cols[:, R_GATE:R_KW]
        kw, qw, k2w, q2w, sub_w = (cols[:, r:r + 1] for r in range(R_KW, ROWS))

        start = ExitStack()
        x_in = sb("x_in", [P, ST, D], stack=start)
        sq_x = sb("sq_x", [P, ST, D], stack=start)
        norm_rows = sb("norm_rows", [2 * KC, P], stack=start)
        start.close()

        one = ExitStack()
        q_stack = sb("q_stack", [P, 2 * DA_HEADS, S], F32R, stack=one)
        dup = ExitStack()
        qk_dup = sb("qk_dup", [P, ST, 16 * HD], stack=dup)
        dup.close()
        va = sb("va", [P, ST, 512], stack=one)
        rqkT = sb("rqkT", [P, 4, S], stack=one)
        prob = sb("prob", [P, 2, 2, S], stack=one)
        wT = sb("wT", [P, 2, S], stack=one)
        sq = sb("sq", [P, S], stack=one)
        th = sb("th", [P, S], stack=one)
        rs_row_1 = sb("rs_row_1", [P, S], stack=one)
        o_raw = sb("o_raw", [P, 4, ST, P], stack=one)
        vr = sb("vr", [P, ST, 512], stack=one)
        gT = sb("gT", [P, KC, S], stack=one)
        mix_hi = sb("mix_hi", [P, KC, S], F32R, stack=one)
        mix_lo = sb("mix_lo", [P, KC, S], F32R, stack=one)
        k_hi2, k_lo2 = mix_hi, mix_lo
        table = sb("table", [P, 2, TAB], stack=one)
        diff = sb("diff", [P, TAB], stack=one)
        one.close()
        stage = prob[:].rearrange("p a b s -> p (a b) s")

        two = ExitStack()
        x1 = sb("x1", [P, ST, D], stack=two)
        gT2 = sb("gT2", [P, KC, S], stack=two)
        yc_hi = sb("yc_hi", [P, KC, S], F32R, stack=two)
        yc_lo = sb("yc_lo", [P, KC, S], F32R, stack=two)
        th2 = sb("th2", [P, S], stack=two)
        acc = sb("acc", [P, S], stack=two)
        later = ExitStack()
        o2_hi = sb("o2_hi", [P, KC, S], F32R, stack=later)
        o2_lo = sb("o2_lo", [P, KC, S], F32R, stack=later)
        part = sb("part", [P, KC, S], stack=later)
        later.close()
        qT2 = sb("qT2", [P, KC, S], stack=two)
        kT2 = sb("kT2", [P, KV_HEADS, S], stack=two)
        v2 = sb("v2", [P, ST, KV_HEADS, 2 * HD], stack=two)
        prob2 = sb("prob2", [P, 2, GROUP, 256], stack=two)
        pT = sb("pT", [P, 2, 2, GROUP, P], stack=two)
        sq2 = sb("sq2", [P, S], stack=two)
        vt = sb("vt", [P, S], stack=two)
        cv = sb("cv", [P, S + 2], stack=two)
        two.close()
        x_rows = (x_in, x1)
        x_raw = ((xt_hi, xt_lo), (yc_hi, yc_lo))
        ones = (table[:, 1, 0:P], th2[:, 0:P])
        diag = (table[:, 1, P:P + S], vt[:])
        rs_row = (rs_row_1[:], acc[:])
        x_tmp = cv[:, 0:S]
        k_dup = qT2[:, 0:4, :]
        stage2 = prob2[:].rearrange("p a b s -> p (a b s)").rearrange("p (t s) -> p t s", t=4)

        proj = ctx.enter_context(nc.psum_tensor("proj", [P, SLOTS, S], F32))
        score = ctx.enter_context(nc.psum_tensor("score", [P, 2, S], F32))
        bank_t = ctx.enter_context(nc.psum_tensor("bank_t", [P, S], F32))
        bank_o = ctx.enter_context(nc.psum_tensor("bank_o", [P, S], F32))

        x_landed = [sem(f"x_landed{s}") for s in range(ST)]
        x_again = sem("x_again")
        norms_landed = sem("norms_landed"); norms_turned = sem("norms_turned"); norms_ready = sem("norms_ready")
        params = sem("params")
        rows_turned = sem("rows_turned")
        raw_landed = [sem(f"raw_landed{i}") for i in range(SLOTS)]
        slot_open = sem("slot_open")
        hi_done = sem("hi_done")
        w_split = sem("w_split")
        piece_done = sem("piece_done")
        natural_done = sem("natural_done")
        evacuated = [sem(f"evacuated{b}") for b in range(SLOTS)]
        xt_done = sem("xt_done")
        xt_hi_done = sem("xt_hi_done")
        xt_split = sem("xt_split")
        setup = sem("setup")
        setup_mask = sem("setup_mask")
        ssq_done = sem("ssq_done")
        rs_done = sem("rs_done")
        diag_done = sem("diag_done"); rs_turned = sem("rs_turned"); rs_row_done = sem("rs_row_done")
        xt_scaled = sem("xt_scaled")
        dec_abs = sem("dec_abs"); dec_exp = sem("dec_exp")
        lam_sum = sem("lam_sum"); lam_exp = sem("lam_exp")
        weights_ready = sem("weights_ready")
        sq_done = sem("sq_done"); sq_used = sem("sq_used")
        heads_done = sem("heads_done")
        qk_hi_done = sem("qk_hi_done")
        t_done = sem("t_done"); t_free = sem("t_free")
        scores_done = sem("scores_done"); score_read = sem("score_read")
        neg_max = sem("neg_max"); exp_done = sem("exp_done"); weight_done = sem("weight_done")
        av_done = sem("av_done"); o_free = sem("o_free"); o_normed = sem("o_normed")
        diff_done = sem("diff_done"); distance_done = sem("distance_done")
        decay_arg = sem("decay_arg"); decay_done = sem("decay_done")
        ret_scores = sem("ret_scores"); ret_weight = sem("ret_weight")
        gates_done = sem("gates_done")
        th_done = sem("th_done"); mixed = sem("mixed")
        scores2 = sem("scores2"); score2_read = sem("score2_read"); neg_max2 = sem("neg_max2")
        exp2_done = sem("exp2_done"); weight2_done = sem("weight2_done"); av2_done = sem("av2_done")
        o2_gated = sem("o2_gated")
        o2_split = sem("o2_split"); yc_done = sem("yc_done"); merged = sem("merged")
        cv_zero = sem("cv_zero")
        act_chain = sem("act_chain"); dve_chain = sem("dve_chain"); pool_chain = sem("pool_chain")
        out_written = sem("out_written")

        def wait_tile(eng, u, j):
            if UNIT[u][0] == NAT and j < 3:
                eng.wait_ge(natural_done, 3 * NATURAL_BEFORE[u] + j + 1)
            else:
                eng.wait_ge(piece_done, 4 * u + j + 1)

        def wait_evacuated(eng, u, j):
            eng.wait_ge(evacuated[j], u + 1)

        def bank(u, j):
            return proj[:, j, :]

        map_banks = [bank_t[:], bank_o[:]]
        xt_banks = [score[:, 0, :], score[:, 1, :], bank_o[:], bank_t[:]]

        N_PARAMS = 18
        block = ctx.enter_context(nc.Block())

        @block.sync
        def _(sp):
            def load_piece(n):
                u, q = divmod(n, 4)
                kind, cols = UNIT[u]
                if kind == NAT:
                    w, c = cols[0]
                    src = a[w][0, 256 * q:256 * q + 256, c:c + 512].rearrange("(k p) c -> p k c", p=P)
                    dst = w_raw[:, n % SLOTS, :].rearrange("p (k c) -> p k c", k=2)
                else:
                    w, c = cols[q]
                    src = a[w][0, :, c:c + P].rearrange("(k p) c -> p k c", p=P)
                    dst = w_raw[:, n % SLOTS, :].rearrange("p (k c) -> p k c", k=KC)
                sp.dma_start(dst, src).then_inc(raw_landed[n % SLOTS], 16)

            for s in range(ST):
                sp.dma_start(x_in[:, s, :], a["x"][0, s * P:(s + 1) * P, :]).then_inc(x_landed[s], 16)
                if s == 1:
                    load_piece(0)

            def load_parameters():
                sp.dma_start(rows[0:R_GATE, :], a["conv_w_2"][0].rearrange("k (t p) -> (k t) p", p=P)).then_inc(params, 16)
                sp.dma_start(rows[R_GATE:R_KW, :], a["gate_b_2"].rearrange("o (t p) -> (o t) p", p=P)).then_inc(params, 16)
                for i, w in enumerate(("k_norm_w", "q_norm_w", "k_norm_g_2", "q_norm_g_2")):
                    for h in range(2):
                        sp.dma_start(rows[R_KW + i:R_KW + i + 1, h * HD:(h + 1) * HD], a[w]).then_inc(params, 16)
                sp.dma_start(rows[ROWS - 1:ROWS, :], a["subln_w"]).then_inc(params, 16)
                for i, w in enumerate(("lambda_q1", "lambda_q2", "lambda_k1", "lambda_k2")):
                    sp.dma_start(lam_v[:, i, :], a[w][0, :].partition_broadcast(P)).then_inc(params, 16)
                for i, w in enumerate(("ret_decay_fwd", "ret_decay_bwd")):
                    sp.dma_start(dec[:, 4 * i:4 * i + 4], a[w][0, :].partition_broadcast(P)).then_inc(params, 16)
                sp.dma_start(sink[:], a["sinks_2"][0, :].partition_broadcast(P)).then_inc(params, 16)

            for n in range(1, PIECES):
                if n == SLOTS:
                    load_parameters()
                if n >= SLOTS:
                    sp.wait_ge(piece_done, n - SLOTS + 1)
                load_piece(n)
            for h in range(2):
                for s in range(ST):
                    wait_evacuated(sp, U_OUT + h, s)
                    sp.dma_start(a["out"][0, s * P:(s + 1) * P, h * 512:(h + 1) * 512],
                                 x1[:, s, h * 512:(h + 1) * 512]).then_inc(out_written, 16)
            sp.wait_ge(out_written, 16 * 2 * ST)

        @block.gpsimd
        def _(pool):
            pool.memset(ident[:], 0.0).then_inc(pool_chain, 1)
            pool.wait_ge(pool_chain, 1)
            pool.affine_select(out=ident[:], in_=ident[:], compare_op=ALU.not_equal, fill=1.0, base=0,
                               pattern=[[-1, P]], channel_multiplier=1).then_inc(setup, 1)

            pool.iota(table[:, 0, :].bitcast(I32), pattern=[[1, TAB]], base=-CENTRE, channel_multiplier=-1).then_inc(setup, 1)
            pool.memset(mask[:], 0.0).then_inc(pool_chain, 1)
            pool.wait_ge(pool_chain, 2)
            pool.affine_select(out=mask[:], in_=mask[:], compare_op=ALU.is_ge, fill=BIG, base=P,
                               pattern=[[-1, 2 * P]], channel_multiplier=1).then_inc(pool_chain, 1)
            pool.wait_ge(pool_chain, 3)
            pool.affine_select(out=mask[:], in_=mask[:], compare_op=ALU.is_ge, fill=BIG, base=-1,
                               pattern=[[1, 2 * P]], channel_multiplier=-1).then_inc(pool_chain, 1)
            pool.memset(own[:], 1.0).then_inc(pool_chain, 1)
            pool.wait_ge(pool_chain, 5)
            pool.affine_select(out=own[:], in_=own[:], compare_op=ALU.is_ge, fill=0.0, base=0,
                               pattern=[[1, P]], channel_multiplier=-1).then_inc(setup_mask, 1)

            def split(n, slot):
                pool.tensor_scalar(w_hi[:, slot, :], w_raw[:, slot, :], 1.0, 1.0, ALU.mult, ALU.mult).then_inc(hi_done, 1)
                pool.wait_ge(hi_done, n + 1)
                pool.tensor_tensor(w_lo[:, slot, :], w_raw[:, slot, :], w_hi[:, slot, :].bitcast(F32),
                                   ALU.subtract).then_inc(w_split, 1)

            for n in range(SLOTS):
                pool.wait_ge(raw_landed[n], 16)
                split(n, n)
            with pool.Fori(1, PIECES // SLOTS) as g:
                for slot in range(SLOTS):
                    pool.wait_ge(raw_landed[slot], 16 * g + 16)
                    pool.wait_ge(piece_done, SLOTS * g + slot - SLOTS + 1)
                    pool.sem_inc(slot_open, 1)
                    split(SLOTS * g + slot, slot)

        @block.scalar
        def _(act):
            for b, w in enumerate(("norm_w", "norm_g_2")):
                act.dma_start(norm_rows[KC * b:KC * b + KC, :], a[w][0].rearrange("(t p) -> t p", p=P)).then_inc(norms_landed, 16)

            chain = [0]

            def done(ins):
                chain[0] += 1
                ins.then_inc(act_chain, 1)
                act.wait_ge(act_chain, chain[0])

            def take_xt(m):
                b, c = divmod(m, KC)
                act.wait_ge(xt_done, m + 1)
                if m == KC + 4:
                    act.wait_ge(ssq_done, 3 * ST)
                act.activation(x_raw[b][0][:, c, :], xt_banks[c % 4], ACT.Copy, scale=norm_cols[:, m:m + 1]).then_inc(xt_hi_done, 1)

            def row_squares(s):
                act.wait_ge(x_landed[s], 16)
                act.activation(sq_x[:, s, :], x_in[:, s, :], ACT.Square, accum_out=ssq[:, s:s + 1]).then_inc(ssq_done, 1)

            row_squares(0)
            row_squares(1)
            act.wait_ge(norms_ready, 1)
            for c in range(4):
                take_xt(c)
            row_squares(2)
            row_squares(3)
            squares = [0]

            def square(dst, src):
                if squares[0]:
                    act.wait_ge(sq_used, squares[0])
                act.activation(dst, src, ACT.Square).then_inc(sq_done, 1)
                squares[0] += 1

            def distance_table(h):
                act.activation(table[:, h % 2, :], diff[:], ACT.Abs, scale=2.0 ** (-8.0 * (h + 1) / DA_HEADS)).then_inc(distance_done, 1)

            last_tanh = ()

            for n in range(PIECES):
                for half in range(2):
                    for u, j in tiles_done(n, half):
                        if u >= U_CONV and u < U_GATE_A and j in (1, 2):
                            continue
                        if u >= U_GATE_A and (u >= U_OUT or j % 2):
                            continue
                        if u == U_RQK:
                            continue
                        wait_tile(act, u, j)
                        b = bank(u, j)
                        if u in (U_K, U_Q):
                            if u == U_Q:
                                act.wait_ge(heads_done, ST)
                            act.wait_ge(rs_done, 1)
                            act.activation(stage[:, j, :], b, ACT.Copy, scale=rs_x[:, 0, j:j + 1]).then_inc(evacuated[j], 1)
                            wait_evacuated(act, u, j)
                            square(sq[:], stage[:, j, :])
                        elif u == U_V:
                            act.wait_ge(t_done, T_USE[("QT", 3)] + 1)
                            act.activation(va[:, j, :], b, ACT.Copy, scale=rs_x[:, 0, j:j + 1]).then_inc(evacuated[j], 1)
                        elif u == U_RV:
                            act.activation(vr[:, j, :], b, ACT.Copy, scale=rs_x[:, 0, j:j + 1]).then_inc(evacuated[j], 1)
                        elif u in (U_GA, U_GR):
                            g = 4 * (u - U_GA) + j
                            wait_evacuated(act, u, j)
                            if g:
                                act.wait_ge(gates_done, g)
                            act.activation(th[:], gT[:, g, :], ACT.Tanh, scale=0.5).then_inc(th_done, 1)
                        elif u in (U_O0, U_O1):
                            h = u - U_O0
                            wait_evacuated(act, u, j)
                            act.wait_ge(sq_used, squares[0])
                            act.wait_ge(ssq_done, ST + ST * h + j)
                            act.activation(sq[:], x1[:, j, h * 512:(h + 1) * 512], ACT.Square,
                                           accum_out=ssq_half[:, j, h:h + 1]).then_inc(ssq_done, 1)
                        elif u == U_KV:
                            act.wait_ge(rs_done, 2)
                            done(act.activation(v2[:, j, :, :].rearrange("p h (c d) -> p h c d", c=2),
                                                b[:, 256:512].rearrange("p (h d) -> p h d", h=KV_HEADS).unsqueeze(2).broadcast_to([P, KV_HEADS, 2, HD]),
                                                ACT.Copy, scale=rs_x[:, 1, j:j + 1]))
                            act.activation(stage2[:, j, 0:256], b[:, 0:256], ACT.Copy, scale=rs_x[:, 1, j:j + 1]).then_inc(evacuated[j], 1)
                            wait_evacuated(act, u, j)
                            square(sq2[:, 0:256], stage2[:, j, 0:256])
                        elif u in (U_Q20, U_Q21):
                            if u == U_Q20:
                                act.wait_ge(heads_done, 8 + ST)
                            else:
                                act.wait_ge(t_done, T_USE[("QT2", 3)] + 1)
                            act.activation(stage2[:, j, :], b, ACT.Copy, scale=rs_x[:, 1, j:j + 1]).then_inc(evacuated[j], 1)
                            wait_evacuated(act, u, j)
                            square(sq2[:], stage2[:, j, :])
                        elif U_CONV <= u < U_GATE_A and j == 0:
                            if u > U_CONV:
                                wait_evacuated(act, u - 1, 1)
                            act.activation(vt[:], b, ACT.Copy).then_inc(evacuated[0], 1)
                        else:
                            if U_CONV < u <= U_GATE_A and last_tanh[0] < U_GATE_A:
                                act.wait_ge(yc_done, u - U_CONV)
                            elif last_tanh:
                                wait_evacuated(act, last_tanh[0], last_tanh[1] + (u >= U_GATE_A))
                            last_tanh = (u, j)
                            if u < U_GATE_A:
                                act.activation(th2[:], b, ACT.Tanh, scale=0.5).then_inc(th_done, 1)
                            else:
                                t = 2 * ((u - U_GATE_A) % (KC // 2)) + j // 2 + (KC if u >= U_GATE_B else 0)
                                act.activation(th2[:], b, ACT.Tanh, bias=half_b[:, t:t + 1], scale=0.5).then_inc(evacuated[j], 1)

                    for kind, m in STEPS[(n, half)]:
                        if kind == "XT":
                            take_xt(m)
                        elif kind == "RS_ROW":
                            act.wait_ge(rs_turned, m + 1)
                            act.activation(rs_row[m], bank_o[:], ACT.Copy).then_inc(rs_row_done, 1)
                        elif kind == "ROWS":
                            act.wait_ge(dec_abs, 1)
                            act.activation(dec_e[:], dec_a[:], ACT.Exp, scale=-1.0).then_inc(dec_exp, 1)
                            act.wait_ge(lam_sum, 1)
                            act.activation(lam_e[:], lam_s[:], ACT.Exp).then_inc(lam_exp, 1)
                        elif kind in ("KT", "QT"):
                            if (kind, m) == ("KT", 0):
                                act.wait_ge(weights_ready, 1)
                            act.wait_ge(t_done, T_USE[(kind, m)] + 1)
                            for mp in range(2):
                                act.activation((k_hi2 if kind == "KT" else q_stack)[:, 2 * m + mp, :], map_banks[mp], ACT.Copy,
                                               scale=(kw if kind == "KT" else qws[:])).then_inc(qk_hi_done, 1)
                        elif kind == "TW":
                            act.wait_ge(t_done, T_USE[(kind, m)] + 1)
                            if m >= 2:
                                act.wait_ge(av_done, m - 1)
                            act.activation(wT[:, m % 2, :], bank_t[:], ACT.Copy).then_inc(t_free, 1)
                        elif kind == "S":
                            act.wait_ge(neg_max, m + 1)
                            for mp in range(2):
                                act.activation(prob[:, m % 2, mp, :], prob[:, m % 2, mp, :], ACT.Exp,
                                               bias=neg_mx[:, m % 2, mp:mp + 1],
                                               accum_out=den[:, m % 2, mp:mp + 1]).then_inc(exp_done, 1)
                            if m % ST == 0 and ST <= m < DA_STEPS - ST:
                                distance_table(m // ST + 1)
                        elif kind in ("AV", "RA") and m % ST == ST - 1:
                            h = m // ST + (DA_HEADS if kind == "RA" else 0)
                            act.wait_ge(av_done, ST * h + ST)
                            if h >= 4:
                                act.wait_ge(t_done, T_USE[("F", h - 4)] + 1)
                            o = o_raw[:, h % 4, :, :].rearrange("p i v -> p (i v)")
                            if kind == "AV":
                                for i in range(ST):
                                    last = act.activation(o_raw[:, h, i, :], bank_o[:, i * P:(i + 1) * P], ACT.Copy,
                                                          scale=rec[:, (m - m % ST + i) % 8, 0:1])
                                last.then_inc(o_free, 1)
                            else:
                                act.activation(o, bank_o[:], ACT.Copy).then_inc(o_free, 1)
                            act.wait_ge(o_free, h + 1)
                            square(sq[:], o)
                        elif kind in ("KT2", "QT2"):
                            act.wait_ge(t_done, T_USE[(kind, m)] + 1)
                            act.activation((kT2 if kind == "KT2" else qT2)[:, m, :], bank_t[:], ACT.Copy,
                                           scale=(k2w if kind == "KT2" else q2ws[:])).then_inc(t_free, 1)
                        elif kind == "S2":
                            act.wait_ge(neg_max2, m + 1)
                            for r in range(GROUP):
                                act.activation(prob2[:, m % 2, r, 0:P], prob2[:, m % 2, r, 0:P], ACT.Exp,
                                               bias=neg_m2[:, m % 4, r:r + 1], accum_out=den2[:, m % 4, r:r + 1])
                            act.activation(sink_e[:, m % 4, :], sink_m[:, m % 4, :], ACT.Exp).then_inc(exp2_done, 1)
                    if (n, half) == (4 * U_V, 0):
                        act.wait_ge(diff_done, 1)
                        act.wait_ge(rs_turned, 1)
                        distance_table(0)
                        distance_table(1)
                    g = 2 * (n - DA_FIRST) + half
                    if DA_STEPS - 1 <= g < DA_STEPS - 1 + 4 * RET_HEADS and (g - DA_STEPS + 1) % 4 == 0:
                        h = (g - DA_STEPS + 1) // 4
                        act.wait_ge(decay_arg, h + 1)
                        act.activation(table[:, h % 2, :], table[:, h % 2, :], ACT.Exp).then_inc(decay_done, 1)
                    if (n, half) == (4 * U_GR + 3, 1):
                        act.wait_ge(scores_done, DA_STEPS)
                        act.dma_start(x1[:], a["x"][0].rearrange("(t p) d -> p t d", p=P)).then_inc(x_again, 16)

        @block.vector
        def _(dve):
            chain = [0]

            def done(ins):
                chain[0] += 1
                ins.then_inc(dve_chain, 1)
                dve.wait_ge(dve_chain, chain[0])

            def rsqrt(n, width):
                v, y, t = rs_v[:, 0:n], rs_y[:, 0:n], rs_t[:, 0:n]
                done(dve.tensor_scalar(v, v, 1.0 / width, EPS, ALU.mult, ALU.add))
                done(dve.tensor_scalar(t.bitcast(I32), v.bitcast(I32), 1, None, ALU.logical_shift_right))
                done(dve.tensor_scalar(y.bitcast(I32), t.bitcast(I32), -1.0, float(RSQRT_SEED), ALU.mult, ALU.add))
                for _ in range(3):
                    done(dve.scalar_tensor_tensor(out=t, in0=y, scalar=-0.5, in1=y, op0=ALU.mult, op1=ALU.mult))
                    done(dve.tensor_tensor(t, t, v, ALU.mult))
                    done(dve.scalar_tensor_tensor(out=y, in0=t, scalar=1.5, in1=y, op0=ALU.add, op1=ALU.mult))

            def take_xt_low(m):
                b, c = divmod(m, KC)
                dve.wait_ge(xt_hi_done, m + 1)
                dve.scalar_tensor_tensor(out=x_raw[b][1][:, c, :], in0=xt_banks[c % 4], scalar=norm_cols[:, m:m + 1],
                                         in1=x_raw[b][0][:, c, :].bitcast(F32), op0=ALU.mult, op1=ALU.subtract).then_inc(xt_split, 1)

            dve.wait_ge(norms_turned, 1)
            dve.tensor_copy(norm_cols[:], bank_t[:, 0:2 * KC]).then_inc(norms_ready, 1)
            dve.wait_ge(norms_ready, 1)
            for c in range(4):
                take_xt_low(c)

            def prepare_parameters():
                dve.wait_ge(params, 16 * N_PARAMS)
                done(dve.tensor_scalar(dec_a[:], dec[:], -1.0, None, ALU.mult))
                dve.tensor_tensor(dec_a[:], dec_a[:], dec[:], ALU.max).then_inc(dec_abs, 1)
                dve.wait_ge(rows_turned, 1)
                done(dve.tensor_copy(cols[:], bank_t[:, 0:ROWS]))
                done(dve.tensor_tensor_reduce(lam_j[:], lam_v[:, 0, :], lam_v[:, 2, :], 1.0, 0.0, ALU.mult, ALU.add, lam_s[:, 0:1]))
                dve.tensor_tensor_reduce(lam_j[:], lam_v[:, 1, :], lam_v[:, 3, :], 1.0, 0.0, ALU.mult, ALU.add,
                                         lam_s[:, 1:2]).then_inc(lam_sum, 1)
                dve.tensor_scalar(q2ws[:], q2w, QK_SCALE, None, ALU.mult)
                dve.tensor_scalar(sub_s[:], sub_w, 1.0 - LAMBDA_INIT, 0.5, ALU.mult, ALU.mult)
                dve.tensor_scalar(neg_sink[:], sink[:], -1.0, None, ALU.mult)
                dve.tensor_scalar(half_b[:], gate_b, 0.5, None, ALU.mult)
                dve.tensor_scalar(qws[:], qw, QK_SCALE, None, ALU.mult).then_inc(weights_ready, 1)
                dve.wait_ge(dec_exp, 1)
                done(dve.tensor_scalar(dec_z[:], dec_e[:], 2.0, None, ALU.add))
                done(dve.reciprocal(dec_z[:], dec_z[:]))
                done(dve.tensor_tensor(dec_z[:], dec_z[:], dec_e[:], ALU.mult))
                done(dve.tensor_tensor(dec_q[:], dec_z[:], dec_z[:], ALU.mult))
                done(dve.tensor_scalar(dec_p[:], dec_q[:], 1.0 / 17, None, ALU.mult))
                for k in range(15, 2, -2):
                    done(dve.scalar_tensor_tensor(out=dec_p[:], in0=dec_p[:], scalar=1.0 / k, in1=dec_q[:], op0=ALU.add, op1=ALU.mult))
                done(dve.scalar_tensor_tensor(out=dec_p[:], in0=dec_p[:], scalar=1.0, in1=dec_z[:], op0=ALU.add, op1=ALU.mult))
                done(dve.tensor_scalar(dec_p[:], dec_p[:], 2.0, None, ALU.mult))
                done(dve.scalar_tensor_tensor(out=log_g[:], in0=dec[:], scalar=0.0, in1=dec_p[:], op0=ALU.min, op1=ALU.subtract))
                done(dve.tensor_scalar(neg_log_b[:], log_g[:, 4:8], -1.0, None, ALU.mult))
                dve.wait_ge(lam_exp, 1)
                done(dve.scalar_tensor_tensor(out=neg_lam[:], in0=lam_e[:, 1:2], scalar=LAMBDA_INIT, in1=lam_e[:, 0:1],
                                              op0=ALU.subtract, op1=ALU.subtract))
                dve.wait_ge(setup, 2)
                dve.tensor_copy(diff[:], table[:, 0, :].bitcast(I32)).then_inc(diff_done, 1)

            def decay_exponent(h):
                done(dve.tensor_scalar(table[:, h % 2, :], diff[:], neg_log_b[:, h:h + 1], None, ALU.mult))
                dve.scalar_tensor_tensor(out=table[:, h % 2, :], in0=diff[:], scalar=log_g[:, h:h + 1], in1=table[:, h % 2, :],
                                         op0=ALU.mult, op1=ALU.min).then_inc(decay_arg, 1)

            sums = [0]

            def head_sums(dst, buf, heads):
                sums[0] += 1
                dve.wait_ge(sq_done, sums[0])
                dve.tensor_reduce(dst, buf.rearrange("p (h d) -> p h d", h=heads), AXX, ALU.add).then_inc(sq_used, 1)

            tanhs = [KC]

            def take_tiles(n, half):
                for u, j in tiles_done(n, half):
                    b = bank(u, j)
                    if u in (U_K, U_Q, U_KV, U_Q20, U_Q21):
                        heads = 4 if u == U_KV else 8
                        st, buf = (stage, sq) if u < U_KV else (stage2, sq2)
                        head_sums(rs_v[:, heads * j:heads * j + heads], buf[:, 0:heads * HD], heads)
                        if j == 3:
                            dve.wait_ge(sq_used, sums[0])
                            rsqrt(4 * heads, HD)
                            for s in range(ST):
                                y = rs_y[:, heads * s:heads * s + heads]
                                src = st[:, s, 0:heads * HD].rearrange("p (h d) -> p h d", h=heads)
                                if u in (U_K, U_Q, U_KV):
                                    if u == U_Q and s == 0:
                                        dve.wait_ge(t_done, T_USE[("KT", 3)] + 1)
                                    dst = (k_dup if u == U_KV else qk_dup)[:, s, :]
                                    dve.tensor_tensor(
                                        dst.rearrange("p (h c d) -> p h c d", h=heads, c=2),
                                        src.unsqueeze(2).broadcast_to([P, heads, 2, HD]),
                                        y.unsqueeze(2).unsqueeze(3).broadcast_to([P, heads, 2, HD]), ALU.mult).then_inc(heads_done, 1)
                                else:
                                    dve.tensor_tensor(src, src, y.unsqueeze(2).broadcast_to([P, heads, HD]),
                                                      ALU.mult).then_inc(heads_done, 1)
                    elif u in (U_RQK, U_GA, U_GR):
                        wait_tile(dve, u, j)
                        dst = rqkT[:, j, :] if u == U_RQK else gT[:, 4 * (u - U_GA) + j, :]
                        dve.scalar_tensor_tensor(out=dst, in0=b, scalar=QK_SCALE if u == U_RQK and j >= 2 else 1.0, in1=rs_row[0],
                                                 op0=ALU.mult, op1=ALU.mult).then_inc(evacuated[j], 1)
                    elif u in (U_Z0, U_Z1):
                        tanhs[0] += 1
                        dve.wait_ge(th_done, tanhs[0])
                        dve.scalar_tensor_tensor(out=gT2[:, 4 * (u - U_Z0) + j, :], in0=th2[:], scalar=1.0, in1=b,
                                                 op0=ALU.add, op1=ALU.mult).then_inc(evacuated[j], 1)
                    elif u in (U_O0, U_O1, U_OUT, U_OUT + 1):
                        if (u, j) == (U_O0, 0):
                            dve.wait_ge(x_again, 16)
                        wait_tile(dve, u, j)
                        h = (u - U_O0) if u <= U_O1 else u - U_OUT
                        xh = x1[:, j, h * 512:(h + 1) * 512]
                        dve.tensor_tensor(xh, b, xh, ALU.add).then_inc(evacuated[j], 1)
                    elif U_CONV <= u < U_GATE_A:
                        t = u - U_CONV
                        if j == 0 and t == 0:
                            dve.memset(cv[:, 0:2], 0.0).then_inc(cv_zero, 1)
                            dve.wait_ge(cv_zero, 1)
                        if j == 1:
                            wait_evacuated(dve, u, 0)
                            wait_tile(dve, u, 1)
                            dve.tensor_tensor(cv[:, 2:S + 2], b, vt[:], ALU.mult).then_inc(evacuated[1], 1)
                            wait_evacuated(dve, u, 1)
                            done(dve.tensor_scalar(acc[:], cv[:, 0:S], conv_w[:, 0, t:t + 1], None, ALU.mult))
                            for k in (1, 2):
                                done(dve.scalar_tensor_tensor(out=acc[:], in0=cv[:, k:S + k], scalar=conv_w[:, k, t:t + 1],
                                                              in1=acc[:], op0=ALU.mult, op1=ALU.add))
                        if j == 2:
                            wait_tile(dve, u, 2)
                            dve.tensor_tensor(acc[:], b, acc[:], ALU.mult).then_inc(evacuated[2], 1)
                            wait_evacuated(dve, u, 2)
                        if j == 3:
                            tanhs[0] += 1
                            dve.wait_ge(th_done, tanhs[0])
                            dve.scalar_tensor_tensor(out=th2[:], in0=th2[:], scalar=1.0, in1=b,
                                                     op0=ALU.add, op1=ALU.mult).then_inc(evacuated[3], 1)
                            wait_evacuated(dve, u, 3)
                            done(dve.scalar_tensor_tensor(out=acc[:], in0=acc[:], scalar=0.5, in1=th2[:], op0=ALU.mult, op1=ALU.mult))
                            done(dve.tensor_copy(yc_hi[:, t, :], acc[:]))
                            dve.tensor_tensor(yc_lo[:, t, :], acc[:], yc_hi[:, t, :].bitcast(F32), ALU.subtract).then_inc(yc_done, 1)
                    elif U_GATE_A <= u < U_OUT and j % 2:
                        t = 2 * ((u - U_GATE_A) % (KC // 2)) + j // 2
                        wait_evacuated(dve, u, j - 1)
                        wait_tile(dve, u, j)
                        if u >= U_GATE_B and t:
                            dve.wait_ge(merged, t)
                        dst = part[:, t, :] if u < U_GATE_B else acc[:]
                        dve.scalar_tensor_tensor(out=dst, in0=th2[:], scalar=1.0, in1=b,
                                                 op0=ALU.add, op1=ALU.mult).then_inc(evacuated[j], 1)
                        if u >= U_GATE_B:
                            wait_evacuated(dve, u, j)
                            done(dve.tensor_tensor(acc[:], acc[:], part[:, t, :], ALU.add))
                            done(dve.tensor_scalar(yc_hi[:, t, :], acc[:], 0.5, None, ALU.mult))
                            dve.scalar_tensor_tensor(out=yc_lo[:, t, :], in0=acc[:], scalar=0.5, in1=yc_hi[:, t, :].bitcast(F32),
                                                     op0=ALU.mult, op1=ALU.subtract).then_inc(merged, 1)

            def take_steps(n, half):
                for kind, m in STEPS[(n, half)]:
                    if kind == "XT":
                        take_xt_low(m)
                    elif kind == "RS_X":
                        dve.wait_ge(ssq_done, ST + 2 * ST * m)
                        if m == 0:
                            done(dve.tensor_copy(rs_v[:, 0:ST], ssq[:]))
                        else:
                            done(dve.tensor_tensor(rs_v[:, 0:ST], ssq_half[:, :, 0], ssq_half[:, :, 1], ALU.add))
                        rsqrt(ST, D)
                        dve.tensor_copy(rs_x[:, m, :], rs_y[:, 0:ST]).then_inc(rs_done, 1)
                        dve.memset(ones[m], 1.0)
                        dve.tensor_tensor(diag[m].rearrange("p (s r) -> p s r", s=ST), ident[:].unsqueeze(1).broadcast_to([P, ST, P]),
                                          rs_y[:, 0:ST].unsqueeze(2).broadcast_to([P, ST, P]), ALU.mult).then_inc(diag_done, 1)
                        dve.wait_ge(diag_done, m + 1)
                    elif kind == "ROWS":
                        prepare_parameters()
                    elif kind in ("KT", "QT"):
                        for mp in range(2):
                            dve.wait_ge(qk_hi_done, 2 * T_USE[(kind, m)] + mp + 1)
                            rows_, dst, high, scale = ((slice(0, P), k_lo2, k_hi2, kw) if kind == "KT" else (slice(HD, P), q_stack, q_stack, qws))
                            low = dve.scalar_tensor_tensor(out=dst[rows_, 2 * m + mp, :], in0=map_banks[mp][rows_, :], scalar=scale[rows_, :],
                                                           in1=high[rows_, 2 * m + mp, :].bitcast(F32), op0=ALU.mult, op1=ALU.subtract)
                        low.then_inc(t_free, 1)
                    elif kind == "XS":
                        dve.wait_ge(rs_row_done, 2)
                        if m:
                            dve.wait_ge(xt_scaled, m)
                        done(dve.tensor_tensor(x_tmp, x_raw[1][0][:, m, :].bitcast(F32), x_raw[1][1][:, m, :].bitcast(F32), ALU.add))
                        done(dve.tensor_tensor(x_tmp, x_tmp, rs_row[1], ALU.mult))
                        done(dve.tensor_copy(xt_hi[:, m, :], x_tmp))
                        dve.tensor_tensor(xt_lo[:, m, :], x_tmp, xt_hi[:, m, :].bitcast(F32), ALU.subtract).then_inc(xt_scaled, 1)
                    elif kind == "GATE":
                        dve.wait_ge(th_done, m + 1)
                        dve.scalar_tensor_tensor(out=gT[:, m, :], in0=th[:], scalar=1.0, in1=gT[:, m, :],
                                                 op0=ALU.add, op1=ALU.mult).then_inc(gates_done, 1)
                    elif kind == "S":
                        h, i = divmod(m, ST)
                        sl = m % 2
                        if i == 0:
                            dve.wait_ge(distance_done, h + 1)
                        dve.wait_ge(scores_done, m + 1)
                        if m >= 2:
                            dve.wait_ge(t_done, T_USE[("TW", m - 2)] + 1)
                        for mp in range(2):
                            dve.tensor_tensor_reduce(prob[:, sl, mp, :], score[:, mp, :], table[:, h % 2, CENTRE - i * P:CENTRE - i * P + S],
                                                     1.0, -3e38, ALU.subtract, ALU.max, mx[:, sl, mp:mp + 1]).then_inc(score_read, 1)
                        dve.wait_ge(score_read, 2 * m + 2)
                        dve.tensor_scalar(neg_mx[:, sl, :], mx[:, sl, :], -1.0, None, ALU.mult).then_inc(neg_max, 1)
                    elif kind == "W":
                        sl = m % 2
                        if m >= 8 and m % ST == 0:
                            dve.wait_ge(o_free, m // ST - 1)
                        dve.wait_ge(exp_done, 2 * m + 2)
                        done(dve.reciprocal(rec[:, m % 8, :], den[:, sl, :]))
                        done(dve.scalar_tensor_tensor(out=lam_rec[:, sl, :], in0=rec[:, m % 8, 1:2], scalar=den[:, sl, 0:1], in1=neg_lam[:],
                                                      op0=ALU.mult, op1=ALU.mult))
                        dve.scalar_tensor_tensor(out=prob[:, sl, 0, :], in0=prob[:, sl, 1, :], scalar=lam_rec[:, sl, 0:1],
                                                 in1=prob[:, sl, 0, :], op0=ALU.mult, op1=ALU.add).then_inc(weight_done, 1)
                        if m in (DA_STEPS - 3, DA_STEPS - 2):
                            decay_exponent(m - DA_STEPS + 3)
                    elif kind == "RS":
                        h, i = divmod(m, ST)
                        if i == 0:
                            dve.wait_ge(decay_done, h + 1)
                        dve.wait_ge(ret_scores, m + 1)
                        if m < 2:
                            dve.wait_ge(t_done, T_USE[("TW", DA_STEPS - 2 + m)] + 1)
                        else:
                            dve.wait_ge(av_done, DA_STEPS + m - 1)
                        dve.tensor_tensor(prob[:, m % 2, 0, :], score[:, m % 2, :], table[:, h % 2, i * P:i * P + S],
                                          ALU.mult).then_inc(ret_weight, 1)
                        if i == ST - 1 and h + 2 < RET_HEADS:
                            dve.wait_ge(ret_weight, m + 1)
                            decay_exponent(h + 2)
                    elif kind == "AN":
                        h = m
                        head_sums(rs_v[:, ST * h:ST * h + ST], sq[:], ST)
                        if h == DA_HEADS - 1:
                            dve.wait_ge(sq_used, sums[0])
                            rsqrt(DA_STEPS, P)
                            for h in range(DA_HEADS):
                                o = o_raw[:, h, :, :]
                                dve.tensor_tensor(o, o, rs_y[:, ST * h:ST * h + ST].unsqueeze(2).broadcast_to([P, ST, P]), ALU.mult).then_inc(o_normed, 1)
                    elif kind == "RA" and m % ST == ST - 1:
                        h = m // ST
                        head_sums(rs_v[:, 0:ST], sq[:], ST)
                        dve.wait_ge(sq_used, sums[0])
                        rsqrt(ST, P)
                        o = o_raw[:, h, :, :]
                        dve.tensor_tensor(o, o, rs_y[:, 0:ST].unsqueeze(2).broadcast_to([P, ST, P]), ALU.mult).then_inc(o_normed, 1)
                    elif kind == "F":
                        dve.wait_ge(t_done, T_USE[(kind, m)] + 1)
                        dve.wait_ge(gates_done, m + 1)
                        dve.scalar_tensor_tensor(out=gT[:, m, :], in0=bank_t[:], scalar=sub_s[:, 0:1] if m < DA_HEADS else 0.5,
                                                 in1=gT[:, m, :], op0=ALU.mult, op1=ALU.mult).then_inc(t_free, 1)
                        dve.wait_ge(t_free, T_USE[(kind, m)] + 1)
                        done(dve.tensor_copy(mix_hi[:, m, :], gT[:, m, :]))
                        dve.tensor_tensor(mix_lo[:, m, :], gT[:, m, :], mix_hi[:, m, :].bitcast(F32), ALU.subtract).then_inc(mixed, 1)
                    elif kind == "S2":
                        i, j = divmod(m, KV_HEADS)
                        width = P if i == 0 else 2 * P
                        if m == 0:
                            dve.wait_ge(setup_mask, 1)
                        dve.wait_ge(scores2, m + 1)
                        if m >= 2:
                            dve.wait_ge(t_done, T_USE[("TP", m - 2)] + 1)
                        for r in range(GROUP):
                            last = dve.tensor_tensor_reduce(
                                prob2[:, m % 2, r, 0:width], score[:, r % 2, (r // 2) * 256:(r // 2) * 256 + width],
                                mask[:, 2 * P - width:2 * P], 1.0, -3e38, ALU.subtract, ALU.max, mx2[:, m % 4, r:r + 1])
                        last.then_inc(score2_read, 1)
                        dve.wait_ge(score2_read, m + 1)
                        if i:
                            done(dve.tensor_tensor(prob2[:, m % 2, :, 0:P], prob2[:, m % 2, :, 0:P], prob2[:, m % 2, :, P:2 * P], ALU.max))
                        done(dve.scalar_tensor_tensor(out=neg_m2[:, m % 4, :], in0=mx2[:, m % 4, :], scalar=-1.0,
                                                      in1=neg_sink[:, 4 * j:4 * j + 4], op0=ALU.mult, op1=ALU.min))
                        dve.tensor_tensor(sink_m[:, m % 4, :], neg_m2[:, m % 4, :], sink[:, 4 * j:4 * j + 4], ALU.add).then_inc(neg_max2, 1)
                    elif kind == "W2":
                        dve.wait_ge(exp2_done, m + 1)
                        done(dve.tensor_tensor(den2[:, m % 4, :], den2[:, m % 4, :], sink_e[:, m % 4, :], ALU.add))
                        done(dve.reciprocal(rec2[:, m % 4, :], den2[:, m % 4, :]))
                        w = prob2[:, m % 2, :, 0:P]
                        dve.tensor_tensor(w, w, rec2[:, m % 4, :].unsqueeze(2).broadcast_to([P, GROUP, P]), ALU.mult).then_inc(weight2_done, 1)
                    elif kind == "TP":
                        dve.wait_ge(t_done, T_USE[(kind, m)] + 1)
                        if m >= 2:
                            dve.wait_ge(av2_done, m - 1)
                        w = bank_t[:].rearrange("p (r x) -> p r x", r=GROUP)
                        mine = dve.tensor_tensor(pT[:, m % 2, 1, :, :], w, own[:].unsqueeze(1).broadcast_to([P, GROUP, P]), ALU.mult)
                        if m < KV_HEADS:
                            mine.then_inc(t_free, 1)
                        else:
                            done(mine)
                            dve.tensor_tensor(pT[:, m % 2, 0, :, :], w, pT[:, m % 2, 1, :, :], ALU.subtract).then_inc(t_free, 1)
                    elif kind == "AV2":
                        i, j = divmod(m, KV_HEADS)
                        dve.wait_ge(av2_done, m + 1)
                        for c in (2 * j, 2 * j + 1):
                            wait_evacuated(dve, U_Z0 + c // 4, c % 4)
                        for odd in range(2):
                            r = slice(odd * HD, (odd + 1) * HD)
                            g2 = gT2[r, 2 * j:2 * j + 2, i * P:(i + 1) * P]
                            o2 = bank_o[r, :].rearrange("p (c odd q) -> p c odd q", c=2, odd=2)[:, :, odd, :]
                            last = dve.scalar_tensor_tensor(out=g2, in0=o2, scalar=0.5, in1=g2, op0=ALU.mult, op1=ALU.mult)
                        last.then_inc(o2_gated, 1)
                    elif kind == "OS":
                        dve.wait_ge(o2_gated, WIN_STEPS)
                        done(dve.tensor_copy(o2_hi[:, m, :], gT2[:, m, :]))
                        dve.tensor_tensor(o2_lo[:, m, :], gT2[:, m, :], o2_hi[:, m, :].bitcast(F32), ALU.subtract).then_inc(o2_split, 1)

            for n in range(PIECES):
                for half in range(2):
                    if n < WIN_FIRST:
                        take_tiles(n, half)
                    take_steps(n, half)
                    if n >= WIN_FIRST:
                        take_tiles(n, half)

        @block.tensor
        def _(pe):
            def products(out, left, right, first, last):
                pe.matmul(out, left[0], right[0], start=first, stop=False)
                pe.matmul(out, left[0], right[1], start=False, stop=False)
                return pe.matmul(out, left[1], right[0], start=False, stop=last)

            def transposes(step, sources, outs):
                if T_USE[step]:
                    pe.wait_ge(t_free, T_USE[step])
                for src, dst in zip(sources, outs):
                    last = pe.transpose(dst, src, ident[:])
                last.then_inc(t_done, 1)

            def quarters(t):
                return [t[:, c * P:(c + 1) * P] for c in range(4)]

            def step(kind, m):
                if kind == "XT":
                    b, c = divmod(m, KC)
                    if b:
                        for s in range(ST):
                            wait_evacuated(pe, U_O0 + c // 4, s)
                    if c >= 4:
                        pe.wait_ge(xt_split, m - 3)
                    for src, dst in zip([x_rows[b][:, s, c * P:(c + 1) * P] for s in range(ST)], quarters(xt_banks[c % 4])):
                        last = pe.transpose(dst, src, ident[:])
                    last.then_inc(xt_done, 1)
                elif kind == "RS_ROW":
                    pe.wait_ge(diag_done, m + 1)
                    pe.wait_ge(xt_split, KC * m + KC - 1)
                    pe.matmul(bank_o[:], ones[m], diag[m], start=True, stop=True).then_inc(rs_turned, 1)
                elif kind == "ROWS":
                    pe.wait_ge(params, 16 * N_PARAMS)
                    pe.wait_ge(xt_split, KC)
                    pe.transpose(bank_t[:, 0:ROWS], rows[:], ident[0:ROWS, 0:ROWS]).then_inc(rows_turned, 1)
                elif kind in ("KT", "QT"):
                    pe.wait_ge(heads_done, ST if kind == "KT" else 2 * ST)
                    transposes((kind, m), [qk_dup[:, s, (2 * m + mp) * P:(2 * m + mp + 1) * P]
                                           for mp in range(2) for s in range(ST)], quarters(bank_t) + quarters(bank_o))
                elif kind == "S":
                    h, i = divmod(m, ST)
                    if m == 0:
                        pe.wait_ge(t_free, T_USE[("QT", 3)] + 1)
                    else:
                        pe.wait_ge(score_read, 2 * m)
                    for mp in range(2):
                        q = q_stack[:, 2 * h + mp, i * P:(i + 1) * P]
                        pe.matmul(score[:, mp, :], q, k_hi2[:, 2 * h + mp, :], start=True, stop=False)
                        last = pe.matmul(score[:, mp, :], q, k_lo2[:, 2 * h + mp, :], start=False, stop=True)
                    last.then_inc(scores_done, 1)
                elif kind == "TW":
                    pe.wait_ge(weight_done, m + 1)
                    transposes((kind, m), quarters(prob[:, m % 2, 0, :]), quarters(bank_t))
                elif kind == "AV":
                    h, i = divmod(m, ST)
                    pe.wait_ge(t_free, T_USE[("TW", m)] + 1)
                    if m == 0:
                        for j in range(ST):
                            wait_evacuated(pe, U_V, j)
                    if i == 0 and h:
                        pe.wait_ge(o_free, h)
                    for c in range(4):
                        last = pe.matmul(bank_o[:, i * P:(i + 1) * P], wT[:, m % 2, c * P:(c + 1) * P],
                                         va[:, c, h * P:(h + 1) * P], start=(c == 0), stop=(c == 3))
                    last.then_inc(av_done, 1)
                elif kind == "RS":
                    h, i = divmod(m, ST)
                    r = slice((h % 2) * HD, (h % 2 + 1) * HD)
                    if m == 0:
                        for j in range(4):
                            wait_evacuated(pe, U_RQK, j)
                    if m < 2:
                        pe.wait_ge(score_read, 2 * DA_STEPS)
                    else:
                        pe.wait_ge(ret_weight, m - 1)
                    for c in range(4):
                        k = ST - 1 - c
                        last = pe.matmul(score[:, m % 2, c * P:(c + 1) * P], rqkT[r, 2 + h // 2, k * P:(k + 1) * P],
                                         rqkT[r, h // 2, i * P:(i + 1) * P], start=True, stop=True)
                    last.then_inc(ret_scores, 1)
                elif kind == "RA":
                    h, i = divmod(m, ST)
                    pe.wait_ge(ret_weight, m + 1)
                    if m == 0:
                        for j in range(ST):
                            wait_evacuated(pe, U_RV, j)
                    if i == 0:
                        pe.wait_ge(o_free, DA_HEADS + h)
                    for c in range(4):
                        last = pe.matmul(bank_o[:, i * P:(i + 1) * P], prob[:, m % 2, 0, c * P:(c + 1) * P],
                                         vr[:, ST - 1 - c, h * P:(h + 1) * P], start=(c == 0), stop=(c == 3))
                    last.then_inc(av_done, 1)
                elif kind == "F":
                    pe.wait_ge(o_normed, m + 1)
                    transposes((kind, m), [o_raw[:, m % 4, i, :] for i in range(ST)], quarters(bank_t))
                elif kind == "KT2":
                    pe.wait_ge(heads_done, 3 * ST)
                    transposes((kind, m), [k_dup[:, s, m * P:(m + 1) * P] for s in range(ST)], quarters(bank_t))
                elif kind == "QT2":
                    pe.wait_ge(heads_done, (4 + m // 4) * ST)
                    transposes((kind, m), [stage2[:, s, (m % 4) * P:(m % 4 + 1) * P] for s in range(ST)], quarters(bank_t))
                elif kind == "S2":
                    i, j = divmod(m, KV_HEADS)
                    keys = slice(max(i - 1, 0) * P, (i + 1) * P)
                    width = P if i == 0 else 2 * P
                    if m == 0:
                        pe.wait_ge(t_free, T_USE[("QT2", 7)] + 1)
                    else:
                        pe.wait_ge(score2_read, m)
                    for r in range(GROUP):
                        half = slice((r % 2) * HD, (r % 2 + 1) * HD)
                        last = pe.matmul(score[:, r % 2, (r // 2) * 256:(r // 2) * 256 + width],
                                         qT2[half, 2 * j + r // 2, i * P:(i + 1) * P], kT2[half, j, keys], start=True, stop=True)
                    last.then_inc(scores2, 1)
                elif kind == "TP":
                    pe.wait_ge(weight2_done, m + 1)
                    transposes((kind, m), [prob2[:, m % 2, r, 0:P] for r in range(GROUP)], quarters(bank_t))
                elif kind == "AV2":
                    i, j = divmod(m, KV_HEADS)
                    pe.wait_ge(t_free, T_USE[("TP", m)] + 1)
                    if m == 0:
                        for s in range(ST):
                            wait_evacuated(pe, U_KV, s)
                        pe.wait_ge(o_free, DA_HEADS + RET_HEADS)
                    else:
                        pe.wait_ge(o2_gated, m)
                    tiles = [1] if i == 0 else [0, 1]
                    for c in tiles:
                        last = pe.matmul(bank_o[:], v2[:, i - 1 + c, j, :], pT[:, m % 2, c, :, :].rearrange("p r q -> p (r q)"),
                                         start=(c == tiles[0]), stop=(c == 1))
                    last.then_inc(av2_done, 1)

            pe.wait_ge(setup, 1)
            pe.wait_ge(norms_landed, 32)
            pe.transpose(bank_t[:, 0:2 * KC], norm_rows[:], ident[0:2 * KC, 0:2 * KC]).then_inc(norms_turned, 1)
            pe.wait_ge(norms_ready, 1)
            for s in range(ST):
                pe.wait_ge(x_landed[s], 16)
                for c in range(4):
                    last = pe.transpose(xt_banks[c][:, s * P:(s + 1) * P], x_in[:, s, c * P:(c + 1) * P], ident[:])
                    if s == ST - 1:
                        last.then_inc(xt_done, 1)
            for n in range(PIECES):
                u, q = divmod(n, 4)
                slot = n % SLOTS
                if u in (U_KV, U_Q20, U_Q21):
                    left = x_raw[1]
                elif u in (U_O0, U_O1):
                    left = (mix_hi, mix_lo)
                elif u >= U_OUT:
                    left = (yc_hi, yc_lo)
                else:
                    left = (xt_hi, xt_lo)
                if UNIT[u][0] == NAT:
                    w = [t[:, slot, :].rearrange("p (k c) -> p k c", k=2) for t in (w_hi, w_lo)]
                    order = [(kk, s) for kk in range(2) for s in range(ST)] if q < 3 else [(kk, s) for s in range(ST) for kk in range(2)]
                    for e, (kk, s) in enumerate(order):
                        if q == 0 and kk == 0 and u:
                            pe.wait_ge(evacuated[s], u)
                        if u in (U_K, U_KV) and (s == 0 or q == 3):
                            pe.wait_ge(xt_split, (KC if u == U_KV else 0) + 2 * q + kk + 1)
                        if u == U_O0 and (s == 0 or q == 3):
                            pe.wait_ge(mixed, 2 * q + kk + 1)
                        if u == U_OUT and (s == 0 or q == 3):
                            pe.wait_ge(merged, 2 * q + kk + 1)
                        if e == 0:
                            pe.wait_ge(w_split, n + 1)
                        k = 2 * q + kk
                        last = products(bank(u, s), [t[:, k, s * P:(s + 1) * P] for t in left], [t[:, kk, :] for t in w],
                                        k == 0, k == KC - 1)
                        if e == 7:
                            last.then_inc(piece_done, 1)
                        elif q == 3 and kk == 1:
                            last.then_inc(natural_done, 1)
                        if e % 4 == 3:
                            for kind, m in STEPS[(n, e // 4)]:
                                step(kind, m)
                else:
                    w = [t[:, slot, :].rearrange("p (k c) -> p k c", k=KC) for t in (w_hi, w_lo)]
                    right = left
                    if U_GATE_A <= u < U_OUT and q % 2:
                        right = (yc_hi, yc_lo) if u < U_GATE_B else (o2_hi, o2_lo)
                        if u == U_GATE_A:
                            pe.wait_ge(yc_done, KC)
                        if u == U_GATE_B:
                            pe.wait_ge(o2_split, KC)
                    if u == U_Z0 and q == 0:
                        pe.wait_ge(xt_scaled, KC)
                    pe.wait_ge(evacuated[q], u)
                    pe.wait_ge(w_split, n + 1)
                    for k in range(KC):
                        last = products(bank(u, q), [t[:, k, :] for t in w], [t[:, k, :] for t in right], k == 0, k == KC - 1)
                        if k == KC - 1:
                            last.then_inc(piece_done, 1)
                        if k % 4 == 3:
                            for kind, m in STEPS[(n, k // 4)]:
                                step(kind, m)


_INS = ["x", "norm_w", "w_in", "q_norm_w", "k_norm_w", "lambda_q1", "lambda_k1", "lambda_q2", "lambda_k2", "subln_w",
        "ret_decay_fwd", "ret_decay_bwd", "w_out", "norm_g_2", "w_in_2", "conv_w_2", "q_norm_g_2", "k_norm_g_2",
        "sinks_2", "w_conv_out_2", "w_attn_out_2", "gate_b_2", "w_out_2"]


def kernel(**inputs):
    import numpy as _np
    import concourse.bacc as _bacc
    from concourse import mybir as _mybir
    from concourse.bass_utils import run_bass_kernel_spmd as _run

    nc = _bacc.Bacc("TRN2", target_bir_lowering=False, num_devices=1)
    arrays, args = {}, {}
    for name in _INS:
        v = _np.ascontiguousarray(inputs[name])
        arrays[f"in_{name}_dram"] = v
        args[name] = nc.dram_tensor(f"in_{name}_dram", v.shape, _mybir.dt.from_np(v.dtype), kind="ExternalInput").ap()
    args["out"] = nc.dram_tensor("out_0_dram", (1, S, D), _mybir.dt.float32, kind="ExternalOutput").ap()
    build(nc, args)
    r = _run(nc, [arrays], core_ids=[0])
    return r.results[0]["out_0_dram"]
```

```python
from contextlib import ExitStack

import concourse.bass as bass
from concourse import mybir

F32 = mybir.dt.float32
F32R = mybir.dt.float32r
I32 = mybir.dt.int32
ALU = mybir.AluOpType
ACT = mybir.ActivationFunctionType
AXX = mybir.AxisListType.X

P = 128
S = 512
ST = S // P
D = 1024
KC = D // P
EPS = 1e-6
LAMBDA_INIT = 0.8 - 0.6
HD = 64
QK_SCALE = HD ** -0.5
DA_HEADS = 4
RET_HEADS = 4
KV_HEADS = 4
GROUP = 4
TAB = (2 * ST - 1) * P
CENTRE = (ST - 1) * P
BIG = 1e30
R_GATE = 3 * KC
R_KW = R_GATE + 2 * KC
ROWS = R_KW + 5
SLOTS = 4
RSQRT_SEED = 0x5F3759DF

NAT, TRA = "natural", "transposed"
(U_K, U_Q, U_V, U_RQK, U_RV, U_GA, U_GR, U_O0, U_O1, U_KV, U_Q20, U_Q21, U_Z0, U_Z1) = range(14)
U_CONV = 14
U_GATE_A = U_CONV + KC
U_GATE_B = U_GATE_A + KC // 2
U_OUT = U_GATE_B + KC // 2
UNITS = U_OUT + 2
PIECES = 4 * UNITS
CV, CB, CC, CZ, Q2, K2, Z2, G2 = 0, 1024, 2048, 3072, 4096, 5120, 5632, 6656


def unit_columns(u):
    if u < U_CONV:
        return [
            (NAT, [("w_in", 512)]), (NAT, [("w_in", 0)]), (NAT, [("w_in", 1024)]),
            (NAT, [("w_in", 2048)]), (NAT, [("w_in", 2560)]),
            (TRA, [("w_in", 1536 + P * j) for j in range(4)]), (TRA, [("w_in", 3072 + P * j) for j in range(4)]),
            (NAT, [("w_out", 0)]), (NAT, [("w_out", 512)]),
            (NAT, [("w_in_2", K2)]), (NAT, [("w_in_2", Q2)]), (NAT, [("w_in_2", Q2 + 512)]),
            (TRA, [("w_in_2", Z2 + P * j) for j in range(4)]),
            (TRA, [("w_in_2", Z2 + 512 + P * j) for j in range(4)])][u]
    if u < U_GATE_A:
        t = u - U_CONV
        return TRA, [("w_in_2", c + P * t) for c in (CV, CC, CB, CZ)]
    if u < U_OUT:
        t = 2 * ((u - U_GATE_A) % (KC // 2))
        gate, other = (G2, "w_conv_out_2") if u < U_GATE_B else (G2 + D, "w_attn_out_2")
        return TRA, [("w_in_2", gate + P * t), (other, P * t), ("w_in_2", gate + P * t + P), (other, P * t + P)]
    return NAT, [("w_out_2", 512 * (u - U_OUT))]


UNIT = [unit_columns(u) for u in range(UNITS)]
NATURAL_BEFORE = [sum(UNIT[v][0] == NAT for v in range(u)) for u in range(UNITS)]


DA_STEPS = DA_HEADS * ST
WIN_STEPS = ST * KV_HEADS
DA_FIRST = 4 * U_RQK
RET_FIRST = DA_STEPS + 6
WIN_FIRST = 4 * U_Z0 + 5
XS_HOOKS = (9, 10, 11, 12, 13, 14, 20, 21)


TURNS = [("KT", U_Q, 0), ("QT", U_V, 0), ("KT2", U_Q20, 0), ("QT2", U_Q21, 0), ("QT2", U_Z0, 4)]


def steps_after(n, half):
    out = []
    i = 2 * n + half
    if 0 <= i < 4:
        out.append(("XT", 4 + i))
    i = 2 * (n - 4 * U_O1 - 1) + half
    if 0 <= i < 4:
        out.append(("XT", KC + i))
    i = 2 * (n - 4 * U_KV) + half - 1
    if 0 <= i < 4:
        out.append(("XT", KC + 4 + i))
    for b, unit in enumerate((U_K, U_KV)):
        i = 2 * (n - 4 * unit) + half
        if i == 4:
            out.append(("RS_X", b))
        if i == 6:
            out.append(("RS_ROW", b))
    if (n, half) == (2, 1):
        out.append(("ROWS", 0))
    i = 2 * (n - 4 * U_GA) + half
    if 2 <= i < 2 + 2 * KC and i % 2 == 0:
        out.append(("GATE", i // 2 - 1))
    for kind, unit, first in TURNS:
        j = 2 * (n - 4 * unit) + half - (4 if kind == "QT" else 3)
        if 0 <= j < 4:
            out.append((kind, first + j))
    i = 2 * (n - 4 * U_KV) + half
    if i in XS_HOOKS:
        out.append(("XS", XS_HOOKS.index(i)))
    if (n, half) == (3, 0):
        out.append(("DECAYS", 0))
    g = 2 * (n - DA_FIRST) + half
    if 3 <= g < DA_STEPS + 3:
        out.append(("AV", g - 3))
    if 2 <= g < DA_STEPS + 2:
        out.append(("TW", g - 2))
    if 0 <= g < DA_STEPS:
        out.append(("S", g))
    if 1 <= g < DA_STEPS + 1:
        out.append(("W", g - 1))
    if 3 <= g < DA_STEPS + 3 and g % ST == (ST - 1 + 3) % ST:
        out.append(("AN", (g - 3) // ST))
    out += [("ON", h) for h in range(DA_HEADS) if g == DA_STEPS + 3 + h // 2]
    if g in (10, 11):
        out.append(("RN", g - 10))
    if g == DA_STEPS:
        out += [("RN", 2), ("RN", 3)]
    x = 2 * (g - DA_STEPS - 1)
    if 0 <= x < 8:
        out += [("RT", x), ("RT", x + 1)]
    h, odd = divmod(g - RET_FIRST, 2)
    if not odd:
        if 0 <= h < RET_HEADS:
            out += [("KV", h), ("RS", h)]
        if 1 <= h < RET_HEADS + 1:
            out.append(("RA", h - 1))
    finals = {20: 0, 21: 1, 23: 2, 25: 3, 27: 4, 29: 5, 31: 6, 34: 7}
    if g in finals:
        out.append(("F", finals[g]))
    if odd and 1 <= h < RET_HEADS + 1:
        out.append(("RB", h - 1))
    k, phase = divmod(2 * (n - WIN_FIRST) + half, 3)
    if phase == 0:
        if 0 <= k < WIN_STEPS:
            out.append(("S2", k))
        if 2 <= k < WIN_STEPS + 2:
            out += [("AV2", k - 2), ("AG", k - 2)]
    elif phase == 1:
        if 1 <= k < WIN_STEPS + 1:
            out.append(("TP", k - 1))
        if 0 <= k < WIN_STEPS:
            out.append(("W2", k))
    elif 1 <= k < WIN_STEPS + 1:
        out.append(("TL", k - 1))
    i = 2 * (n - WIN_FIRST) + half - 3 * (WIN_STEPS + 2)
    if 0 <= i < 2 * KC and i % 2 == 0:
        out.append(("OS", i // 2))
    return out


def tiles_wait(n, half):
    k, phase = divmod(2 * (n - WIN_FIRST) + half, 3)
    return half == 1 and 0 <= k < WIN_STEPS + 2 and phase in (0, 1)


STEPS = {(n, half): steps_after(n, half) for n in range(PIECES) for half in range(2)}
BANK_T_USERS = ("KT", "QT", "TW", "F", "KT2", "QT2", "TP")
T_USE = {}
for _n in range(PIECES):
    for _half in range(2):
        for _step in STEPS[(_n, _half)]:
            if _step[0] in BANK_T_USERS:
                T_USE[_step] = len(T_USE)


def tiles_done(n, half):
    u, q = divmod(n, 4)
    if UNIT[u][0] == TRA:
        return [(u, q)] if half == 1 else []
    return [(u, 2 * half), (u, 2 * half + 1)] if q == 3 else []


def build(nc, a):
    with ExitStack() as ctx:
        def sb(name, shape, dt=F32, stack=ctx):
            return stack.enter_context(nc.sbuf_tensor(name, shape, dt))

        def sem(name):
            return ctx.enter_context(nc.semaphore(name))

        w_hi = sb("w_hi", [P, SLOTS, D], F32R)
        landing = ExitStack()
        w_raw = sb("w_raw", [P, SLOTS, D], stack=landing)
        landing.close()
        w_lo = sb("w_lo", [P, SLOTS, D], F32R)
        xt_hi = sb("xt_hi", [P, KC, S], F32R)
        xt_lo = sb("xt_lo", [P, KC, S], F32R)
        ident = sb("ident", [P, P])
        mask = sb("mask", [P, 2 * P])
        own = sb("own", [P, P])
        cols = sb("cols", [P, ROWS])
        norm_cols = sb("norm_cols", [P, 2 * KC])
        qws = sb("qws", [P, 1]); q2ws = sb("q2ws", [P, 1]); sub_s = sb("sub_s", [P, 1])
        lam_s = sb("lam_s", [P, 2]); lam_e = sb("lam_e", [P, 2]); neg_lam = sb("neg_lam", [P, 1])
        lam_j = sb("lam_j", [P, HD])
        dec = sb("dec", [P, 8]); dec_a = sb("dec_a", [P, 8]); dec_e = sb("dec_e", [P, 8])
        dec_z = sb("dec_z", [P, 8]); dec_q = sb("dec_q", [P, 8]); dec_p = sb("dec_p", [P, 8])
        log_g = sb("log_g", [P, 8]); steps_to = sb("steps_to", [P, 4])
        ret_c = sb("ret_c", [P, 6, RET_HEADS]); rs_k = sb("rs_k", [P, ST])
        neg_log_b = sb("neg_log_b", [P, 4])
        sink = sb("sink", [P, 16]); neg_sink = sb("neg_sink", [P, 16])
        half_b = sb("half_b", [P, 16])
        rs_x = sb("rs_x", [P, 2, ST])
        ssq = sb("ssq", [P, 4]); ssq_half = sb("ssq_half", [P, 4, 2])
        rs_v = sb("rs_v", [P, 32]); rs_y = sb("rs_y", [P, 32]); rs_t = sb("rs_t", [P, 32])
        mx = sb("mx", [P, 2, 2]); neg_mx = sb("neg_mx", [P, 2, 2]); den = sb("den", [P, 2, 2])
        rec = sb("rec", [P, 8, 2]); lam_rec = sb("lam_rec", [P, 2, 1])
        mx2 = sb("mx2", [P, 4, 4]); neg_m2 = sb("neg_m2", [P, 4, 4]); sink_m = sb("sink_m", [P, 4, 4])
        den2 = sb("den2", [P, 4, 4]); sink_e = sb("sink_e", [P, 4, 4]); rec2 = sb("rec2", [P, 4, 4])

        conv_w = cols[:, 0:R_GATE].rearrange("p (k t) -> p k t", k=3)
        gate_b = cols[:, R_GATE:R_KW]
        kw, qw, k2w, q2w, sub_w = (cols[:, r:r + 1] for r in range(R_KW, ROWS))

        start = ExitStack()
        x_in = sb("x_in", [P, ST, D], stack=start)
        sq_x = sb("sq_x", [P, ST, D], stack=start)
        norm_rows = sb("norm_rows", [2 * KC, P], stack=start)
        rows = sb("rows", [ROWS, P], stack=start); lam_v = sb("lam_v", [P, 4, HD], stack=start)
        start.close()

        one = ExitStack()
        scoring = ExitStack()
        q_stack = sb("q_stack", [P, 2 * DA_HEADS, S], F32R, stack=scoring)
        scoring.close()
        q_decay = sb("q_decay", [P, ST, RET_HEADS, 2, HD], stack=one)
        q_decT = sb("q_decT", [P, RET_HEADS, S], stack=one)
        dup = ExitStack()
        k_heads = sb("k_heads", [P, ST, 8 * HD], stack=dup)
        dup.close()
        va = sb("va", [P, ST, 512], stack=one)
        rqk = sb("rqk", [P, ST, 512], stack=one)
        prob = sb("prob", [P, 2, 2, S], stack=one)
        weighing = ExitStack()
        wT = sb("wT", [P, 2, S], stack=weighing)
        weighing.close()
        rqT = sb("rqT", [P, 2, S], stack=one)
        sq = sb("sq", [P, S], stack=one)
        th = sb("th", [P, S], stack=one)
        rs_row_1 = sb("rs_row_1", [P, S], stack=one)
        o_raw = sb("o_raw", [P, 4, ST, P], stack=one)
        vr = sb("vr", [P, ST, 512], stack=one)
        gT = sb("gT", [P, KC, S], stack=one)
        mix_hi = sb("mix_hi", [P, KC, S], F32R, stack=one)
        mix_lo = sb("mix_lo", [P, KC, S], F32R, stack=one)
        k_hi2, k_lo2 = mix_hi, mix_lo
        table = sb("table", [P, 2, TAB], stack=one)
        diff = sb("diff", [P, TAB], stack=one)
        rkT = sb("rkT", [P, 2, S], stack=one)
        k_decay = sb("k_decay", [P, ST, RET_HEADS, 2, HD], stack=one)
        dmat = sb("dmat", [P, RET_HEADS, P], stack=one)
        one.close()
        stage = prob[:].rearrange("p a b s -> p (a b) s")

        two = ExitStack()
        x1 = sb("x1", [P, ST, D], stack=two)
        gT2 = sb("gT2", [P, KC, S], stack=two)
        yc_hi = sb("yc_hi", [P, KC, S], F32R, stack=two)
        yc_lo = sb("yc_lo", [P, KC, S], F32R, stack=two)
        th2 = sb("th2", [P, S], stack=two)
        acc = sb("acc", [P, S], stack=two)
        later = ExitStack()
        o2_hi = sb("o2_hi", [P, KC, S], F32R, stack=later)
        o2_lo = sb("o2_lo", [P, KC, S], F32R, stack=later)
        part = sb("part", [P, KC, S], stack=later)
        later.close()
        turning = ExitStack()
        k_dup = sb("k_dup", [P, ST, S], stack=turning)
        turning.close()
        q2_stack = sb("q2_stack", [P, 8, S], F32R, stack=two)
        k2_hi = sb("k2_hi", [P, KV_HEADS, S], F32R, stack=two)
        k2_lo = sb("k2_lo", [P, KV_HEADS, S], F32R, stack=two)
        v2 = sb("v2", [P, ST, KV_HEADS, 2, HD], F32R, stack=two)
        o2_sum = sb("o2_sum", [P, 2, P], stack=two)
        prob2 = sb("prob2", [P, 2, GROUP, 256], stack=two)
        pT = sb("pT", [P, 2, GROUP, P], stack=two)
        sq2 = sb("sq2", [P, S], stack=two)
        vt = sb("vt", [P, S], stack=two)
        cv = sb("cv", [P, S + 2], stack=two)
        two.close()
        x_rows = (x_in, x1)
        x_raw = ((xt_hi, xt_lo), (yc_hi, yc_lo))
        ones = (table[:, 1, 0:P], th2[:, 0:P])
        diag = (table[:, 1, P:P + S], vt[:])
        rs_row = (rs_row_1[:], acc[:])
        x_tmp = cv[:, 0:S]
        pT_hi, pT_lo = (t[:, 6:8, :].rearrange("p c (r q) -> p c r q", r=GROUP) for t in (yc_hi, yc_lo))

        def q2(h):
            if h < 8:
                return q2_stack[:, h, :].rearrange("p (s q) -> p s q", s=ST)
            return (yc_hi if h < 12 else yc_lo)[:, 2:2 + ST, (h % 4) * P:(h % 4 + 1) * P]

        def halves(c):
            return (slice(0, HD), slice(HD, P))[::1 - 2 * c]

        stage2 = prob2[:].rearrange("p a b s -> p (a b s)").rearrange("p (t s) -> p t s", t=4)

        proj = ctx.enter_context(nc.psum_tensor("proj", [P, SLOTS, S], F32))
        score = ctx.enter_context(nc.psum_tensor("score", [P, 2, S], F32))
        bank_t = ctx.enter_context(nc.psum_tensor("bank_t", [P, S], F32))
        bank_o = ctx.enter_context(nc.psum_tensor("bank_o", [P, S], F32))

        def o2_heads(rows_, odd):
            return bank_o[rows_, :].rearrange("p (c odd q) -> p c odd q", c=2, odd=2)[:, :, odd, :]

        x_landed = [sem(f"x_landed{s}") for s in range(ST)]
        x_again = sem("x_again")
        norms_landed = sem("norms_landed"); norms_turned = sem("norms_turned"); norms_ready = sem("norms_ready")
        params = sem("params")
        rows_turned = sem("rows_turned")
        raw_landed = [sem(f"raw_landed{i}") for i in range(SLOTS)]
        slot_open = sem("slot_open")
        hi_done = sem("hi_done")
        w_split = sem("w_split")
        piece_done = sem("piece_done")
        natural_done = sem("natural_done")
        evacuated = [sem(f"evacuated{b}") for b in range(SLOTS)]
        xt_done = sem("xt_done")
        xt_hi_done = sem("xt_hi_done")
        xt_split = sem("xt_split")
        setup = sem("setup")
        setup_mask = sem("setup_mask")
        ssq_done = sem("ssq_done")
        rs_done = sem("rs_done")
        diag_done = sem("diag_done"); rs_turned = sem("rs_turned"); rs_row_done = sem("rs_row_done")
        xt_scaled = sem("xt_scaled")
        dec_abs = sem("dec_abs"); dec_exp = sem("dec_exp")
        lam_sum = sem("lam_sum"); lam_exp = sem("lam_exp")
        weights_ready = sem("weights_ready")
        sq_done = sem("sq_done"); sq_used = sem("sq_used")
        heads_done = sem("heads_done")
        qk_hi_done = sem("qk_hi_done")
        qk2_hi_done = sem("qk2_hi_done")
        t_done = sem("t_done"); t_free = sem("t_free")
        scores_done = sem("scores_done"); score_read = sem("score_read")
        neg_max = sem("neg_max"); exp_done = sem("exp_done"); weight_done = sem("weight_done")
        av_done = sem("av_done"); o_free = sem("o_free"); o_normed = sem("o_normed")
        diff_done = sem("diff_done"); distance_done = sem("distance_done")
        decay_arg = sem("decay_arg"); decay_done = sem("decay_done")
        ret_scaled = sem("ret_scaled")
        rt_done = sem("rt_done"); rt_free = sem("rt_free")
        kr_done = sem("kr_done"); kr_free = sem("kr_free")
        gates_done = sem("gates_done")
        th_done = sem("th_done"); mixed = sem("mixed")
        scores2 = sem("scores2"); score2_read = sem("score2_read"); neg_max2 = sem("neg_max2")
        exp2_done = sem("exp2_done"); weight2_done = sem("weight2_done")
        rec2_done = sem("rec2_done")
        v2_hi_done = sem("v2_hi_done"); pT_done = sem("pT_done"); pT_hi_done = sem("pT_hi_done"); pT_split = sem("pT_split")
        av2_done = sem("av2_done")
        o2_low = sem("o2_low")
        o2_summed = sem("o2_summed")
        o2_gated = sem("o2_gated")
        o2_split = sem("o2_split"); yc_done = sem("yc_done"); merged = sem("merged")
        cv_zero = sem("cv_zero")
        act_chain = sem("act_chain"); dve_chain = sem("dve_chain"); pool_chain = sem("pool_chain")
        out_written = sem("out_written")

        def wait_tile(eng, u, j):
            if UNIT[u][0] == NAT and j < 3:
                eng.wait_ge(natural_done, 3 * NATURAL_BEFORE[u] + j + 1)
            else:
                eng.wait_ge(piece_done, 4 * u + j + 1)

        def wait_evacuated(eng, u, j):
            eng.wait_ge(evacuated[j], u + 1)

        def bank(u, j):
            return proj[:, j, :]

        turn_banks = [bank_t, bank_o]
        xt_banks = [score[:, 0, :], score[:, 1, :], bank_o[:], bank_t[:]]

        N_PARAMS = 18
        block = ctx.enter_context(nc.Block())

        @block.sync
        def _(sp):
            def load_piece(n):
                u, q = divmod(n, 4)
                kind, cols = UNIT[u]
                if kind == NAT:
                    w, c = cols[0]
                    src = a[w][0, 256 * q:256 * q + 256, c:c + 512].rearrange("(k p) c -> p k c", p=P)
                    dst = w_raw[:, n % SLOTS, :].rearrange("p (k c) -> p k c", k=2)
                else:
                    w, c = cols[q]
                    src = a[w][0, :, c:c + P].rearrange("(k p) c -> p k c", p=P)
                    dst = w_raw[:, n % SLOTS, :].rearrange("p (k c) -> p k c", k=KC)
                sp.dma_start(dst, src).then_inc(raw_landed[n % SLOTS], 16)

            for s in range(ST):
                sp.dma_start(x_in[:, s, :], a["x"][0, s * P:(s + 1) * P, :]).then_inc(x_landed[s], 16)
                if s == 1:
                    load_piece(0)

            def load_parameters():
                sp.dma_start(rows[0:R_GATE, :], a["conv_w_2"][0].rearrange("k (t p) -> (k t) p", p=P)).then_inc(params, 16)
                sp.dma_start(rows[R_GATE:R_KW, :], a["gate_b_2"].rearrange("o (t p) -> (o t) p", p=P)).then_inc(params, 16)
                for i, w in enumerate(("k_norm_w", "q_norm_w", "k_norm_g_2", "q_norm_g_2")):
                    for h in range(2):
                        sp.dma_start(rows[R_KW + i:R_KW + i + 1, h * HD:(h + 1) * HD], a[w]).then_inc(params, 16)
                sp.dma_start(rows[ROWS - 1:ROWS, :], a["subln_w"]).then_inc(params, 16)
                for i, w in enumerate(("lambda_q1", "lambda_q2", "lambda_k1", "lambda_k2")):
                    sp.dma_start(lam_v[:, i, :], a[w][0, :].partition_broadcast(P)).then_inc(params, 16)
                for i, w in enumerate(("ret_decay_fwd", "ret_decay_bwd")):
                    sp.dma_start(dec[:, 4 * i:4 * i + 4], a[w][0, :].partition_broadcast(P)).then_inc(params, 16)
                sp.dma_start(sink[:], a["sinks_2"][0, :].partition_broadcast(P)).then_inc(params, 16)

            for n in range(1, PIECES):
                if n == SLOTS:
                    load_parameters()
                if n >= SLOTS:
                    sp.wait_ge(piece_done, n - SLOTS + 1)
                load_piece(n)
            for h in range(2):
                for s in range(ST):
                    wait_evacuated(sp, U_OUT + h, s)
                    sp.dma_start(a["out"][0, s * P:(s + 1) * P, h * 512:(h + 1) * 512],
                                 x1[:, s, h * 512:(h + 1) * 512]).then_inc(out_written, 16)
            sp.wait_ge(out_written, 16 * 2 * ST)

        @block.gpsimd
        def _(pool):
            pool.memset(ident[:], 0.0).then_inc(pool_chain, 1)
            pool.wait_ge(pool_chain, 1)
            pool.affine_select(out=ident[:], in_=ident[:], compare_op=ALU.not_equal, fill=1.0, base=0,
                               pattern=[[-1, P]], channel_multiplier=1).then_inc(setup, 1)

            pool.iota(table[:, 0, :].bitcast(I32), pattern=[[1, TAB]], base=-CENTRE, channel_multiplier=-1).then_inc(setup, 1)
            pool.memset(mask[:], 0.0).then_inc(pool_chain, 1)
            pool.wait_ge(pool_chain, 2)
            pool.affine_select(out=mask[:], in_=mask[:], compare_op=ALU.is_ge, fill=BIG, base=P,
                               pattern=[[-1, 2 * P]], channel_multiplier=1).then_inc(pool_chain, 1)
            pool.wait_ge(pool_chain, 3)
            pool.affine_select(out=mask[:], in_=mask[:], compare_op=ALU.is_ge, fill=BIG, base=-1,
                               pattern=[[1, 2 * P]], channel_multiplier=-1).then_inc(pool_chain, 1)
            pool.memset(own[:], 1.0).then_inc(pool_chain, 1)
            pool.wait_ge(pool_chain, 5)
            pool.affine_select(out=own[:], in_=own[:], compare_op=ALU.is_ge, fill=0.0, base=0,
                               pattern=[[1, P]], channel_multiplier=-1).then_inc(setup_mask, 1)

            def split(n, slot):
                pool.tensor_scalar(w_hi[:, slot, :], w_raw[:, slot, :], 1.0, 1.0, ALU.mult, ALU.mult).then_inc(hi_done, 1)
                pool.wait_ge(hi_done, n + 1)
                pool.tensor_tensor(w_lo[:, slot, :], w_raw[:, slot, :], w_hi[:, slot, :].bitcast(F32),
                                   ALU.subtract).then_inc(w_split, 1)

            for n in range(SLOTS):
                pool.wait_ge(raw_landed[n], 16)
                split(n, n)
            with pool.Fori(1, PIECES // SLOTS) as g:
                for slot in range(SLOTS):
                    pool.wait_ge(raw_landed[slot], 16 * g + 16)
                    pool.wait_ge(piece_done, SLOTS * g + slot - SLOTS + 1)
                    pool.sem_inc(slot_open, 1)
                    split(SLOTS * g + slot, slot)

        @block.scalar
        def _(act):
            for b, w in enumerate(("norm_w", "norm_g_2")):
                act.dma_start(norm_rows[KC * b:KC * b + KC, :], a[w][0].rearrange("(t p) -> t p", p=P)).then_inc(norms_landed, 16)

            chain = [0]

            def done(ins):
                chain[0] += 1
                ins.then_inc(act_chain, 1)
                act.wait_ge(act_chain, chain[0])

            def take_xt(m):
                b, c = divmod(m, KC)
                act.wait_ge(xt_done, m + 1)
                if m == KC + 4:
                    act.wait_ge(ssq_done, 3 * ST)
                act.activation(x_raw[b][0][:, c, :], xt_banks[c % 4], ACT.Copy, scale=norm_cols[:, m:m + 1]).then_inc(xt_hi_done, 1)

            def row_squares(s):
                act.wait_ge(x_landed[s], 16)
                act.activation(sq_x[:, s, :], x_in[:, s, :], ACT.Square, accum_out=ssq[:, s:s + 1]).then_inc(ssq_done, 1)

            row_squares(0)
            row_squares(1)
            act.wait_ge(norms_ready, 1)
            for c in range(4):
                take_xt(c)
            row_squares(2)
            row_squares(3)
            squares = [0]

            def square(dst, src):
                if squares[0]:
                    act.wait_ge(sq_used, squares[0])
                act.activation(dst, src, ACT.Square).then_inc(sq_done, 1)
                squares[0] += 1

            def distance_table(h):
                act.activation(table[:, h % 2, :], diff[:], ACT.Abs, scale=2.0 ** (-8.0 * (h + 1) / DA_HEADS)).then_inc(distance_done, 1)

            last_tanh = ()

            def take_low(m):
                act.wait_ge(av2_done, m + 1)
                if m:
                    act.wait_ge(o2_gated, m)
                for odd in range(2):
                    act.activation(o2_sum[odd * HD:(odd + 1) * HD, :, :], o2_heads(slice(HD, P), odd), ACT.Copy).then_inc(o2_low, 1)

            def take_retention(m):
                act.wait_ge(rt_done, m + 1)
                if m == 6:
                    act.wait_ge(av_done, DA_STEPS)
                dst = rkT[:, m, :] if m < 2 else q_decT[:, m - 2, :] if m < 6 else rqT[:, m - 6, :]
                act.activation(dst, score[:, m % 2, :], ACT.Copy).then_inc(rt_free, 1)

            for n in range(PIECES):
                for half in range(2):
                    for kind, m in STEPS[(n, half)]:
                        if kind == "RT":
                            take_retention(m)
                    for u, j in tiles_done(n, half):
                        if u >= U_CONV and u < U_GATE_A and j in (1, 2):
                            continue
                        if u >= U_GATE_A and (u >= U_OUT or j % 2):
                            continue
                        wait_tile(act, u, j)
                        b = bank(u, j)
                        if u in (U_K, U_Q):
                            if u == U_Q:
                                act.wait_ge(heads_done, ST)
                            act.wait_ge(rs_done, 1)
                            act.activation(stage[:, j, :], b, ACT.Copy, scale=rs_x[:, 0, j:j + 1]).then_inc(evacuated[j], 1)
                            if u == U_K:
                                wait_evacuated(act, u, j)
                                square(sq[:], stage[:, j, :])
                        elif u == U_V:
                            act.wait_ge(t_done, T_USE[("KT", 3)] + 1)
                            act.activation(va[:, j, :], b, ACT.Copy, scale=rs_x[:, 0, j:j + 1]).then_inc(evacuated[j], 1)
                        elif u == U_RQK:
                            act.wait_ge(t_done, T_USE[("KT", 3)] + 1)
                            act.activation(rqk[:, j, 0:256], b[:, 0:256], ACT.Copy, scale=rs_x[:, 0, j:j + 1])
                            act.activation(rqk[:, j, 256:512], b[:, 256:512], ACT.Copy, scale=rs_k[:, j:j + 1]).then_inc(evacuated[j], 1)
                        elif u == U_RV:
                            act.activation(vr[:, j, :], b, ACT.Copy, scale=rs_x[:, 0, j:j + 1]).then_inc(evacuated[j], 1)
                        elif u in (U_GA, U_GR):
                            g = 4 * (u - U_GA) + j
                            wait_evacuated(act, u, j)
                            if g:
                                act.wait_ge(gates_done, g)
                            act.activation(th[:], gT[:, g, :], ACT.Tanh, scale=0.5).then_inc(th_done, 1)
                        elif u in (U_O0, U_O1):
                            h = u - U_O0
                            wait_evacuated(act, u, j)
                            act.wait_ge(sq_used, squares[0])
                            act.wait_ge(ssq_done, ST + ST * h + j)
                            act.activation(sq[:], x1[:, j, h * 512:(h + 1) * 512], ACT.Square,
                                           accum_out=ssq_half[:, j, h:h + 1]).then_inc(ssq_done, 1)
                        elif u == U_KV:
                            act.wait_ge(rs_done, 2)
                            done(act.activation(stage2[:, j, 0:256], b[:, 0:256], ACT.Copy, scale=rs_x[:, 1, j:j + 1]))
                            act.activation(v2[:, j, :, 0, :],
                                                b[:, 256:512].rearrange("p (h d) -> p h d", h=KV_HEADS),
                                                ACT.Copy, scale=rs_x[:, 1, j:j + 1]).then_inc(v2_hi_done, 1)
                            square(sq2[:, 0:256], stage2[:, j, 0:256])
                        elif u in (U_Q20, U_Q21):
                            if u == U_Q20:
                                act.wait_ge(heads_done, 8 + ST)
                            else:
                                act.wait_ge(t_done, T_USE[("QT2", 3)] + 1)
                            act.activation(stage2[:, j, :], b, ACT.Copy, scale=rs_x[:, 1, j:j + 1]).then_inc(evacuated[j], 1)
                            wait_evacuated(act, u, j)
                            square(sq2[:], stage2[:, j, :])
                        elif U_CONV <= u < U_GATE_A and j == 0:
                            if u > U_CONV:
                                wait_evacuated(act, u - 1, 1)
                            act.activation(vt[:], b, ACT.Copy).then_inc(evacuated[0], 1)
                        else:
                            if U_CONV < u <= U_GATE_A and last_tanh[0] < U_GATE_A:
                                act.wait_ge(yc_done, u - U_CONV)
                            elif last_tanh:
                                wait_evacuated(act, last_tanh[0], last_tanh[1] + (u >= U_GATE_A))
                            last_tanh = (u, j)
                            if u < U_GATE_A:
                                act.activation(th2[:], b, ACT.Tanh, scale=0.5).then_inc(th_done, 1)
                            else:
                                t = 2 * ((u - U_GATE_A) % (KC // 2)) + j // 2 + (KC if u >= U_GATE_B else 0)
                                act.activation(th2[:], b, ACT.Tanh, bias=half_b[:, t:t + 1], scale=0.5).then_inc(evacuated[j], 1)

                    if (n, half) == (4 * U_Q + 3, 1):
                        for j in range(ST):
                            wait_evacuated(act, U_Q, j)
                            square(sq[:], stage[:, j, :])

                    for kind, m in STEPS[(n, half)]:
                        if kind == "XT":
                            take_xt(m)
                        elif kind == "RS_ROW":
                            act.wait_ge(rs_turned, m + 1)
                            act.activation(rs_row[m], bank_o[:], ACT.Copy).then_inc(rs_row_done, 1)
                        elif kind == "ROWS":
                            act.wait_ge(dec_abs, 1)
                            act.activation(dec_e[:], dec_a[:], ACT.Exp, scale=-1.0).then_inc(dec_exp, 1)
                            act.wait_ge(lam_sum, 1)
                            act.activation(lam_e[:], lam_s[:], ACT.Exp).then_inc(lam_exp, 1)
                        elif kind == "KT":
                            if m == 0:
                                act.wait_ge(weights_ready, 1)
                            act.wait_ge(t_done, T_USE[(kind, m)] + 1)
                            for mp in range(2):
                                here, there = halves(mp)
                                for r in (here, there):
                                    last = act.activation(k_hi2[r, 2 * m + mp, :], turn_banks[m % 2][here, :], ACT.Copy, scale=kw[here, :])
                                last.then_inc(qk_hi_done, 1)
                        elif kind == "QT":
                            act.wait_ge(t_done, T_USE[(kind, m)] + 1)
                            for mp in range(2):
                                here, _ = halves(mp)
                                act.activation(q_stack[here, 2 * m + mp, :], bank_t[here, :], ACT.Copy, scale=qws[here, :]).then_inc(qk_hi_done, 1)
                        elif kind == "TW":
                            act.wait_ge(t_done, T_USE[(kind, m)] + 1)
                            if m >= 2:
                                act.wait_ge(av_done, m - 1)
                            act.activation(wT[:, m % 2, :], bank_t[:], ACT.Copy).then_inc(t_free, 1)
                        elif kind == "S":
                            act.wait_ge(neg_max, m + 1)
                            for mp in range(2):
                                act.activation(prob[:, m % 2, mp, :], prob[:, m % 2, mp, :], ACT.Exp,
                                               bias=neg_mx[:, m % 2, mp:mp + 1],
                                               accum_out=den[:, m % 2, mp:mp + 1]).then_inc(exp_done, 1)
                            if m % ST == 0 and ST <= m < DA_STEPS - ST:
                                distance_table(m // ST + 1)
                        elif kind == "RA" or kind == "AV" and m % ST == ST - 1:
                            h = m // ST if kind == "AV" else DA_HEADS + m
                            act.wait_ge(av_done, m + 1 if kind == "AV" else DA_STEPS + m + 1)
                            if h >= 4:
                                act.wait_ge(t_done, T_USE[("F", h - 4)] + 1)
                            o = o_raw[:, h % 4, :, :].rearrange("p i v -> p (i v)")
                            if kind == "AV":
                                for i in range(ST):
                                    last = act.activation(o_raw[:, h, i, :], bank_o[:, i * P:(i + 1) * P], ACT.Copy,
                                                          scale=rec[:, (m - m % ST + i) % 8, 0:1])
                                last.then_inc(o_free, 1)
                            else:
                                act.activation(o, bank_o[:], ACT.Copy).then_inc(o_free, 1)
                            act.wait_ge(o_free, h + 1)
                            square(sq[:], o)
                        elif kind == "KT2":
                            act.wait_ge(t_done, T_USE[(kind, m)] + 1)
                            act.activation(k2_hi[:, m, :], bank_t[:], ACT.Copy, scale=k2w).then_inc(qk2_hi_done, 1)
                        elif kind == "QT2":
                            act.wait_ge(t_done, T_USE[(kind, m)] + 1)
                            for c in range(2):
                                here, _ = halves(c)
                                act.activation(q2(2 * m + c)[here, :, :], bank_t[here, :].rearrange("p (s q) -> p s q", s=ST),
                                               ACT.Copy, scale=q2ws[here, :]).then_inc(qk2_hi_done, 1)
                        elif kind == "S2":
                            if m >= 2:
                                take_low(m - 2)
                            act.wait_ge(neg_max2, m + 1)
                            for r in range(GROUP):
                                act.activation(prob2[:, m % 2, r, 0:P], prob2[:, m % 2, r, 0:P], ACT.Exp,
                                               bias=neg_m2[:, m % 4, r:r + 1], accum_out=den2[:, m % 4, r:r + 1])
                            act.activation(sink_e[:, m % 4, :], sink_m[:, m % 4, :], ACT.Exp).then_inc(exp2_done, 1)
                        elif kind == "W2":
                            act.wait_ge(rec2_done, m + 1)
                            for r in range(GROUP):
                                last = act.activation(prob2[:, m % 2, r, 0:P], prob2[:, m % 2, r, 0:P], ACT.Copy, scale=rec2[:, m % 4, r:r + 1])
                            last.then_inc(weight2_done, 1)
                        elif kind == "AV2" and m >= WIN_STEPS - 2:
                            take_low(m)
                        elif kind == "TP":
                            tiles = 1 if m < KV_HEADS else 2
                            act.wait_ge(pT_done, m + 1)
                            if m:
                                act.wait_ge(av2_done, m)
                            act.activation(pT_hi[:, 0:tiles, :, :], pT[:, 0:tiles, :, :], ACT.Copy).then_inc(pT_hi_done, 1)
                    if (n, half) == (4 * U_V, 0):
                        act.wait_ge(diff_done, 1)
                        act.wait_ge(rs_turned, 1)
                        distance_table(0)
                        distance_table(1)
                    if (n, half) == (4 * U_RQK, 0):
                        act.wait_ge(decay_arg, 1)
                        act.activation(ret_c[:], ret_c[:], ACT.Exp)
                        act.activation(dmat[:], dmat[:], ACT.Exp).then_inc(decay_done, 1)
                    if (n, half) == (4 * U_GR + 3, 1):
                        act.wait_ge(scores_done, DA_STEPS)
                        act.dma_start(x1[:], a["x"][0].rearrange("(t p) d -> p t d", p=P)).then_inc(x_again, 16)

        @block.vector
        def _(dve):
            chain = [0]

            def done(ins):
                chain[0] += 1
                ins.then_inc(dve_chain, 1)
                dve.wait_ge(dve_chain, chain[0])

            def rsqrt(n, width):
                v, y, t = rs_v[:, 0:n], rs_y[:, 0:n], rs_t[:, 0:n]
                done(dve.tensor_scalar(v, v, 1.0 / width, EPS, ALU.mult, ALU.add))
                done(dve.tensor_scalar(t.bitcast(I32), v.bitcast(I32), 1, None, ALU.logical_shift_right))
                done(dve.tensor_scalar(y.bitcast(I32), t.bitcast(I32), -1.0, float(RSQRT_SEED), ALU.mult, ALU.add))
                for _ in range(3):
                    done(dve.scalar_tensor_tensor(out=t, in0=y, scalar=-0.5, in1=y, op0=ALU.mult, op1=ALU.mult))
                    done(dve.tensor_tensor(t, t, v, ALU.mult))
                    done(dve.scalar_tensor_tensor(out=y, in0=t, scalar=1.5, in1=y, op0=ALU.add, op1=ALU.mult))

            def take_xt_low(m):
                b, c = divmod(m, KC)
                dve.wait_ge(xt_hi_done, m + 1)
                dve.scalar_tensor_tensor(out=x_raw[b][1][:, c, :], in0=xt_banks[c % 4], scalar=norm_cols[:, m:m + 1],
                                         in1=x_raw[b][0][:, c, :].bitcast(F32), op0=ALU.mult, op1=ALU.subtract).then_inc(xt_split, 1)

            dve.wait_ge(norms_turned, 1)
            dve.tensor_copy(norm_cols[:], bank_t[:, 0:2 * KC]).then_inc(norms_ready, 1)
            dve.wait_ge(norms_ready, 1)
            for c in range(4):
                take_xt_low(c)

            def prepare_parameters():
                dve.wait_ge(params, 16 * N_PARAMS)
                done(dve.tensor_scalar(dec_a[:], dec[:], -1.0, None, ALU.mult))
                dve.tensor_tensor(dec_a[:], dec_a[:], dec[:], ALU.max).then_inc(dec_abs, 1)
                dve.wait_ge(rows_turned, 1)
                done(dve.tensor_copy(cols[:], bank_t[:, 0:ROWS]))
                done(dve.tensor_tensor_reduce(lam_j[:], lam_v[:, 0, :], lam_v[:, 2, :], 1.0, 0.0, ALU.mult, ALU.add, lam_s[:, 0:1]))
                dve.tensor_tensor_reduce(lam_j[:], lam_v[:, 1, :], lam_v[:, 3, :], 1.0, 0.0, ALU.mult, ALU.add,
                                         lam_s[:, 1:2]).then_inc(lam_sum, 1)
                dve.tensor_scalar(q2ws[:], q2w, QK_SCALE, None, ALU.mult)
                dve.tensor_scalar(sub_s[:], sub_w, 1.0 - LAMBDA_INIT, 0.5, ALU.mult, ALU.mult)
                dve.tensor_scalar(neg_sink[:], sink[:], -1.0, None, ALU.mult)
                dve.tensor_scalar(half_b[:], gate_b, 0.5, None, ALU.mult)
                dve.tensor_scalar(qws[:], qw, QK_SCALE, None, ALU.mult).then_inc(weights_ready, 1)
                dve.wait_ge(dec_exp, 1)
                done(dve.tensor_scalar(dec_z[:], dec_e[:], 2.0, None, ALU.add))
                done(dve.reciprocal(dec_z[:], dec_z[:]))
                done(dve.tensor_tensor(dec_z[:], dec_z[:], dec_e[:], ALU.mult))
                done(dve.tensor_tensor(dec_q[:], dec_z[:], dec_z[:], ALU.mult))
                done(dve.tensor_scalar(dec_p[:], dec_q[:], 1.0 / 17, None, ALU.mult))
                for k in range(15, 2, -2):
                    done(dve.scalar_tensor_tensor(out=dec_p[:], in0=dec_p[:], scalar=1.0 / k, in1=dec_q[:], op0=ALU.add, op1=ALU.mult))
                done(dve.scalar_tensor_tensor(out=dec_p[:], in0=dec_p[:], scalar=1.0, in1=dec_z[:], op0=ALU.add, op1=ALU.mult))
                done(dve.tensor_scalar(dec_p[:], dec_p[:], 2.0, None, ALU.mult))
                done(dve.scalar_tensor_tensor(out=log_g[:], in0=dec[:], scalar=0.0, in1=dec_p[:], op0=ALU.min, op1=ALU.subtract))
                done(dve.tensor_scalar(neg_log_b[:], log_g[:, 4:8], -1.0, None, ALU.mult))
                dve.wait_ge(lam_exp, 1)
                done(dve.scalar_tensor_tensor(out=neg_lam[:], in0=lam_e[:, 1:2], scalar=LAMBDA_INIT, in1=lam_e[:, 0:1],
                                              op0=ALU.subtract, op1=ALU.subtract))
                dve.wait_ge(setup, 2)
                dve.tensor_copy(diff[:], table[:, 0, :].bitcast(I32)).then_inc(diff_done, 1)

            def prepare_decays():
                dve.wait_ge(diff_done, 1)
                minus_p = diff[:, CENTRE:CENTRE + 1]
                for k, (sign, steps) in enumerate(((-1.0, 1.0), (1.0, P), (1.0, P - 1.0), (-1.0, 0.0))):
                    dve.tensor_scalar(steps_to[:, k:k + 1], minus_p, sign, float(steps), ALU.mult, ALU.add).then_inc(dve_chain, 1)
                    chain[0] += 1
                dve.wait_ge(dve_chain, chain[0])
                for k in range(4):
                    dve.tensor_scalar(ret_c[:, k, :], log_g[:, 4 * (k % 2):4 * (k % 2) + 4], steps_to[:, k:k + 1], None, ALU.mult)
                dve.tensor_scalar(ret_c[:, 4:6, :], log_g[:].rearrange("p (c h) -> p c h", c=2), float(P), None, ALU.mult)
                near = diff[:, CENTRE:CENTRE + P]
                for h in range(RET_HEADS):
                    done(dve.tensor_scalar(dmat[:, h, :], near, neg_log_b[:, h:h + 1], None, ALU.mult))
                    last = dve.scalar_tensor_tensor(out=dmat[:, h, :], in0=near, scalar=log_g[:, h:h + 1], in1=dmat[:, h, :],
                                                    op0=ALU.mult, op1=ALU.min)
                last.then_inc(decay_arg, 1)

            sums = [0]

            def head_sums(dst, buf, heads):
                sums[0] += 1
                dve.wait_ge(sq_done, sums[0])
                dve.tensor_reduce(dst, buf.rearrange("p (h d) -> p h d", h=heads), AXX, ALU.add).then_inc(sq_used, 1)

            tanhs = [KC]

            def take_tiles(n, half):
                for u, j in tiles_done(n, half):
                    b = bank(u, j)
                    if u in (U_K, U_Q, U_KV, U_Q20, U_Q21):
                        heads = 4 if u == U_KV else 8
                        st, buf = (stage, sq) if u < U_KV else (stage2, sq2)
                        if u == U_KV:
                            dve.wait_ge(v2_hi_done, j + 1)
                            dve.scalar_tensor_tensor(out=v2[:, j, :, 1, :], in0=b[:, 256:512].rearrange("p (h d) -> p h d", h=KV_HEADS),
                                                     scalar=rs_x[:, 1, j:j + 1], in1=v2[:, j, :, 0, :].bitcast(F32),
                                                     op0=ALU.mult, op1=ALU.subtract).then_inc(evacuated[j], 1)
                        for i in {0: (), 1: (), 2: (0, 1, 2), 3: (3,)}[j] if u == U_Q else (j,):
                            head_sums(rs_v[:, heads * i:heads * i + heads], buf[:, 0:heads * HD], heads)
                        if j == 3:
                            dve.wait_ge(sq_used, sums[0])
                            rsqrt(4 * heads, HD)
                            for s in range(ST):
                                y = rs_y[:, heads * s:heads * s + heads]
                                src = st[:, s, 0:heads * HD].rearrange("p (h d) -> p h d", h=heads)
                                if u == U_K:
                                    dve.tensor_tensor(k_heads[:, s, :].rearrange("p (h d) -> p h d", h=heads), src,
                                                      y.unsqueeze(2).broadcast_to([P, heads, HD]), ALU.mult).then_inc(heads_done, 1)
                                elif u == U_KV:
                                    dst = k_dup[:, s, :]
                                    dve.tensor_tensor(
                                        dst.rearrange("p (h c d) -> p h c d", h=heads, c=2),
                                        src.unsqueeze(2).broadcast_to([P, heads, 2, HD]),
                                        y.unsqueeze(2).unsqueeze(3).broadcast_to([P, heads, 2, HD]), ALU.mult).then_inc(heads_done, 1)
                                else:
                                    dve.tensor_tensor(src, src, y.unsqueeze(2).broadcast_to([P, heads, HD]),
                                                      ALU.mult).then_inc(heads_done, 1)
                    elif u in (U_GA, U_GR):
                        wait_tile(dve, u, j)
                        dve.tensor_tensor(gT[:, 4 * (u - U_GA) + j, :], b, rs_row[0], ALU.mult).then_inc(evacuated[j], 1)
                    elif u in (U_Z0, U_Z1):
                        tanhs[0] += 1
                        dve.wait_ge(th_done, tanhs[0])
                        dve.scalar_tensor_tensor(out=gT2[:, 4 * (u - U_Z0) + j, :], in0=th2[:], scalar=1.0, in1=b,
                                                 op0=ALU.add, op1=ALU.mult).then_inc(evacuated[j], 1)
                    elif u in (U_O0, U_O1, U_OUT, U_OUT + 1):
                        if (u, j) == (U_O0, 0):
                            dve.wait_ge(x_again, 16)
                        wait_tile(dve, u, j)
                        h = (u - U_O0) if u <= U_O1 else u - U_OUT
                        xh = x1[:, j, h * 512:(h + 1) * 512]
                        dve.tensor_tensor(xh, b, xh, ALU.add).then_inc(evacuated[j], 1)
                    elif U_CONV <= u < U_GATE_A:
                        t = u - U_CONV
                        if j == 0 and t == 0:
                            dve.memset(cv[:, 0:2], 0.0).then_inc(cv_zero, 1)
                            dve.wait_ge(cv_zero, 1)
                        if j == 1:
                            wait_evacuated(dve, u, 0)
                            wait_tile(dve, u, 1)
                            dve.tensor_tensor(cv[:, 2:S + 2], b, vt[:], ALU.mult).then_inc(evacuated[1], 1)
                            wait_evacuated(dve, u, 1)
                            done(dve.tensor_scalar(acc[:], cv[:, 0:S], conv_w[:, 0, t:t + 1], None, ALU.mult))
                            for k in (1, 2):
                                done(dve.scalar_tensor_tensor(out=acc[:], in0=cv[:, k:S + k], scalar=conv_w[:, k, t:t + 1],
                                                              in1=acc[:], op0=ALU.mult, op1=ALU.add))
                        if j == 2:
                            wait_tile(dve, u, 2)
                            dve.tensor_tensor(acc[:], b, acc[:], ALU.mult).then_inc(evacuated[2], 1)
                            wait_evacuated(dve, u, 2)
                        if j == 3:
                            tanhs[0] += 1
                            dve.wait_ge(th_done, tanhs[0])
                            dve.scalar_tensor_tensor(out=th2[:], in0=th2[:], scalar=1.0, in1=b,
                                                     op0=ALU.add, op1=ALU.mult).then_inc(evacuated[3], 1)
                            wait_evacuated(dve, u, 3)
                            done(dve.scalar_tensor_tensor(out=acc[:], in0=acc[:], scalar=0.5, in1=th2[:], op0=ALU.mult, op1=ALU.mult))
                            done(dve.tensor_copy(yc_hi[:, t, :], acc[:]))
                            dve.tensor_tensor(yc_lo[:, t, :], acc[:], yc_hi[:, t, :].bitcast(F32), ALU.subtract).then_inc(yc_done, 1)
                    elif U_GATE_A <= u < U_OUT and j % 2:
                        t = 2 * ((u - U_GATE_A) % (KC // 2)) + j // 2
                        wait_evacuated(dve, u, j - 1)
                        wait_tile(dve, u, j)
                        if u >= U_GATE_B and t:
                            dve.wait_ge(merged, t)
                        dst = part[:, t, :] if u < U_GATE_B else acc[:]
                        dve.scalar_tensor_tensor(out=dst, in0=th2[:], scalar=1.0, in1=b,
                                                 op0=ALU.add, op1=ALU.mult).then_inc(evacuated[j], 1)
                        if u >= U_GATE_B:
                            wait_evacuated(dve, u, j)
                            done(dve.tensor_tensor(acc[:], acc[:], part[:, t, :], ALU.add))
                            done(dve.tensor_scalar(yc_hi[:, t, :], acc[:], 0.5, None, ALU.mult))
                            dve.scalar_tensor_tensor(out=yc_lo[:, t, :], in0=acc[:], scalar=0.5, in1=yc_hi[:, t, :].bitcast(F32),
                                                     op0=ALU.mult, op1=ALU.subtract).then_inc(merged, 1)

            def take_steps(n, half):
                for kind, m in STEPS[(n, half)]:
                    if kind == "XT":
                        take_xt_low(m)
                    elif kind == "RS_X":
                        dve.wait_ge(ssq_done, ST + 2 * ST * m)
                        if m == 0:
                            done(dve.tensor_copy(rs_v[:, 0:ST], ssq[:]))
                        else:
                            done(dve.tensor_tensor(rs_v[:, 0:ST], ssq_half[:, :, 0], ssq_half[:, :, 1], ALU.add))
                        rsqrt(ST, D)
                        if m == 0:
                            dve.tensor_scalar(rs_k[:], rs_y[:, 0:ST], QK_SCALE, None, ALU.mult)
                        dve.tensor_copy(rs_x[:, m, :], rs_y[:, 0:ST]).then_inc(rs_done, 1)
                        dve.memset(ones[m], 1.0)
                        dve.tensor_tensor(diag[m].rearrange("p (s r) -> p s r", s=ST), ident[:].unsqueeze(1).broadcast_to([P, ST, P]),
                                          rs_y[:, 0:ST].unsqueeze(2).broadcast_to([P, ST, P]), ALU.mult).then_inc(diag_done, 1)
                        dve.wait_ge(diag_done, m + 1)
                    elif kind == "ROWS":
                        prepare_parameters()
                    elif kind == "DECAYS":
                        prepare_decays()
                    elif kind in ("KT", "QT"):
                        for mp in range(2):
                            here, there = halves(mp)
                            dve.wait_ge(qk_hi_done, 2 * T_USE[(kind, m)] + mp + 1)
                            dst, high, scale = (k_lo2, k_hi2, kw) if kind == "KT" else (q_stack, q_stack, qws)
                            b = turn_banks[m % 2 if kind == "KT" else 0]
                            for r in ((here, there) if kind == "KT" else (there,)):
                                low = dve.scalar_tensor_tensor(out=dst[r, 2 * m + mp, :], in0=b[here, :], scalar=scale[here, :],
                                                               in1=high[here, 2 * m + mp, :].bitcast(F32), op0=ALU.mult, op1=ALU.subtract)
                        low.then_inc(t_free, 1)
                    elif kind == "KT2":
                        dve.wait_ge(qk2_hi_done, m + 1)
                        dve.scalar_tensor_tensor(out=k2_lo[:, m, :], in0=bank_t[:], scalar=k2w, in1=k2_hi[:, m, :].bitcast(F32),
                                                 op0=ALU.mult, op1=ALU.subtract).then_inc(t_free, 1)
                    elif kind == "QT2":
                        for c in range(2):
                            here, there = halves(c)
                            dve.wait_ge(qk2_hi_done, KV_HEADS + 2 * m + c + 1)
                            low = dve.scalar_tensor_tensor(out=q2(2 * m + c)[there, :, :], in0=bank_t[here, :].rearrange("p (s q) -> p s q", s=ST),
                                                           scalar=q2ws[here, :], in1=q2(2 * m + c)[here, :, :].bitcast(F32),
                                                           op0=ALU.mult, op1=ALU.subtract)
                        low.then_inc(t_free, 1)
                    elif kind == "XS":
                        dve.wait_ge(rs_row_done, 2)
                        if m:
                            dve.wait_ge(xt_scaled, m)
                        done(dve.tensor_tensor(x_tmp, x_raw[1][0][:, m, :].bitcast(F32), x_raw[1][1][:, m, :].bitcast(F32), ALU.add))
                        done(dve.tensor_tensor(x_tmp, x_tmp, rs_row[1], ALU.mult))
                        done(dve.tensor_copy(xt_hi[:, m, :], x_tmp))
                        dve.tensor_tensor(xt_lo[:, m, :], x_tmp, xt_hi[:, m, :].bitcast(F32), ALU.subtract).then_inc(xt_scaled, 1)
                    elif kind == "GATE":
                        dve.wait_ge(th_done, m + 1)
                        dve.scalar_tensor_tensor(out=gT[:, m, :], in0=th[:], scalar=1.0, in1=gT[:, m, :],
                                                 op0=ALU.add, op1=ALU.mult).then_inc(gates_done, 1)
                    elif kind == "S":
                        h, i = divmod(m, ST)
                        sl = m % 2
                        if i == 0:
                            dve.wait_ge(distance_done, h + 1)
                        dve.wait_ge(scores_done, m + 1)
                        if m >= 2:
                            dve.wait_ge(t_done, T_USE[("TW", m - 2)] + 1)
                        for mp in range(2):
                            dve.tensor_tensor_reduce(prob[:, sl, mp, :], score[:, mp, :], table[:, h % 2, CENTRE - i * P:CENTRE - i * P + S],
                                                     1.0, -3e38, ALU.subtract, ALU.max, mx[:, sl, mp:mp + 1]).then_inc(score_read, 1)
                        dve.wait_ge(score_read, 2 * m + 2)
                        dve.tensor_scalar(neg_mx[:, sl, :], mx[:, sl, :], -1.0, None, ALU.mult).then_inc(neg_max, 1)
                    elif kind == "W":
                        sl = m % 2
                        if m >= 8 and m % ST == 0:
                            dve.wait_ge(o_free, m // ST - 1)
                        dve.wait_ge(exp_done, 2 * m + 2)
                        done(dve.reciprocal(rec[:, m % 8, :], den[:, sl, :]))
                        done(dve.scalar_tensor_tensor(out=lam_rec[:, sl, :], in0=rec[:, m % 8, 1:2], scalar=den[:, sl, 0:1], in1=neg_lam[:],
                                                      op0=ALU.mult, op1=ALU.mult))
                        dve.scalar_tensor_tensor(out=prob[:, sl, 0, :], in0=prob[:, sl, 1, :], scalar=lam_rec[:, sl, 0:1],
                                                 in1=prob[:, sl, 0, :], op0=ALU.mult, op1=ALU.add).then_inc(weight_done, 1)
                    elif kind == "RN":
                        dve.wait_ge(decay_done, 1)
                        if m == 0:
                            for j in range(ST):
                                wait_evacuated(dve, U_RQK, j)
                        c = m % 2
                        src = rqk[:, :, 256:512] if m < 2 else rqk[:, :, 0:256]
                        dve.tensor_tensor((k_decay if m < 2 else q_decay)[:, :, :, c, :], src.rearrange("p s (h d) -> p s h d", h=RET_HEADS),
                                          ret_c[:, 2 + c if m < 2 else c, :].unsqueeze(1).unsqueeze(3).broadcast_to([P, ST, RET_HEADS, HD]),
                                          ALU.mult).then_inc(ret_scaled, 1)
                    elif kind == "KV":
                        kv, state = ([t[:, c * P:(c + 1) * P] for c in range(ST)] for t in (score[:, 0, :], prob[:, m % 2, 1, :]))
                        f, b = slice(0, HD), slice(HD, P)
                        dve.wait_ge(kr_done, 2 * m + 1)
                        if m < 2:
                            dve.wait_ge(weight_done, DA_STEPS)
                        else:
                            dve.wait_ge(av_done, DA_STEPS + m - 1)
                        dve.memset(state[0][f, :], 0.0)
                        dve.memset(state[3][b, :], 0.0)
                        dve.tensor_copy(state[1][f, :], kv[0][f, :])
                        done(dve.tensor_copy(state[2][b, :], kv[3][b, :]))
                        for k in (1, 2):
                            dve.scalar_tensor_tensor(out=state[k + 1][f, :], in0=state[k][f, :], scalar=ret_c[f, 4, m:m + 1],
                                                     in1=kv[k][f, :], op0=ALU.mult, op1=ALU.add)
                            back = dve.scalar_tensor_tensor(out=state[2 - k][b, :], in0=state[3 - k][b, :], scalar=ret_c[b, 5, m:m + 1],
                                                            in1=kv[3 - k][b, :], op0=ALU.mult, op1=ALU.add)
                            if k == 1:
                                done(back)
                        back.then_inc(kr_free, 1)
                    elif kind == "RS":
                        dve.wait_ge(kr_done, 2 * m + 2)
                        if m < 2:
                            dve.wait_ge(t_done, T_USE[("TW", DA_STEPS - 1)] + 1)
                        dve.tensor_tensor(prob[:, m % 2, 0, :].rearrange("p (c q) -> p c q", c=ST), score[:, 1, :].rearrange("p (c q) -> p c q", c=ST),
                                          dmat[:, m, :].unsqueeze(1).broadcast_to([P, ST, P]), ALU.mult).then_inc(kr_free, 1)
                    elif kind == "AN":
                        h = m
                        head_sums(rs_v[:, ST * h:ST * h + ST], sq[:], ST)
                        if h == DA_HEADS - 1:
                            dve.wait_ge(sq_used, sums[0])
                            rsqrt(DA_STEPS, P)
                    elif kind == "ON":
                        o = o_raw[:, m, :, :]
                        dve.tensor_tensor(o, o, rs_y[:, ST * m:ST * m + ST].unsqueeze(2).broadcast_to([P, ST, P]), ALU.mult).then_inc(o_normed, 1)
                    elif kind == "RB":
                        h = m
                        head_sums(rs_v[:, 0:ST], sq[:], ST)
                        dve.wait_ge(sq_used, sums[0])
                        dve.wait_ge(o_normed, DA_HEADS + h)
                        rsqrt(ST, P)
                        o = o_raw[:, h, :, :]
                        dve.tensor_tensor(o, o, rs_y[:, 0:ST].unsqueeze(2).broadcast_to([P, ST, P]), ALU.mult).then_inc(o_normed, 1)
                    elif kind == "F":
                        dve.wait_ge(t_done, T_USE[(kind, m)] + 1)
                        dve.wait_ge(gates_done, m + 1)
                        dve.scalar_tensor_tensor(out=gT[:, m, :], in0=bank_t[:], scalar=sub_s[:, 0:1] if m < DA_HEADS else 0.5,
                                                 in1=gT[:, m, :], op0=ALU.mult, op1=ALU.mult).then_inc(t_free, 1)
                        dve.wait_ge(t_free, T_USE[(kind, m)] + 1)
                        done(dve.tensor_copy(mix_hi[:, m, :], gT[:, m, :]))
                        dve.tensor_tensor(mix_lo[:, m, :], gT[:, m, :], mix_hi[:, m, :].bitcast(F32), ALU.subtract).then_inc(mixed, 1)
                    elif kind == "S2":
                        i, j = divmod(m, KV_HEADS)
                        width = P if i == 0 else 2 * P
                        if m == 0:
                            dve.wait_ge(setup_mask, 1)
                        dve.wait_ge(scores2, m + 1)
                        if m >= 2:
                            dve.wait_ge(t_done, T_USE[("TP", m - 2)] + 1)
                        for r in range(GROUP):
                            last = dve.tensor_tensor_reduce(
                                prob2[:, m % 2, r, 0:width], score[:, r % 2, (r // 2) * 256:(r // 2) * 256 + width],
                                mask[:, 2 * P - width:2 * P], 1.0, -3e38, ALU.subtract, ALU.max, mx2[:, m % 4, r:r + 1])
                        last.then_inc(score2_read, 1)
                        dve.wait_ge(score2_read, m + 1)
                        if i:
                            done(dve.tensor_tensor(prob2[:, m % 2, :, 0:P], prob2[:, m % 2, :, 0:P], prob2[:, m % 2, :, P:2 * P], ALU.max))
                        done(dve.scalar_tensor_tensor(out=neg_m2[:, m % 4, :], in0=mx2[:, m % 4, :], scalar=-1.0,
                                                      in1=neg_sink[:, 4 * j:4 * j + 4], op0=ALU.mult, op1=ALU.min))
                        dve.tensor_tensor(sink_m[:, m % 4, :], neg_m2[:, m % 4, :], sink[:, 4 * j:4 * j + 4], ALU.add).then_inc(neg_max2, 1)
                    elif kind == "W2":
                        dve.wait_ge(exp2_done, m + 1)
                        done(dve.tensor_tensor(den2[:, m % 4, :], den2[:, m % 4, :], sink_e[:, m % 4, :], ALU.add))
                        dve.reciprocal(rec2[:, m % 4, :], den2[:, m % 4, :]).then_inc(rec2_done, 1)
                    elif kind == "TP":
                        dve.wait_ge(t_done, T_USE[(kind, m)] + 1)
                        if m:
                            dve.wait_ge(pT_split, m)
                        w = bank_t[:].rearrange("p (r x) -> p r x", r=GROUP)
                        mine = dve.tensor_tensor(pT[:, 0, :, :], w, own[:].unsqueeze(1).broadcast_to([P, GROUP, P]), ALU.mult)
                        if m >= KV_HEADS:
                            done(mine)
                            mine = dve.tensor_tensor(pT[:, 1, :, :], w, pT[:, 0, :, :], ALU.subtract)
                        mine.then_inc(pT_done, 1)
                    elif kind == "TL":
                        tiles = 1 if m < KV_HEADS else 2
                        dve.wait_ge(pT_hi_done, m + 1)
                        dve.tensor_tensor(pT_lo[:, 0:tiles, :, :], pT[:, 0:tiles, :, :], pT_hi[:, 0:tiles, :, :].bitcast(F32),
                                          ALU.subtract).then_inc(pT_split, 1)
                    elif kind == "AG":
                        i, j = divmod(m, KV_HEADS)
                        for c in (2 * j, 2 * j + 1):
                            wait_evacuated(dve, U_Z0 + c // 4, c % 4)
                        for odd in range(2):
                            r = slice(odd * HD, (odd + 1) * HD)
                            dve.wait_ge(o2_low, 2 * m + odd + 1)
                            dve.tensor_tensor(o2_sum[r, :, :], o2_heads(slice(0, HD), odd), o2_sum[r, :, :], ALU.add).then_inc(o2_summed, 1)
                        dve.wait_ge(o2_summed, 2 * m + 2)
                        g2 = gT2[:, 2 * j:2 * j + 2, i * P:(i + 1) * P]
                        dve.scalar_tensor_tensor(out=g2, in0=o2_sum[:], scalar=0.5, in1=g2, op0=ALU.mult, op1=ALU.mult).then_inc(o2_gated, 1)
                    elif kind == "OS":
                        dve.wait_ge(o2_gated, WIN_STEPS)
                        done(dve.tensor_copy(o2_hi[:, m, :], gT2[:, m, :]))
                        dve.tensor_tensor(o2_lo[:, m, :], gT2[:, m, :], o2_hi[:, m, :].bitcast(F32), ALU.subtract).then_inc(o2_split, 1)

            for n in range(PIECES):
                for half in range(2):
                    if n < WIN_FIRST:
                        take_tiles(n, half)
                    take_steps(n, half)
                    if half == 0 and tiles_wait(n - 1, 1):
                        take_tiles(n - 1, 1)
                    if n >= WIN_FIRST and not tiles_wait(n, half):
                        take_tiles(n, half)

        @block.tensor
        def _(pe):
            def products(out, left, right, first, last):
                pe.matmul(out, left[0], right[0], start=first, stop=False)
                pe.matmul(out, left[0], right[1], start=False, stop=False)
                return pe.matmul(out, left[1], right[0], start=False, stop=last)

            def transposes(step, sources, outs):
                if step[0] == "TP" and step[1]:
                    pe.wait_ge(pT_done, step[1])
                elif step[0] == "KT":
                    if step[1] >= 2:
                        pe.wait_ge(t_free, T_USE[step] - 1)
                elif T_USE[step]:
                    pe.wait_ge(t_free, T_USE[step])
                for src, dst in zip(sources, outs):
                    last = pe.transpose(dst, src, ident[:])
                last.then_inc(t_done, 1)

            def quarters(t):
                return [t[:, c * P:(c + 1) * P] for c in range(4)]

            def step(kind, m):
                if kind == "XT":
                    b, c = divmod(m, KC)
                    if b:
                        for s in range(ST):
                            wait_evacuated(pe, U_O0 + c // 4, s)
                    if c >= 4:
                        pe.wait_ge(xt_split, m - 3)
                    for src, dst in zip([x_rows[b][:, s, c * P:(c + 1) * P] for s in range(ST)], quarters(xt_banks[c % 4])):
                        last = pe.transpose(dst, src, ident[:])
                    last.then_inc(xt_done, 1)
                elif kind == "RS_ROW":
                    pe.wait_ge(diag_done, m + 1)
                    pe.wait_ge(xt_split, KC * m + KC - 1)
                    pe.matmul(bank_o[:], ones[m], diag[m], start=True, stop=True).then_inc(rs_turned, 1)
                elif kind == "ROWS":
                    pe.wait_ge(params, 16 * N_PARAMS)
                    pe.wait_ge(xt_split, KC)
                    pe.transpose(bank_t[:, 0:ROWS], rows[:], ident[0:ROWS, 0:ROWS]).then_inc(rows_turned, 1)
                elif kind in ("KT", "QT"):
                    pe.wait_ge(heads_done, ST if kind == "KT" else 2 * ST)
                    src = k_heads if kind == "KT" else stage
                    transposes((kind, m), [src[:, s, m * P:(m + 1) * P] for s in range(ST)], quarters(turn_banks[m % 2 if kind == "KT" else 0]))
                elif kind == "S":
                    h, i = divmod(m, ST)
                    if m == 0:
                        pe.wait_ge(t_free, T_USE[("QT", 3)] + 1)
                    else:
                        pe.wait_ge(score_read, 2 * m)
                    for mp in range(2):
                        q = q_stack[:, 2 * h + mp, i * P:(i + 1) * P]
                        pe.matmul(score[:, mp, :], q, k_hi2[:, 2 * h + mp, :], start=True, stop=False)
                        last = pe.matmul(score[:, mp, :], q, k_lo2[:, 2 * h + mp, :], start=False, stop=True)
                    last.then_inc(scores_done, 1)
                elif kind == "TW":
                    pe.wait_ge(weight_done, m + 1)
                    transposes((kind, m), quarters(prob[:, m % 2, 0, :]), quarters(bank_t))
                elif kind == "AV":
                    h, i = divmod(m, ST)
                    pe.wait_ge(t_free, T_USE[("TW", m)] + 1)
                    if m == 0:
                        for j in range(ST):
                            wait_evacuated(pe, U_V, j)
                    if i == 0 and h:
                        pe.wait_ge(o_free, h)
                    for c in range(4):
                        last = pe.matmul(bank_o[:, i * P:(i + 1) * P], wT[:, m % 2, c * P:(c + 1) * P],
                                         va[:, c, h * P:(h + 1) * P], start=(c == 0), stop=(c == 3))
                    last.then_inc(av_done, 1)
                elif kind == "RT":
                    if m < 2:
                        pe.wait_ge(score_read, 2 * DA_STEPS)
                    else:
                        pe.wait_ge(rt_free, m - 1)
                    if m == 0:
                        for j in range(ST):
                            wait_evacuated(pe, U_RQK, j)
                    if m == 2:
                        pe.wait_ge(ret_scaled, 4)
                    for s in range(ST):
                        if m < 2:
                            src = rqk[:, s, 256 + m * P:256 + (m + 1) * P]
                        elif m < 6:
                            src = q_decay[:, s, m - 2, :, :].rearrange("p c d -> p (c d)")
                        else:
                            src = rqk[:, s, (m - 6) * P:(m - 5) * P]
                        last = pe.transpose(score[:, m % 2, s * P:(s + 1) * P], src, ident[:])
                    last.then_inc(rt_done, 1)
                elif kind == "KV":
                    if m == 0:
                        pe.wait_ge(rt_free, 8)
                        for j in range(ST):
                            wait_evacuated(pe, U_RV, j)
                    else:
                        pe.wait_ge(kr_free, 2 * m - 1)
                    for c in range(ST):
                        last = pe.matmul(score[:, 0, c * P:(c + 1) * P], k_decay[:, c, m, :, :].rearrange("p c d -> p (c d)"),
                                         vr[:, c, m * P:(m + 1) * P], start=True, stop=True)
                    last.then_inc(kr_done, 1)
                elif kind == "RS":
                    if m:
                        pe.wait_ge(kr_free, 2 * m)
                    r = slice((m % 2) * HD, (m % 2 + 1) * HD)
                    for c in range(ST):
                        last = pe.matmul(score[:, 1, c * P:(c + 1) * P], rkT[r, m // 2, c * P:(c + 1) * P],
                                         rqT[r, m // 2, c * P:(c + 1) * P], start=True, stop=True)
                    last.then_inc(kr_done, 1)
                elif kind == "RA":
                    pe.wait_ge(kr_free, 2 * m + 2)
                    pe.wait_ge(o_free, DA_HEADS + m)
                    for c in range(ST):
                        tile = slice(c * P, (c + 1) * P)
                        pe.matmul(bank_o[:, tile], prob[:, m % 2, 0, tile], vr[:, c, m * P:(m + 1) * P], start=True, stop=False)
                        last = pe.matmul(bank_o[:, tile], q_decT[:, m, tile], prob[:, m % 2, 1, tile], start=False, stop=True)
                    last.then_inc(av_done, 1)
                elif kind == "F":
                    pe.wait_ge(o_normed, m + 1)
                    transposes((kind, m), [o_raw[:, m % 4, i, :] for i in range(ST)], quarters(bank_t))
                elif kind == "KT2":
                    pe.wait_ge(heads_done, 3 * ST)
                    transposes((kind, m), [k_dup[:, s, m * P:(m + 1) * P] for s in range(ST)], quarters(bank_t))
                elif kind == "QT2":
                    pe.wait_ge(heads_done, (4 + m // 4) * ST)
                    transposes((kind, m), [stage2[:, s, (m % 4) * P:(m % 4 + 1) * P] for s in range(ST)], quarters(bank_t))
                elif kind == "S2":
                    i, j = divmod(m, KV_HEADS)
                    keys = slice(max(i - 1, 0) * P, (i + 1) * P)
                    width = P if i == 0 else 2 * P
                    if m == 0:
                        pe.wait_ge(t_free, T_USE[("QT2", 7)] + 1)
                    else:
                        pe.wait_ge(score2_read, m)
                    for r in range(GROUP):
                        dst = score[:, r % 2, (r // 2) * 256:(r // 2) * 256 + width]
                        pe.matmul(dst, q2(GROUP * j + r)[:, i, :], k2_hi[:, j, keys], start=True, stop=False)
                        last = pe.matmul(dst, q2(GROUP * j + r)[:, i, :], k2_lo[:, j, keys], start=False, stop=True)
                    last.then_inc(scores2, 1)
                elif kind == "TP":
                    pe.wait_ge(weight2_done, m + 1)
                    transposes((kind, m), [prob2[:, m % 2, r, 0:P] for r in range(GROUP)], quarters(bank_t))
                elif kind == "AV2":
                    i, j = divmod(m, KV_HEADS)
                    pe.wait_ge(pT_split, m + 1)
                    if m == 0:
                        for s in range(ST):
                            wait_evacuated(pe, U_KV, s)
                        pe.wait_ge(o_free, DA_HEADS + RET_HEADS)
                    else:
                        pe.wait_ge(o2_summed, 2 * m)
                    tiles = 1 if i == 0 else 2
                    for c in range(tiles):
                        v_parts = v2[:, i - c, j, :, :].rearrange("p c d -> p (c d)")
                        pe.matmul(bank_o[:], v_parts, pT_hi[:, c, :, :].rearrange("p r q -> p (r q)"), start=c == 0, stop=False)
                        last = pe.matmul(bank_o[:], v_parts, pT_lo[:, c, :, :].rearrange("p r q -> p (r q)"), start=False, stop=c == tiles - 1)
                    last.then_inc(av2_done, 1)

            pe.wait_ge(setup, 1)
            pe.wait_ge(norms_landed, 32)
            pe.transpose(bank_t[:, 0:2 * KC], norm_rows[:], ident[0:2 * KC, 0:2 * KC]).then_inc(norms_turned, 1)
            pe.wait_ge(norms_ready, 1)
            for s in range(ST):
                pe.wait_ge(x_landed[s], 16)
                for c in range(4):
                    last = pe.transpose(xt_banks[c][:, s * P:(s + 1) * P], x_in[:, s, c * P:(c + 1) * P], ident[:])
                    if s == ST - 1:
                        last.then_inc(xt_done, 1)
            for n in range(PIECES):
                u, q = divmod(n, 4)
                slot = n % SLOTS
                if u in (U_KV, U_Q20, U_Q21):
                    left = x_raw[1]
                elif u in (U_O0, U_O1):
                    left = (mix_hi, mix_lo)
                elif u >= U_OUT:
                    left = (yc_hi, yc_lo)
                else:
                    left = (xt_hi, xt_lo)
                if UNIT[u][0] == NAT:
                    w = [t[:, slot, :].rearrange("p (k c) -> p k c", k=2) for t in (w_hi, w_lo)]
                    order = [(kk, s) for kk in range(2) for s in range(ST)] if q < 3 else [(kk, s) for s in range(ST) for kk in range(2)]
                    for e, (kk, s) in enumerate(order):
                        if q == 0 and kk == 0 and u:
                            pe.wait_ge(evacuated[s], u)
                        if u in (U_K, U_KV) and (s == 0 or q == 3):
                            pe.wait_ge(xt_split, (KC if u == U_KV else 0) + 2 * q + kk + 1)
                        if u == U_O0 and (s == 0 or q == 3):
                            pe.wait_ge(mixed, 2 * q + kk + 1)
                        if u == U_OUT and (s == 0 or q == 3):
                            pe.wait_ge(merged, 2 * q + kk + 1)
                        if e == 0:
                            pe.wait_ge(w_split, n + 1)
                        k = 2 * q + kk
                        last = products(bank(u, s), [t[:, k, s * P:(s + 1) * P] for t in left], [t[:, kk, :] for t in w],
                                        k == 0, k == KC - 1)
                        if e == 7:
                            last.then_inc(piece_done, 1)
                        elif q == 3 and kk == 1:
                            last.then_inc(natural_done, 1)
                        if e % 4 == 3:
                            for kind, m in STEPS[(n, e // 4)]:
                                step(kind, m)
                else:
                    w = [t[:, slot, :].rearrange("p (k c) -> p k c", k=KC) for t in (w_hi, w_lo)]
                    right = left
                    if U_GATE_A <= u < U_OUT and q % 2:
                        right = (yc_hi, yc_lo) if u < U_GATE_B else (o2_hi, o2_lo)
                        if u == U_GATE_A:
                            pe.wait_ge(yc_done, KC)
                        if u == U_GATE_B:
                            pe.wait_ge(o2_split, KC)
                    if u == U_Z0 and q == 0:
                        pe.wait_ge(xt_scaled, KC)
                    pe.wait_ge(evacuated[q], u)
                    pe.wait_ge(w_split, n + 1)
                    for k in range(KC):
                        last = products(bank(u, q), [t[:, k, :] for t in w], [t[:, k, :] for t in right], k == 0, k == KC - 1)
                        if k == KC - 1:
                            last.then_inc(piece_done, 1)
                        if k % 4 == 3:
                            for kind, m in STEPS[(n, k // 4)]:
                                step(kind, m)


_INS = ["x", "norm_w", "w_in", "q_norm_w", "k_norm_w", "lambda_q1", "lambda_k1", "lambda_q2", "lambda_k2", "subln_w",
        "ret_decay_fwd", "ret_decay_bwd", "w_out", "norm_g_2", "w_in_2", "conv_w_2", "q_norm_g_2", "k_norm_g_2",
        "sinks_2", "w_conv_out_2", "w_attn_out_2", "gate_b_2", "w_out_2"]


def kernel(**inputs):
    import numpy as _np
    import concourse.bacc as _bacc
    from concourse import mybir as _mybir
    from concourse.bass_utils import run_bass_kernel_spmd as _run

    nc = _bacc.Bacc("TRN2", target_bir_lowering=False, num_devices=1)
    arrays, args = {}, {}
    for name in _INS:
        v = _np.ascontiguousarray(inputs[name])
        arrays[f"in_{name}_dram"] = v
        args[name] = nc.dram_tensor(f"in_{name}_dram", v.shape, _mybir.dt.from_np(v.dtype), kind="ExternalInput").ap()
    args["out"] = nc.dram_tensor("out_0_dram", (1, S, D), _mybir.dt.float32, kind="ExternalOutput").ap()
    build(nc, args)
    r = _run(nc, [arrays], core_ids=[0])
    return r.results[0]["out_0_dram"]
```
